# Optimizing a Trainium2 kernel written in Bass

```python
import jax, jax.numpy as jnp
from jax import lax
import numpy as np

D_MODEL = 1024
BATCH = 1
SEQ = 1024
DEPTH = 1

CHUNK = 64
HEAD_DIM = 64
ATT_HEADS = (D_MODEL // 2) // HEAD_DIM
ATT_KV_HEADS = ATT_HEADS // 4
ATT_GROUP = ATT_HEADS // ATT_KV_HEADS
WINDOW = 128
WINDOW_CHUNKS = WINDOW // CHUNK
RWKV_HEADS = (D_MODEL // 2) // HEAD_DIM
ATT_WIDTH = ATT_HEADS * HEAD_DIM
KV_WIDTH = ATT_KV_HEADS * HEAD_DIM
RWKV_WIDTH = RWKV_HEADS * HEAD_DIM
MIX_WIDTH = ATT_WIDTH + RWKV_WIDTH
DECAY_LORA = 64
AAA_LORA = 64
GATE_LORA = 128
ATT_PROJ = ATT_WIDTH + 2 * KV_WIDTH
RWKV_PROJ = 3 * RWKV_WIDTH + DECAY_LORA + AAA_LORA + GATE_LORA
IN_PROJ = ATT_PROJ + RWKV_PROJ
ATT_SPLITS = [ATT_WIDTH, ATT_WIDTH + KV_WIDTH]
RWKV_SPLITS = [RWKV_WIDTH, 2 * RWKV_WIDTH, 3 * RWKV_WIDTH,
               3 * RWKV_WIDTH + DECAY_LORA, 3 * RWKV_WIDTH + DECAY_LORA + AAA_LORA]
D_FF = 2816
CONV_WIDTH = 3
NORM_EPS = 1e-6
GN_EPS = HEAD_DIM * 1e-5

kernel_name = "hymba_swa_sink_rwkv7_convglu_sandwich"

def rms_norm(x, gain):
    xf = x.astype(jnp.float32)
    xf = xf * lax.rsqrt(jnp.mean(xf * xf, axis=-1, keepdims=True) + NORM_EPS)
    return (xf * gain.astype(jnp.float32)).astype(x.dtype)

def alibi_slopes(n):
    return jnp.exp2(-8.0 * jnp.arange(1, n + 1, dtype=jnp.float32) / n)

def sink_window_attention(q, k, v, sinks):
    b, s, _ = q.shape
    nc = s // CHUNK
    band = WINDOW_CHUNKS * CHUNK
    pad = (WINDOW_CHUNKS - 1) * CHUNK
    qb = q.reshape(b, nc, CHUNK, ATT_KV_HEADS, ATT_GROUP, HEAD_DIM)

    def band_of(t):
        tp = jnp.pad(t, ((0, 0), (pad, 0), (0, 0)))
        parts = [tp[:, w * CHUNK: w * CHUNK + s].reshape(b, nc, CHUNK, ATT_KV_HEADS, HEAD_DIM)
                 for w in range(WINDOW_CHUNKS)]
        return jnp.concatenate(parts, axis=2)

    kb, vb = band_of(k), band_of(v)
    scores = jnp.einsum('bcqkgd,bcskd->bckgqs', qb, kb).astype(jnp.float32) * (HEAD_DIM ** -0.5)
    qi = jnp.arange(CHUNK)[:, None]
    kj = jnp.arange(band)[None, :]
    dist = jnp.abs(qi + pad - kj).astype(jnp.float32)
    slopes = alibi_slopes(ATT_HEADS).reshape(ATT_KV_HEADS, ATT_GROUP)
    scores = scores - slopes[None, None, :, :, None, None] * dist
    key_chunk = jnp.arange(nc)[:, None] - (WINDOW_CHUNKS - 1) + jnp.arange(band)[None, :] // CHUNK
    valid = (key_chunk >= 0)[None, :, None, None, None, :]
    scores = jnp.where(valid, scores, -jnp.inf)
    sink = sinks.astype(jnp.float32).reshape(ATT_KV_HEADS, ATT_GROUP)[None, None, :, :, None, None]
    m = jnp.maximum(jnp.max(scores, axis=-1, keepdims=True), sink)
    e = jnp.exp(scores - m)
    probs = e / (jnp.sum(e, axis=-1, keepdims=True) + jnp.exp(sink - m))
    out = jnp.einsum('bckgqs,bcskd->bcqkgd', probs.astype(v.dtype), vb)
    return out.reshape(b, s, ATT_WIDTH)

def wkv7_scan(r, decay, k, v, kk, a):
    b, s, h, d = r.shape

    def step(state, inp):
        r_t, w_t, k_t, v_t, kk_t, a_t = inp
        sa = jnp.einsum('bhvk,bhk->bhv', state, -kk_t)
        state = (state * w_t[:, :, None, :]
                 + sa[..., None] * (kk_t * a_t)[:, :, None, :]
                 + v_t[..., None] * k_t[:, :, None, :])
        return state, jnp.einsum('bhvk,bhk->bhv', state, r_t)

    xs = tuple(jnp.moveaxis(t, 1, 0) for t in (r, decay, k, v, kk, a))
    s0 = jnp.zeros((b, h, d, d), jnp.float32)
    _, ys = lax.scan(step, s0, xs)
    return jnp.moveaxis(ys, 0, 1)

def rwkv7_time_mix(p, mu, w0, w_w2, a0, w_a2, w_g2, k_k, k_a, r_k, ln_w, ln_b):
    b, s, _ = p.shape
    f32 = jnp.float32
    prev = jnp.pad(p[:, :-1], ((0, 0), (1, 0), (0, 0)))
    p = p + (prev - p) * mu
    r, k, v, wd, ad, gd = jnp.split(p, RWKV_SPLITS, axis=-1)
    w = -jax.nn.softplus(-(w0 + jnp.tanh(wd) @ w_w2)) - 0.5
    a = jax.nn.sigmoid(a0 + ad @ w_a2)
    g = jax.nn.sigmoid(gd) @ w_g2
    heads = lambda t: t.astype(f32).reshape(b, s, RWKV_HEADS, HEAD_DIM)
    r, k, v, w, a = heads(r), heads(k), heads(v), heads(w), heads(a)
    kk = k * k_k.astype(f32).reshape(RWKV_HEADS, HEAD_DIM)
    kk = kk / jnp.maximum(jnp.sqrt(jnp.sum(kk * kk, axis=-1, keepdims=True)), 1e-12)
    k = k * (1.0 + (a - 1.0) * k_a.astype(f32).reshape(RWKV_HEADS, HEAD_DIM))
    decay = jnp.exp(-jnp.exp(w))
    y = wkv7_scan(r, decay, k, v, kk, a)
    mean = jnp.mean(y, axis=-1, keepdims=True)
    var = jnp.mean(jnp.square(y - mean), axis=-1, keepdims=True)
    yn = ((y - mean) * lax.rsqrt(var + GN_EPS)).reshape(b, s, RWKV_WIDTH)
    yn = yn * ln_w.astype(f32) + ln_b.astype(f32)
    bonus = jnp.sum(r * k * r_k.astype(f32), axis=-1, keepdims=True) * v
    out = (yn + bonus.reshape(b, s, RWKV_WIDTH)) * g.astype(f32)
    return out.astype(p.dtype)

def conv_glu_ffn(x, w_up, conv_w, conv_b, w_down):
    u = x @ w_up
    u = lax.conv_general_dilated(
        u, conv_w[:, None, :], window_strides=(1,), padding=[(CONV_WIDTH - 1, 0)],
        dimension_numbers=('NWC', 'WIO', 'NWC'), feature_group_count=u.shape[-1]) + conv_b
    gate, val = jnp.split(u, 2, axis=-1)
    return (jax.nn.gelu(gate, approximate=True) * val) @ w_down

def setup_inputs(seed: int = 0) -> dict:
    key = jax.random.key(seed)
    ks = jax.random.split(key, 24)
    L = DEPTH
    nrm = lambda k, shape, scale: jax.random.normal(k, shape, jnp.float32) * scale
    gain = lambda k, n: 1.0 + nrm(k, (L, n), 0.02)
    return {
        "x": nrm(ks[0], (BATCH, SEQ, D_MODEL), 1.0),
        "norm_mix_pre": gain(ks[1], D_MODEL),
        "w_in": nrm(ks[2], (L, D_MODEL, IN_PROJ), D_MODEL ** -0.5),
        "attn_sinks": nrm(ks[3], (L, ATT_HEADS), 0.5),
        "rwkv_mu": jax.random.uniform(ks[4], (L, RWKV_PROJ), jnp.float32, 0.0, 1.0),
        "rwkv_w0": jax.random.uniform(ks[5], (L, RWKV_WIDTH), jnp.float32, -5.0, 1.0),
        "rwkv_w_w2": nrm(ks[6], (L, DECAY_LORA, RWKV_WIDTH), DECAY_LORA ** -0.5),
        "rwkv_a0": nrm(ks[7], (L, RWKV_WIDTH), 0.1),
        "rwkv_w_a2": nrm(ks[8], (L, AAA_LORA, RWKV_WIDTH), AAA_LORA ** -0.5),
        "rwkv_w_g2": nrm(ks[9], (L, GATE_LORA, RWKV_WIDTH), GATE_LORA ** -0.5),
        "rwkv_k_k": 0.85 + nrm(ks[10], (L, RWKV_WIDTH), 0.05),
        "rwkv_k_a": 1.0 + nrm(ks[11], (L, RWKV_WIDTH), 0.05),
        "rwkv_r_k": nrm(ks[12], (L, RWKV_HEADS, HEAD_DIM), 0.1),
        "rwkv_ln_w": gain(ks[13], RWKV_WIDTH),
        "rwkv_ln_b": nrm(ks[14], (L, RWKV_WIDTH), 0.01),
        "w_out": nrm(ks[15], (L, MIX_WIDTH, D_MODEL), MIX_WIDTH ** -0.5),
        "norm_mix_post": gain(ks[16], D_MODEL),
        "norm_ffn_pre": gain(ks[17], D_MODEL),
        "ffn_w_up": nrm(ks[18], (L, D_MODEL, 2 * D_FF), D_MODEL ** -0.5),
        "ffn_conv_w": nrm(ks[19], (L, CONV_WIDTH, 2 * D_FF), CONV_WIDTH ** -0.5),
        "ffn_conv_b": nrm(ks[20], (L, 2 * D_FF), 0.01),
        "ffn_w_down": nrm(ks[21], (L, D_FF, D_MODEL), D_FF ** -0.5),
        "norm_ffn_post": gain(ks[22], D_MODEL),
    }

def reference(x, norm_mix_pre, w_in, attn_sinks, rwkv_mu, rwkv_w0, rwkv_w_w2, rwkv_a0,
              rwkv_w_a2, rwkv_w_g2, rwkv_k_k, rwkv_k_a, rwkv_r_k, rwkv_ln_w, rwkv_ln_b,
              w_out, norm_mix_post, norm_ffn_pre, ffn_w_up, ffn_conv_w, ffn_conv_b,
              ffn_w_down, norm_ffn_post):
    h = x
    for l in range(DEPTH):
        xn = rms_norm(h, norm_mix_pre[l])
        p = xn @ w_in[l]
        q, k, v = jnp.split(p[..., :ATT_PROJ], ATT_SPLITS, axis=-1)
        y_att = sink_window_attention(q, k, v, attn_sinks[l])
        y_rwkv = rwkv7_time_mix(p[..., ATT_PROJ:], rwkv_mu[l], rwkv_w0[l], rwkv_w_w2[l],
                                rwkv_a0[l], rwkv_w_a2[l], rwkv_w_g2[l], rwkv_k_k[l],
                                rwkv_k_a[l], rwkv_r_k[l], rwkv_ln_w[l], rwkv_ln_b[l])
        mix = jnp.concatenate([y_att, y_rwkv], axis=-1) @ w_out[l]
        h = h + rms_norm(mix, norm_mix_post[l])
        f = conv_glu_ffn(rms_norm(h, norm_ffn_pre[l]), ffn_w_up[l], ffn_conv_w[l],
                         ffn_conv_b[l], ffn_w_down[l])
        h = h + rms_norm(f, norm_ffn_post[l])
    return h


_drawn_inputs = setup_inputs


def setup_inputs(seed=0):
    import zlib

    import numpy as np

    out = dict(_drawn_inputs(seed))
    spreads = {}
    factors = {'attn_sinks': 3.284,
     'rwkv_ln_w': 3.805,
     'rwkv_ln_b': 7.996,
     'norm_mix_post': 3.477,
     'norm_ffn_pre': 3.439,
     'ffn_conv_b': 6.858,
     'norm_ffn_post': 4.904}
    for name, (base, spread) in spreads.items():
        noise = np.random.default_rng([zlib.crc32(name.encode()), seed]).standard_normal(out[name].shape)
        drawn = base * np.exp(spread * noise) if base else spread * noise
        out[name] = __import__('jax').numpy.asarray(drawn.astype(out[name].dtype))
    for name, factor in factors.items():
        out[name] = (out[name] * factor).astype(out[name].dtype)
    return out
```

```python
from contextlib import ExitStack

import numpy as np

import concourse.bass as bass
from concourse import mybir

P = 128
D, SEQ, HALF, FF = 1024, 1024, 512, 2816
HALVES, NT = SEQ // HALF, HALF // P
KT = D // P
CH, HD, HEADS, NP = 64, 64, 8, 4
PJ = FF // P
WIN = 3 * CH
LEVELS = (1, 2, 4, 8, 16, 32)
RAWS, SPLITS = 4, 2
DECAY = float(np.exp(-0.5))
EPS, GN_EPS = 1e-6, HD * 1e-5
ATT = 768
HID = 1e30

F32, F32R = mybir.dt.float32, mybir.dt.float32r
ALU, ACT, AX = mybir.AluOpType, mybir.ActivationFunctionType, mybir.AxisListType.X

MU, W0, A0, KK_, KA, CW, CB, RK = 0, 14, 18, 22, 26, 30, 30 + 6 * PJ, 30 + 8 * PJ
NPAR = RK + 8


class Steps:

    def __init__(self, sem, names, base, times):
        assert len(set(names)) == len(names)
        self.sem, self.names, self.base, self.times, self.at = sem, names, base, times, 0

    def after(self, name, it=0):
        return self.base + self.names.index(name) + 1 + it * len(self.names)

    def end(self):
        return self.base + len(self.names) * self.times

    def step(self, name):
        assert self.names[self.at % len(self.names)] == name, (self.names[self.at % len(self.names)], name)
        self.at += 1
        return 1


def norm_steps():
    pe = [f"tr{i}_{b}" for i in range(NT) for b in range(2)]
    act, vec = [], []
    for i in range(NT):
        act += [f"sq{i}", f"root{i}", f"hi{i}_0", f"hi{i}_1"]
        vec += [f"ms{i}", f"rstd{i}", f"xs{i}", f"lo{i}_0", f"lo{i}_1"]
    return pe, act, vec


def loop_steps():
    pe = ["G0", "G1", "trA", "trV", "sc0", "sc1", "Y1", "trK", "TT1", "sc2", "T1", "sc3",
          "Y2", "trB", "TT2", "MKA0", "T2", "MKA1", "Y3", "MRB0", "TT3", "MRB1", "T3", "PT0",
          "Y4", "MRK0", "TT4", "PT1", "T4", "MRK1", "Y5", "PT2", "TT5", "X1", "T5", "PT3",
          "Y6", "PV", "TT6", "bonus", "Z", "TAT", "UAa", "HVa", "RHa", "HBa", "UAb", "HVb", "RHb",
          "HBb", "YU"]
    act = ["E", "Ei", "Ep", "qs", "kw", "trA", "trV", "Yb1a", "Yb1b", "trK", "Tb1a", "Tb1b",
           "Yb2a", "Yb2b", "trB", "Tb2a", "Tb2b", "ex0", "ex1", "ex2", "ex3",
           "Yb3a", "Yb3b", "ex4", "ex5", "ex6", "ex7", "Tb3a", "Tb3b", "esink",
           "Yb4a", "Yb4b", "PT0", "Tb4a", "Tb4b", "PT1", "Yb5a", "Yb5b", "PT2", "Tb5a", "Tb5b",
           "X1", "PT3", "Tb6a", "Tb6b", "TAT", "Ua0", "Ua1", "Ub0", "Ub1", "Y0", "Y"]
    vec = ["Lp", "AN", "BT", "KT", "RT", "Vst", "G0", "G1", "sb0", "mx0", "sb1", "mx1",
           "Y1", "TT1", "sb2", "mx2", "T1", "sb3", "mx3", "m", "nm", "sd", "Y2", "TT2", "MKA0",
           "T2", "MKA1", "Y3", "MRB0", "TT3", "MRB1", "T3", "Y4", "MRK0", "TT4", "T4", "MRK1",
           "Y5", "TT5", "T5", "den", "rden", "Y6", "PV", "TT6", "bon", "Ha", "Hb"]
    pool = ["KP", "BP", "RK", "tab", "Wa", "BV", "Wb"]
    return pe, act, vec, pool


def plan(sems):
    npe, nact, nvec = norm_steps()
    lpe, lact, lvec, lpool = loop_steps()
    units = [f"u{u}" for u in range(20)]
    shift = [f"{k}{n}" for n in range(4) for k in "bdsc"]
    phases = {
        "norm": (npe, nact, nvec, [], 1),
        "rkv": ([f"u{n}" for n in range(4)], [f"{k}{n}" for n in range(4) for k in ("w", "e")],
                shift, [f"u{n}" for n in range(4)], 3),
        "lora": (["u0", "u1", "u2", "u3"] + [f"{k}{p}" for p in range(NP) for k in "wa"] + ["ss", "vt"],
                 ["w0", "e0", "w1", "e1", "w2", "e2", "w3", "e3", "th", "sg"]
                 + [f"sq{p}" for p in range(NP)] + [f"{k}{p}" for p in range(NP) for k in ("w_", "a_")]
                 + ["vt", "root"],
                 shift[:8] + [f"kr{p}" for p in range(NP)] + ["scan0", "scan1", "scan2", "scan3", "nmax", "rn"],
                 ["u0", "u1", "u2", "u3"], 1),
        "q": (["u0", "u1", "u2", "u3", "bc0", "bc1", "bc2", "bc3"],
              [f"{k}{n}" for n in range(4) for k in ("w", "e")],
              [f"{k}{p}" for p in range(NP) for k in ("kn", "t", "k", "b")],
              ["u0", "u1", "u2", "u3", "zy", "zt", "zp"], 1),
        "mix": (lpe, lact, lvec, lpool, NT),
        "gate": ([f"g{i}" for i in range(NT)] + [f"tr{b}_{i}" for i in range(NT) for b in range(2)],
                 [f"{k}{i}" for i in range(NT) for k in ("sq", "root", "h0_", "h1_")],
                 [f"{k}{i}" for i in range(NT) for k in
                  ("sum", "mean", "yc", "ssq", "var", "rstd", "yn", "lw", "lb", "bv", "g", "l0_", "l1_")],
                 ["kT", "vA"], 1),
        "out": ([f"u{n}" for n in range(8)], [f"u{n}" for n in range(8)], [], [f"u{n}" for n in range(8)], 1),
        "post": ([], [f"{k}{i}" for i in range(NT) for k in ("sqa", "sqb", "root")],
                 [f"{k}{i}" for i in range(NT) for k in ("ss", "ms", "rstd", "ma", "mb", "h")], [], 1),
        "fnorm": (npe, nact, nvec, [], 1),
        "up": ([f"{k}{n}" for n in range(2) for k in "gv"],
               [f"{k}{n}" for n in range(2) for k in ("wg", "wv", "eg", "ev", "ge", "hi")],
               [f"{k}{n}" for n in range(2) for k in
                ("ig", "iv", "cg", "cv", "1g", "1v", "0g", "0v", "kg", "kv", "m", "lo")],
               [f"{k}{n}" for n in range(2) for k in "gv"], PJ // 2),
        "down": ([f"u{n}" for n in range(11)], [f"u{n}" for n in range(11)] + ["f0", "f1"],
                 ["f2", "f3"], [f"u{n}" for n in range(11)], 2),
        "last": ([], [f"{k}{i}" for i in range(NT) for k in ("sq", "root")],
                 [f"{k}{i}" for i in range(NT) for k in ("ms", "rstd", "m", "y")], [], 1),
    }
    base = dict(pe=0, act=0, vec=4, pool=3)
    halves = []
    for _ in range(HALVES):
        half = {}
        for name, row in phases.items():
            half[name] = {}
            for eng, names in zip(("pe", "act", "vec", "pool"), row):
                s = Steps(sems[eng], names, base[eng], row[4])
                base[eng] = s.end()
                half[name][eng] = s
        halves.append(half)
    return halves, list(phases)


def build(nc, a, out):
    with ExitStack() as ctx:
        def sem(name):
            return ctx.enter_context(nc.semaphore(name))

        lo_end = (nc.sbuf_base + 31) // 32 * 32
        cursor = [lo_end]

        def sb(name, shape, dt=F32, at=None):
            size = int(np.prod(shape[1:])) * 4
            where = cursor[0] if at is None else at
            t = nc.alloc_sbuf_tensor_at("s_" + name, list(shape), dt, offset=where)
            if at is None:
                cursor[0] = where + (size + 31) // 32 * 32
            return t

        bank = [ctx.enter_context(nc.psum_tensor(f"bank{b}", [P, 512], F32)) for b in range(8)]

        par = sb("par", [P, NPAR])
        cst = sb("cst", [P, 128 * 4 + 64 * 7 + 32 + 8])
        ident, lower, upper, uppeq = (cst[:, 128 * n:128 * n + 128] for n in range(4))
        eye = cst[:, 512:576]
        level = [cst[:, 576 + 64 * n:640 + 64 * n] for n in range(6)]
        ones8 = cst[:, 960:992].rearrange("p (a b) -> p a b", a=NP)
        sink = cst[:, 992:1000]
        H = [sb(f"H{n}", [P, NP, HD]) for n in range(2)]
        HW = sb("HW", [P, NP, HD])
        shcar = sb("shcar", [P, 14])
        cvcar = sb("cvcar", [P, 2 * PJ, 2])
        kT = sb("kT", [P, P + HALF])
        vA = sb("vA", [P, NT + 1, P])
        gain = sb("gain", [P, D])
        small = sb("small", [P, 64])
        den8 = sb("den8", [P, 6, HEADS])
        ring_at = cursor[0]
        raw = [sb(f"raw{n}", [P, D]) for n in range(RAWS)]
        whi = [sb(f"whi{n}", [P, D], F32R) for n in range(SPLITS)]
        wlo = [sb(f"wlo{n}", [P, D], F32R) for n in range(SPLITS)]
        xhi_at = cursor[0]
        xhi = sb("xhi", [P, KT, HALF], F32R)
        xlo = sb("xlo", [P, KT, HALF], F32R)
        free = cursor[0]

        rkv = sb("rkv", [P, 3, NT, 512])
        sig = sb("sig", [P, NT, 512])
        L = sb("L", [P, NT, 512])
        av = sb("av", [P, NT, 512])
        kk = sb("kk", [P, NT, 512])
        qT = sb("qT", [P, NT, 512])
        rows_y, rows_a, bv = rkv[:, 0], rkv[:, 2], qT
        sg = sb("sg", [P, HALF])
        spread = sb("spread", [8, NP, P])
        edge = sb("edge", [P, HEADS, CH])
        table = sb("table", [P, HEADS, WIN])
        chunks = sb("chunks", [P, 512])
        lora = sb("lora", [P, 512])
        wg2 = sb("wg2", [P, 512])
        mid = cursor[0]
        wa = sb("wa", [P, HALF])
        gd = sb("gd", [P, HALF])
        vT = sb("vT", [P, HALF])
        th = sb("th", [HD, HALF])
        shr = [sb(f"shr{n}", [P, 1 + HALF]) for n in range(2)]
        shd = sb("shd", [P, HALF])
        rn = sb("rn", [8, 3, HALF])
        sq = [sb(f"sq{p}", [P, HALF]) for p in range(NP)]
        endB = cursor[0]

        cursor[0] = xhi_at
        pr = sb("pr", [P, HEADS, 2 * P])
        pT = sb("pT", [P, HEADS, 2, P])
        scb = sb("scb", [P, HEADS, WIN])
        qs = sb("qs", [P, NP, P])
        E, Ei, Ep, Lp = (sb(n, [P, 512]) for n in ("E", "Ei", "Ep", "Lp"))
        assert cursor[0] <= free
        cursor[0] = ring_at
        AN, BT, KTl, RT, Vst, KP, BP, RKp = (sb(n, [P, 512]) for n in ("AN", "BT", "KTl", "RT", "Vst", "KP", "BP", "RKp"))
        G, MKA, MRB, MRK = (sb(n, [P, HEADS, P]) for n in ("G", "MKA", "MRB", "MRK"))
        assert cursor[0] <= xhi_at
        cursor[0] = mid
        At, Kt, Bt, Vt = (sb(n, [P, 512]) for n in ("At", "Kt", "Bt", "Vt"))
        Tst, Tt, Yst = (sb(n, [P, HEADS, CH]) for n in ("Tst", "Tt", "Yst"))
        Ybd, Tbd = (sb(n, [P, HEADS, P]) for n in ("Ybd", "Tbd"))
        X1, U, TAT = (sb(n, [P, 512]) for n in ("X1", "U", "TAT"))
        kw = sb("kw", [P, WIN])
        endD = cursor[0]

        cursor[0] = free
        ghi = sb("ghi", [P, PJ, HALF], F32R)
        glo = sb("glo", [P, PJ, HALF], F32R)
        hres = sb("hres", [P, NT, D])
        cr = [[sb(f"cr{n}{m}", [P, 2 + HALF]) for m in range(2)] for n in range(2)]
        cc = [[sb(f"cc{n}{m}", [P, HALF]) for m in range(2)] for n in range(2)]
        gl = sb("gl", [P, HALF])
        endF = cursor[0]
        xt_at = free
        cursor[0] = mid
        gyn = sb("gyn", [P, 512])
        gsq = sb("gsq", [P, 512])
        lnw, lnb = sb("lnw", [P, 512]), sb("lnb", [P, 512])
        xt = [nc.alloc_sbuf_tensor_at(f"s_xt{n}", [P, D], F32, offset=xt_at + 4096 * n) for n in range(2)]
        xs = [nc.alloc_sbuf_tensor_at(f"s_xs{n}", [P, D], F32, offset=xt_at + 8192 + 4096 * n) for n in range(2)]
        jk = nc.alloc_sbuf_tensor_at("s_jk", [P, D], F32, offset=xt_at + 16384)
        mxo = nc.alloc_sbuf_tensor_at("s_mxo", [P, NT, D], F32, offset=xt_at + 20480)
        fo = nc.alloc_sbuf_tensor_at("s_fo", [P, NT, D], F32, offset=xhi_at)
        fj = nc.alloc_sbuf_tensor_at("s_fj", [P, D], F32, offset=xhi_at + 16384)
        assert max(endB, endD, endF, cursor[0]) <= nc.sbuf_usable_end

        sems = {e: sem(f"{e}_steps") for e in ("pe", "act", "vec", "pool")}
        const_in, mix_in = sem("const_in"), sem("mix_in")
        w_in_ = [sem(f"w_raw{n}") for n in range(RAWS)]
        x_in = [sem(f"x_in{n}") for n in range(2)]
        gain_in, ln_in, h_in, y_out = sem("gain_in"), sem("ln_in"), sem("h_in"), sem("y_out")
        halves, order = plan(sems)

        pe_steps, act_steps, vec_steps, pool_steps = (sems[n] for n in ("pe", "act", "vec", "pool"))

        def after(hf, phase, eng, name, it=0):
            return halves[hf][phase][eng].after(name, it)

        class Pass:

            def __init__(self, hf, ph, it=0):
                self.steps, self.it = halves[hf][ph]["vec"], it
                self.step = self.steps.step

            def after(self, name):
                return self.steps.after(name, self.it)

        def begin(e, hf, phase, me):
            steps = halves[hf][phase]
            if hf or phase != "norm":
                e.wait_ge(pe_steps, steps["pe"].base)
                e.wait_ge(act_steps, steps["act"].base)
            e.wait_ge(vec_steps, steps["vec"].base)
            e.wait_ge(pool_steps, steps["pool"].base)

        w1 = a["w_in"].rearrange("(k p) n -> p k n", p=P)
        wo = a["w_out"]
        wu = a["ffn_w_up"].rearrange("(k p) n -> p k n", p=P)
        wd = a["ffn_w_down"].rearrange("(k p) n -> p k n", p=P)
        UNITS = {"rkv": (4, 3), "lora": (4, 1), "q": (4, 1), "out": (8, 1), "up": (4, PJ // 2), "down": (11, 2)}

        def loads(ph, u):
            return 2 if ph == "q" else 1

        ub, yb = (bank[0], bank[3]), (bank[1], bank[4])

        count = [0] * RAWS
        first = {}
        for hf in range(HALVES):
            for ph, (n, times) in UNITS.items():
                per = [sum(loads(ph, u) for u in range(s, n, RAWS)) for s in range(RAWS)]
                first[hf, ph] = (list(count), per)
                count = [c + p_ * times for c, p_ in zip(count, per)]

        def landed(hf, ph, u, it=0):
            base, per = first[hf, ph]
            return 16 * (base[u % RAWS] + sum(loads(ph, v) for v in range(u % RAWS, u + 1, RAWS)) + per[u % RAWS] * it)

        def unit_name(ph, u):
            return ("g0", "v0", "g1", "v1")[u] if ph == "up" else f"u{u}"

        def split_hi(e, hf, ph, u, it, name, prev):
            e.wait_ge(w_in_[u % RAWS], landed(hf, ph, u, it))
            if prev is not None:
                e.wait_ge(pe_steps, after(hf, ph, "pe", *prev))
            e.activation(whi[u % SPLITS][:], raw[u % RAWS][:], ACT.Copy).then_inc(
                act_steps, halves[hf][ph]["act"].step(name))

        def split_lo(e, hf, ph, u, it, hi_name):
            e.wait_ge(act_steps, after(hf, ph, "act", hi_name, it))
            e.tensor_tensor(wlo[u % SPLITS][:], raw[u % RAWS][:], whi[u % SPLITS][:].bitcast(F32),
                            ALU.subtract).then_inc(pool_steps, halves[hf][ph]["pool"].step(unit_name(ph, u)))

        def before(ph, u, it, n, times):
            if u >= SPLITS:
                return unit_name(ph, u - SPLITS), it
            if times == 1:
                return None
            last = max(v for v in range(n) if v % SPLITS == u % SPLITS)
            return unit_name(ph, last), it - 1

        block = ctx.enter_context(nc.Block())

        @block.sync
        def _(e):
            for dst, src in ((par, "par"), (cst, "cst")):
                e.dma_start(dst[:], a[src]).then_inc(const_in, 16)

            def load(hf, ph, u, it, src, dst=None):
                n, times = UNITS[ph]
                s = halves[hf][ph]["pool"]
                if u >= RAWS:
                    e.wait_ge(s.sem, s.after(unit_name(ph, u - RAWS), it))
                elif times > 1 and not (isinstance(it, int) and it == 0):
                    last = max(v for v in range(n) if v % RAWS == u % RAWS)
                    e.wait_ge(s.sem, s.after(unit_name(ph, last), it - 1))
                elif s.base > 3:
                    e.wait_ge(s.sem, s.base)
                slot = raw[u % RAWS][:] if dst is None else dst
                e.dma_start(slot, src).then_inc(w_in_[u % RAWS], 16)

            for hf in range(HALVES):
                xrow = a["x"].rearrange("(t p) d -> p t d", p=P)
                if hf:
                    for eng in ("vec", "act"):
                        e.wait_ge(sems[eng], halves[hf]["norm"][eng].base)
                e.dma_start(gain[:], a["g_mix_pre"]).then_inc(gain_in, 16)
                for i in range(NT):
                    if i >= 2:
                        e.wait_ge(vec_steps, after(hf, "norm", "vec", f"xs{i - 2}"))
                        e.wait_ge(act_steps, after(hf, "norm", "act", f"sq{i - 2}"))
                    elif hf:
                        e.wait_ge(y_out, 16 * NT * hf)
                    if i == 0:
                        for dst, src in ((spread, "spread"), (edge, "edge"), (table, "alibi" if hf else "first"),
                                         (chunks, "chunks"), (lora, "lora"), (wg2, "wg2")):
                            e.dma_start(dst[:], a[src]).then_inc(mix_in, 16)
                    e.dma_start(xt[i % 2][:], xrow[:, hf * NT + i, :]).then_inc(x_in[i % 2], 16)
                r3 = [raw[s][:].rearrange("p (k n) -> p k n", k=KT) for s in range(RAWS)]
                r2 = [raw[s][:].rearrange("p (k n) -> p k n", k=2) for s in range(RAWS)]
                for u in range(4):
                    load(hf, "rkv", u, 0, w1[:, :, ATT + P * u:ATT + P * u + P], r3[u])
                with e.Fori(1, 3) as g:
                    for u in range(4):
                        load(hf, "rkv", u, g, w1[:, :, bass.ds(g * 512 + (ATT + P * u), P)], r3[u])
                for u, c in enumerate((2304, 2432, 512, 640)):
                    load(hf, "lora", u, 0, w1[:, :, c:c + P], r3[u])
                for u in range(4):
                    load(hf, "q", u, 0, w1[:, :, HD * u:HD * u + HD], r3[u][:, :, 0:HD])
                    e.dma_start(r3[u][:, :, HD:P], w1[:, :, 256 + HD * u:320 + HD * u]).then_inc(w_in_[u], 16)
                e.wait_ge(act_steps, after(hf, "mix", "act", "Y", NT - 1))
                e.wait_ge(vec_steps, after(hf, "mix", "vec", "Hb", NT - 1))
                e.wait_ge(sems["pe"], halves[hf]["mix"]["pe"].end())
                e.dma_start(lnw[:], a["ln_w"]).then_inc(ln_in, 16)
                e.dma_start(lnb[:], a["ln_b"]).then_inc(ln_in, 16)
                e.dma_start(gain[:], a["g_mix_post"]).then_inc(gain_in, 16)
                for u in range(8):
                    n, k = u // 4, 2 * (u % 4)
                    c = slice(512 * n, 512 * n + 512)
                    load(hf, "out", u, 0, wo.rearrange("(k p) n -> p k n", p=P)[:, k:k + 2, c], r2[u % RAWS])
                for eng in ("pe", "act", "vec"):
                    e.wait_ge(sems[eng], halves[hf]["gate"][eng].end())
                for i in range(NT):
                    e.dma_start(hres[:, i, :], xrow[:, hf * NT + i, :]).then_inc(h_in, 16)
                e.wait_ge(sems["vec"], halves[hf]["post"]["vec"].end())
                e.dma_start(gain[:], a["g_ffn_pre"]).then_inc(gain_in, 16)
                for u in range(4):
                    c = (u % 2) * FF + P * (u // 2)
                    load(hf, "up", u, 0, wu[:, :, c:c + P], r3[u])
                with e.Fori(1, PJ // 2) as g:
                    for u in range(4):
                        load(hf, "up", u, g, wu[:, :, bass.ds(g * 256 + ((u % 2) * FF + P * (u // 2)), P)], r3[u])
                e.dma_start(gain[:], a["g_ffn_post"]).then_inc(gain_in, 16)
                for n in range(2):
                    for u in range(11):
                        load(hf, "down", u, n, wd[:, 2 * u:2 * u + 2, 512 * n:512 * n + 512], r2[u % RAWS])
                yrow = out.rearrange("(t p) d -> p t d", p=P)
                for i in range(NT):
                    e.wait_ge(vec_steps, after(hf, "last", "vec", f"y{i}"))
                    e.dma_start(yrow[:, hf * NT + i, :], hres[:, i, :]).then_inc(y_out, 16)
            e.wait_ge(y_out, 16 * NT * HALVES)

        @block.tensor
        def _(e):
            e.wait_ge(const_in, 32)

            def turn(hf, ph, name, dst, pieces):
                for n, src in enumerate(pieces):
                    m = e.transpose(dst[:, P * n:P * n + P], src, ident)
                m.then_inc(pe_steps, halves[hf][ph]["pe"].step(name))

            def norm(hf, ph):
                begin(e, hf, ph, "pe")
                for i in range(NT):
                    e.wait_ge(vec_steps, after(hf, ph, "vec", f"xs{i}"))
                    for b in range(2):
                        if i:
                            e.wait_ge(vec_steps, after(hf, ph, "vec", f"lo{i - 1}_{b}"))
                        turn(hf, ph, f"tr{i}_{b}", bank[b],
                             [xs[i % 2][:, P * k:P * k + P] for k in range(4 * b, 4 * b + 4)])

            def columns(hf, ph, u, it, dst):
                e.wait_ge(pool_steps, after(hf, ph, "pool", unit_name(ph, u), it))
                hi = whi[u % SPLITS][:].rearrange("p (k n) -> p k n", k=KT)
                lo = wlo[u % SPLITS][:].rearrange("p (k n) -> p k n", k=KT)
                for k in range(KT):
                    e.matmul(dst[:], hi[:, k, :], xhi[:, k, :], start=k == 0, stop=False)
                    e.matmul(dst[:], hi[:, k, :], xlo[:, k, :], start=False, stop=False)
                    m = e.matmul(dst[:], lo[:, k, :], xhi[:, k, :], start=False, stop=k == KT - 1)
                m.then_inc(pe_steps, halves[hf][ph]["pe"].step(unit_name(ph, u)))

            def rows(hf, ph, u, it, lhs_hi, lhs_lo, k0, banks, first_k, last_k):
                e.wait_ge(pool_steps, after(hf, ph, "pool", unit_name(ph, u), it))
                hi = whi[u % SPLITS][:].rearrange("p (k n) -> p k n", k=2)
                lo = wlo[u % SPLITS][:].rearrange("p (k n) -> p k n", k=2)
                for kk_ in range(2):
                    k = k0 + kk_
                    for i in range(NT):
                        ts = slice(P * i, P * i + P)
                        e.matmul(banks[i][:], lhs_hi[:, k, ts], hi[:, kk_, :], start=k == first_k, stop=False)
                        e.matmul(banks[i][:], lhs_hi[:, k, ts], lo[:, kk_, :], start=False, stop=False)
                        m = e.matmul(banks[i][:], lhs_lo[:, k, ts], hi[:, kk_, :], start=False, stop=k == last_k)
                m.then_inc(pe_steps, halves[hf][ph]["pe"].step(unit_name(ph, u)))

            def lora_tiles(hf):
                ph = "lora"
                for p in range(NP):
                    if p == 0:
                        e.wait_ge(act_steps, after(hf, ph, "act", "th"))
                    else:
                        e.wait_ge(act_steps, after(hf, ph, "act", f"w_{p - 1}"))
                    ps = slice(P * p, P * p + P)
                    e.matmul(bank[4][:], lora[0:HD, ps], th[:], start=True, stop=True).then_inc(pe_steps, halves[hf][ph]["pe"].step(f"w{p}"))
                    if p == 0:
                        e.wait_ge(vec_steps, after(hf, ph, "vec", "s0"))
                    else:
                        e.wait_ge(act_steps, after(hf, ph, "act", f"a_{p - 1}"))
                    e.matmul(bank[5][:], lora[HD:P, ps], wa[HD:P, :], start=True, stop=True).then_inc(pe_steps, halves[hf][ph]["pe"].step(f"a{p}"))
                e.wait_ge(act_steps, after(hf, ph, "act", "sq3"))
                for p in range(NP):
                    m = e.matmul(bank[6][0:8, :], ones8[:, p, :], sq[p][:], start=p == 0, stop=p == NP - 1)
                m.then_inc(pe_steps, halves[hf][ph]["pe"].step("ss"))
                e.wait_ge(act_steps, after(hf, ph, "act", "e3"))
                turn(hf, ph, "vt", bank[7], [vT[:, P * i:P * i + P] for i in range(NT)])

            def mix_tile(hf, t):
                ph = "mix"
                st = halves[hf][ph]["pe"]

                def rows_of(e_):
                    return slice(HD * e_, HD * e_ + HD)

                def settle():
                    e.nop(nofuse=True)

                def pair(x, h):
                    return x[rows_of(h % 2), P * (h // 2):P * (h // 2) + P]

                def products(name, odd, dst, left, right):
                    for n in range(4):
                        h = 2 * n + odd
                        m = e.matmul(dst[:, P * n:P * n + P], pair(left, h), pair(right, h), start=n == 0,
                                     stop=n == 3, skip_group_check=True)
                    m.then_inc(pe_steps, st.step(name))

                def scores(j):
                    if j >= 2:
                        e.wait_ge(vec_steps, after(hf, ph, "vec", f"sb{j - 2}", t))
                    b = bank[6 + j % 2]
                    for n in range(2):
                        m = e.matmul(b[:, WIN * n:WIN * n + WIN], qs[rows_of(j % 2), 2 * (j // 2) + n, :],
                                     kw[rows_of(j % 2), :], start=n == 0, stop=n == 1,
                                     skip_group_check=True)
                    m.then_inc(pe_steps, st.step(f"sc{j}"))

                def per_head(name, dst, left, right, start, stop=False):
                    for h in range(HEADS):
                        m = e.matmul(dst[:, CH * h:CH * h + CH], left(h), right(h), start=start and h == 0,
                                     stop=stop and h == HEADS - 1, skip_group_check=True)
                    m.then_inc(pe_steps, st.step(name))

                def Y(lv):
                    if lv == 1:
                        e.wait_ge(vec_steps, after(hf, ph, "vec", "G1", t))
                    else:
                        e.wait_ge(vec_steps, after(hf, ph, "vec", f"TT{lv - 1}", t))
                    per_head(f"Y{lv}", bank[2], lambda h: G[:, h, :],
                             (lambda h: eye) if lv == 1 else (lambda h: Tt[:, h, :]), True, True)

                def TT(lv):
                    e.wait_ge(vec_steps, after(hf, ph, "vec", f"Y{lv}", t))
                    if lv > 1:
                        e.wait_ge(act_steps, after(hf, ph, "act", f"Tb{lv - 1}b", t))
                    per_head(f"TT{lv}", bank[3], (lambda h: ident) if lv == 1 else (lambda h: Tbd[:, h, :]),
                             lambda h: Yst[:, h, :], True, True)

                def T(lv):
                    e.wait_ge(act_steps, after(hf, ph, "act", f"Yb{lv}b", t))
                    per_head(f"T{lv}", bank[4], lambda h: Ybd[:, h, :],
                             (lambda h: eye) if lv == 1 else (lambda h: Tst[:, h, :]), True, True)

                def probs(n):
                    e.wait_ge(act_steps, after(hf, ph, "act", f"ex{2 * n + 1}", t))
                    if n < 2:
                        e.wait_ge(vec_steps, after(hf, ph, "vec", f"sb{n + 2}", t))
                    else:
                        e.wait_ge(act_steps, after(hf, ph, "act", f"PT{n - 2}", t))
                    turn(hf, ph, f"PT{n}", bank[6 + n % 2],
                         [pr[:, 2 * n + i // 2, P * (i % 2):P * (i % 2) + P] for i in range(4)])

                e.wait_ge(vec_steps, after(hf, ph, "vec", "BT", t))
                e.wait_ge(vec_steps, after(hf, ph, "vec", "Hb", t - 1))
                products("G0", 0, bank[2], AN, BT)
                products("G1", 1, bank[3], AN, BT)
                turn(hf, ph, "trA", bank[0], [AN[:, P * p:P * p + P] for p in range(NP)])
                e.wait_ge(vec_steps, after(hf, ph, "vec", "Vst", t))
                e.wait_ge(act_steps, after(hf, ph, "act", "Y", t - 1))
                turn(hf, ph, "trV", bank[1], [Vst[:, P * p:P * p + P] for p in range(NP)])
                e.wait_ge(act_steps, after(hf, ph, "act", "kw", t))
                scores(0)
                scores(1)
                Y(1)
                e.wait_ge(pool_steps, after(hf, ph, "pool", "KP", t))
                turn(hf, ph, "trK", bank[5], [KP[:, P * p:P * p + P] for p in range(NP)])
                TT(1)
                scores(2)
                T(1)
                scores(3)
                Y(2)
                e.wait_ge(pool_steps, after(hf, ph, "pool", "BP", t))
                e.wait_ge(act_steps, after(hf, ph, "act", "trA", t))
                turn(hf, ph, "trB", bank[0], [BP[:, P * p:P * p + P] for p in range(NP)])
                TT(2)
                e.wait_ge(vec_steps, after(hf, ph, "vec", "RT", t))
                e.wait_ge(act_steps, after(hf, ph, "act", "trV", t))
                products("MKA0", 0, bank[1], KTl, AN)
                T(2)
                e.wait_ge(act_steps, after(hf, ph, "act", "trK", t))
                products("MKA1", 1, bank[5], KTl, AN)
                Y(3)
                e.wait_ge(act_steps, after(hf, ph, "act", "trB", t))
                products("MRB0", 0, bank[0], BT, RT)
                TT(3)
                e.wait_ge(vec_steps, after(hf, ph, "vec", "MKA0", t))
                products("MRB1", 1, bank[1], BT, RT)
                T(3)
                probs(0)
                Y(4)
                e.wait_ge(vec_steps, after(hf, ph, "vec", "MKA1", t))
                products("MRK0", 0, bank[5], KTl, RT)
                TT(4)
                probs(1)
                T(4)
                e.wait_ge(vec_steps, after(hf, ph, "vec", "MRB0", t))
                products("MRK1", 1, bank[0], KTl, RT)
                Y(5)
                probs(2)
                TT(5)
                e.wait_ge(vec_steps, after(hf, ph, "vec", "MRB1", t))
                per_head("X1", bank[1], lambda h: MKA[:, h, :], lambda h: Vt[:, CH * h:CH * h + CH], True, True)
                T(5)
                probs(3)
                Y(6)
                e.wait_ge(act_steps, after(hf, ph, "act", "PT3", t))
                for h in range(HEADS):
                    for n in range(2):
                        m = e.matmul(bank[6][:, CH * h:CH * h + CH], pT[:, h, n, :],
                                     vA[:, bass.ds(t + n, 1), HD * (h // 4):HD * (h // 4) + HD].rearrange("p a d -> p (a d)"),
                                     start=h == 0 and n == 0, stop=h == HEADS - 1 and n == 1,
                                     skip_group_check=True)
                m.then_inc(pe_steps, st.step("PV"))
                TT(6)
                e.wait_ge(pool_steps, after(hf, ph, "pool", "RK", t))
                for p in range(NP):
                    m = e.matmul(bank[7][:, 2 * p:2 * p + 2], RKp[:, P * p:P * p + P],
                                 par[:, RK + 2 * p:RK + 2 * p + 2], start=p == 0, stop=p == 3,
                                 skip_group_check=True)
                m.then_inc(pe_steps, st.step("bonus"))
                e.wait_ge(act_steps, after(hf, ph, "act", "Tb6b", t))
                e.wait_ge(vec_steps, after(hf, ph, "vec", "MRK1", t))
                for h in range(HEADS):
                    m = e.matmul(ub[h % 2][:, CH * (h // 2):CH * (h // 2) + CH], Tbd[:, h, :],
                                 X1[:, CH * h:CH * h + CH], start=h < 2, stop=False, skip_group_check=True)
                m.then_inc(pe_steps, st.step("Z"))
                for h in range(HEADS):
                    m = e.matmul(bank[5][rows_of(h % 2), P * (h // 2):P * (h // 2) + P],
                                 At[:, CH * h:CH * h + CH], Tbd[:, h, :], start=h < 2, stop=h >= 6,
                                 skip_group_check=True)
                m.then_inc(pe_steps, st.step("TAT"))

                def chunk(c):
                    cs, nm = rows_of(c), "ab"[c]
                    state = H[c]
                    hps = bank[5] if c == 0 else bank[2]
                    if c == 0:
                        e.wait_ge(act_steps, after(hf, ph, "act", "TAT", t))
                        e.wait_ge(vec_steps, after(hf, ph, "vec", "Hb", t - 1))
                    else:
                        e.wait_ge(vec_steps, after(hf, ph, "vec", "Ha", t))
                    settle()
                    for h in range(HEADS):
                        m = e.matmul(ub[h % 2][cs, CH * (h // 2):CH * (h // 2) + CH],
                                     TAT[rows_of(h % 2), P * (h // 2) + CH * c:P * (h // 2) + CH * c + CH],
                                     state[rows_of(h % 2), h // 2, :], start=False, stop=h == 7,
                                     skip_group_check=True)
                    m.then_inc(pe_steps, st.step("UA" + nm))
                    for h in range(HEADS):
                        m = e.matmul(hps[rows_of(h % 2), HD * (h // 2):HD * (h // 2) + HD],
                                     Kt[cs, HD * h:HD * h + HD], Vt[cs, HD * h:HD * h + HD],
                                     start=h < 2, stop=False, skip_group_check=True)
                    m.then_inc(pe_steps, st.step("HV" + nm))
                    if c == 0:
                        for h in range(HEADS):
                            e.matmul(yb[h % 2][:, CH * (h // 2):CH * (h // 2) + CH], MRK[:, h, :],
                                     Vt[:, CH * h:CH * h + CH], start=h < 2, stop=False, skip_group_check=True)
                    for h in range(HEADS):
                        m = e.matmul(yb[h % 2][cs, CH * (h // 2):CH * (h // 2) + CH],
                                     RT[rows_of(h % 2), P * (h // 2) + CH * c:P * (h // 2) + CH * c + CH],
                                     state[rows_of(h % 2), h // 2, :], start=False, stop=False,
                                     skip_group_check=True)
                    m.then_inc(pe_steps, st.step("RH" + nm))
                    e.wait_ge(act_steps, after(hf, ph, "act", "U" + nm + "1", t))
                    settle()
                    for h in range(HEADS):
                        m = e.matmul(hps[rows_of(h % 2), HD * (h // 2):HD * (h // 2) + HD],
                                     Bt[cs, HD * h:HD * h + HD], U[cs, HD * h:HD * h + HD],
                                     start=False, stop=h >= 6, skip_group_check=True)
                    m.then_inc(pe_steps, st.step("HB" + nm))

                chunk(0)
                chunk(1)
                for h in range(HEADS):
                    m = e.matmul(yb[h % 2][:, CH * (h // 2):CH * (h // 2) + CH], MRB[:, h, :],
                                 U[:, CH * h:CH * h + CH], start=False, stop=h >= 6, skip_group_check=True)
                m.then_inc(pe_steps, st.step("YU"))

            for hf in range(HALVES):
                norm(hf, "norm")
                begin(e, hf, "rkv", "pe")
                with e.Fori(0, 3) as g:
                    for u in range(4):
                        if u < 4:
                            e.wait_ge(act_steps, after(hf, "rkv", "act", f"e{u}", g - 1))
                        columns(hf, "rkv", u, g, bank[u])
                e.wait_ge(mix_in, 96 * (hf + 1))
                for u in range(4):
                    e.wait_ge(act_steps, after(hf, "rkv", "act", f"e{u}", 2))
                    columns(hf, "lora", u, 0, bank[u])
                lora_tiles(hf)
                for u in range(4):
                    e.wait_ge(act_steps, after(hf, "lora", "act", f"e{u}"))
                    columns(hf, "q", u, 0, bank[u])
                for p in range(NP):
                    if p == 0:
                        e.wait_ge(vec_steps, after(hf, "lora", "vec", "rn"))
                        e.wait_ge(act_steps, after(hf, "lora", "act", "root"))
                    e.matmul(bank[4 + p][:], spread[:, p, :], rn[:, 2, :], start=True, stop=True).then_inc(pe_steps, halves[hf]["q"]["pe"].step(f"bc{p}"))
                begin(e, hf, "mix", "pe")
                with e.Fori(0, NT) as t:
                    mix_tile(hf, t)
                begin(e, hf, "gate", "pe")

                def g_tile(i):
                    e.matmul(bank[4 + i][:], sg[:, P * i:P * i + P], wg2[:], start=True, stop=True).then_inc(pe_steps, halves[hf]["gate"]["pe"].step(f"g{i}"))

                for i in range(NT):
                    g_tile(i)
                for i in range(NT):
                    for b in range(2):
                        e.wait_ge(vec_steps, after(hf, "gate", "vec", f"g{i}"))
                        if i:
                            e.wait_ge(vec_steps, after(hf, "gate", "vec", f"l{b}_{i - 1}"))
                        turn(hf, "gate", f"tr{b}_{i}", bank[b], [(rows_y if b else rows_a)[:, i, P * k:P * k + P] for k in range(4)])
                begin(e, hf, "out", "pe")
                for u in range(8):
                    n = u // 4
                    rows(hf, "out", u, 0, xhi, xlo, 2 * (u % 4), bank[4 * n:4 * n + 4], 0, KT - 1)
                norm(hf, "fnorm")
                begin(e, hf, "up", "pe")
                with e.Fori(0, PJ // 2) as g:
                    for u in range(4):
                        e.wait_ge(act_steps, after(hf, "up", "act", f"e{'gv'[u % 2]}{u // 2}", g - 1))
                        columns(hf, "up", u, g, bank[u])
                begin(e, hf, "down", "pe")
                with e.Fori(0, 2) as n:
                    e.wait_ge(act_steps, after(hf, "down", "act", "f1", n - 1))
                    e.wait_ge(vec_steps, after(hf, "down", "vec", "f3", n - 1))
                    for u in range(11):
                        rows(hf, "down", u, n, ghi, glo, 2 * u, bank[4:8], 0, PJ - 1)

        @block.scalar
        def _(e):
            e.wait_ge(const_in, 32)

            def norm(hf, ph, src):
                begin(e, hf, ph, "act")
                st = halves[hf][ph]["act"]
                for i in range(NT):
                    if ph == "norm":
                        e.wait_ge(x_in[i % 2], 16 * (2 * hf + i // 2 + 1))
                    e.activation(jk[:], src(i), ACT.Square, accum_out=small[:, i:i + 1]).then_inc(act_steps, st.step(f"sq{i}"))
                    e.wait_ge(vec_steps, after(hf, ph, "vec", f"ms{i}"))
                    e.activation(small[:, 8 + i:9 + i], small[:, 4 + i:5 + i], ACT.Sqrt).then_inc(act_steps, st.step(f"root{i}"))
                    for b in range(2):
                        e.wait_ge(pe_steps, after(hf, ph, "pe", f"tr{i}_{b}"))
                        e.activation(xhi[:, 4 * b:4 * b + 4, P * i:P * i + P],
                                             bank[b][:].rearrange("p (k n) -> p k n", k=4), ACT.Copy).then_inc(act_steps, st.step(f"hi{i}_{b}"))

            def mix_tile(hf, t):
                ph = "mix"
                st = halves[hf][ph]["act"]

                def act(name, dst, src, fn=ACT.Copy, **kw):
                    e.activation(dst, src, fn, **kw).then_inc(act_steps, st.step(name))

                def tile(x):
                    return x[:, bass.ds(t, 1), :].rearrange("p a d -> p (a d)")

                def parity(x, odd):
                    return x.rearrange("p (a b n) -> p b a n", b=2, n=CH)[:, odd]

                def parity_bank(x):
                    return x[:, 0:4 * CH].rearrange("p (a n) -> p a n", a=4)

                def blocks(name, dst, src):
                    for c in range(2):
                        cs = slice(CH * c, CH * c + CH)
                        act(f"{name}{'ab'[c]}", dst[cs, :, cs], src[cs, :, :])

                def Yb(lv):
                    e.wait_ge(vec_steps, after(hf, ph, "vec", f"Y{lv}", t))
                    blocks(f"Yb{lv}", Ybd, Yst)

                def Tb(lv):
                    e.wait_ge(vec_steps, after(hf, ph, "vec", f"T{lv}" if lv < 6 else "TT6", t))
                    blocks(f"Tb{lv}", Tbd, Tst if lv < 6 else Tt)

                def out_of(name, dst, b, pe_name):
                    e.wait_ge(pe_steps, after(hf, ph, "pe", pe_name, t))
                    act(name, dst, b)

                def ex(h):
                    act(f"ex{h}", pr[:, h, CH:2 * P], scb[:, h, :], ACT.Exp, bias=den8[:, 1, h:h + 1],
                        accum_out=den8[:, 3, h:h + 1])

                def pt(n):
                    out_of(f"PT{n}", pT[:, 2 * n:2 * n + 2, :, :],
                           bank[6 + n % 2][:].rearrange("p (a b c) -> p a b c", a=2, b=2), f"PT{n}")

                e.wait_ge(vec_steps, after(hf, ph, "vec", "Hb", t - 1))
                e.wait_ge(pool_steps, after(hf, ph, "pool", "Wb", t - 1))
                act("E", E[:], tile(L), ACT.Exp, scale=-DECAY)
                act("Ei", Ei[:], tile(L), ACT.Exp, scale=DECAY)
                e.wait_ge(vec_steps, after(hf, ph, "vec", "Lp", t))
                act("Ep", Ep[:], Lp[:], ACT.Exp, scale=-DECAY)
                act("qs", qs[:], tile(qT).rearrange("p (j n) -> p j n", j=NP), scale=HD ** -0.5)
                act("kw", kw[:], kT[:, bass.ds(t * P + CH, WIN)])
                e.wait_ge(pe_steps, after(hf, ph, "pe", "YU", t - 1))
                e.wait_ge(pool_steps, after(hf, ph, "pool", "BV", t - 1))
                out_of("trA", At[:], bank[0][:], "trA")
                out_of("trV", Vt[:], bank[1][:], "trV")
                Yb(1)
                out_of("trK", Kt[:], bank[5][:], "trK")
                Tb(1)
                Yb(2)
                out_of("trB", Bt[:], bank[0][:], "trB")
                Tb(2)
                e.wait_ge(vec_steps, after(hf, ph, "vec", "nm", t))
                for h in range(4):
                    ex(h)
                Yb(3)
                for h in range(4, 8):
                    ex(h)
                Tb(3)
                e.wait_ge(vec_steps, after(hf, ph, "vec", "sd", t))
                act("esink", den8[:, 4, :], den8[:, 2, :], ACT.Exp)
                Yb(4)
                pt(0)
                Tb(4)
                pt(1)
                Yb(5)
                pt(2)
                Tb(5)
                out_of("X1", X1[:], bank[1][:], "X1")
                pt(3)
                Tb(6)
                out_of("TAT", TAT[:], bank[5][:], "TAT")
                for c in range(2):
                    cs, nm = slice(CH * c, CH * c + CH), "ab"[c]
                    for odd in range(2):
                        out_of(f"U{nm}{odd}", parity(U[cs, :], odd), parity_bank(ub[odd][cs, :]), "UA" + nm)
                e.wait_ge(pe_steps, after(hf, ph, "pe", "YU", t))
                for odd, nm in enumerate(("Y0", "Y")):
                    act(nm, parity(tile(rows_y), odd), parity_bank(yb[odd]))

            for hf in range(HALVES):
                norm(hf, "norm", lambda i: xt[i % 2][:])
                begin(e, hf, "rkv", "act")
                with e.Fori(0, 3) as g:
                    for n in range(4):
                        split_hi(e, hf, "rkv", n, g, f"w{n}", before("rkv", n, g, 4, 3))
                        e.wait_ge(pe_steps, after(hf, "rkv", "pe", f"u{n}", g))
                        e.wait_ge(vec_steps, after(hf, "rkv", "vec", f"c{n - 2}" if n >= 2 else f"c{n + 2}", g if n >= 2 else g - 1))
                        e.activation(shr[n % 2][:, 1:1 + HALF], bank[n][:], ACT.Copy).then_inc(act_steps, halves[hf]["rkv"]["act"].step(f"e{n}"))
                begin(e, hf, "lora", "act")
                st = halves[hf]["lora"]["act"]
                dst = [shr[0][:, 1:1 + HALF], shr[1][:, 1:1 + HALF], kT[:, P:P + HALF], vT[:]]
                for n in range(4):
                    split_hi(e, hf, "lora", n, 0, f"w{n}", before("lora", n, 0, 4, 1))
                    e.wait_ge(pe_steps, after(hf, "lora", "pe", f"u{n}"))
                    e.activation(dst[n], bank[n][:], ACT.Copy).then_inc(act_steps, st.step(f"e{n}"))
                e.wait_ge(vec_steps, after(hf, "lora", "vec", "s1"))
                e.activation(th[:], wa[0:HD, :], ACT.Tanh).then_inc(act_steps, st.step("th"))
                e.activation(sg[:], gd[:], ACT.Sigmoid).then_inc(act_steps, st.step("sg"))
                for p in range(NP):
                    k_p = rkv[:, 1, :, P * p:P * p + P]
                    e.activation(sq[p][:].rearrange("p (t n) -> p t n", t=NT), k_p, ACT.Square,
                                         scale=par[:, KK_ + p:KK_ + p + 1]).then_inc(act_steps, st.step(f"sq{p}"))
                for p in range(NP):
                    for nm, dst_, off, b in (("w", sig, W0, 4), ("a", av, A0, 5)):
                        e.wait_ge(pe_steps, after(hf, "lora", "pe", f"{nm}{p}"))
                        e.activation(dst_[:, :, P * p:P * p + P],
                                             bank[b][:].rearrange("p (t n) -> p t n", t=NT), ACT.Sigmoid,
                                             bias=par[:, off + p:off + p + 1]).then_inc(act_steps, st.step(f"{nm}_{p}"))
                e.wait_ge(pe_steps, after(hf, "lora", "pe", "vt"))
                e.activation(vA[:, 1:1 + NT, :], bank[7][:].rearrange("p (t n) -> p t n", t=NT), ACT.Copy).then_inc(act_steps, st.step("vt"))
                e.wait_ge(pe_steps, after(hf, "lora", "pe", "ss"))
                e.activation(rn[:, 0, :], bank[6][0:8, :], ACT.Sqrt).then_inc(act_steps, st.step("root"))
                st = halves[hf]["q"]["act"]
                for n in range(4):
                    e.wait_ge(w_in_[n], landed(hf, "q", n))
                    if n < 2:
                        e.wait_ge(pe_steps, after(hf, "lora", "pe", f"u{n + 2}"))
                    else:
                        e.wait_ge(pe_steps, after(hf, "q", "pe", f"u{n - 2}"))
                    e.activation(whi[n % 2][:], raw[n][:], ACT.Copy).then_inc(act_steps, st.step(f"w{n}"))
                    e.wait_ge(pe_steps, after(hf, "q", "pe", f"u{n}"))
                    e.activation(qT[:, :, P * n:P * n + P], bank[n][:].rearrange("p (t n) -> p t n", t=NT), ACT.Copy).then_inc(act_steps, st.step(f"e{n}"))
                begin(e, hf, "mix", "act")
                with e.Fori(0, NT) as t:
                    mix_tile(hf, t)
                begin(e, hf, "gate", "act")
                st = halves[hf]["gate"]["act"]
                for i in range(NT):
                    e.wait_ge(vec_steps, after(hf, "gate", "vec", f"yc{i}"))
                    e.activation(gsq[:], gyn[:], ACT.Square).then_inc(act_steps, st.step(f"sq{i}"))
                    e.wait_ge(vec_steps, after(hf, "gate", "vec", f"var{i}"))
                    e.activation(den8[:, 2, :], den8[:, 1, :], ACT.Sqrt).then_inc(act_steps, st.step(f"root{i}"))
                    for b in range(2):
                        e.wait_ge(pe_steps, after(hf, "gate", "pe", f"tr{b}_{i}"))
                        e.activation(xhi[:, 4 * b:4 * b + 4, P * i:P * i + P],
                                             bank[b][:].rearrange("p (k n) -> p k n", k=4), ACT.Copy).then_inc(act_steps, st.step(f"h{b}_{i}"))
                begin(e, hf, "out", "act")
                for u in range(8):
                    e.wait_ge(w_in_[u % RAWS], landed(hf, "out", u))
                    if u >= SPLITS:
                        e.wait_ge(pe_steps, after(hf, "out", "pe", f"u{u - SPLITS}"))
                    e.activation(whi[u % SPLITS][:], raw[u % RAWS][:], ACT.Copy).then_inc(act_steps, halves[hf]["out"]["act"].step(f"u{u}"))
                begin(e, hf, "post", "act")
                st = halves[hf]["post"]["act"]
                for i in range(NT):
                    e.activation(jk[:, 0:512], bank[i][:], ACT.Square, accum_out=small[:, 16:17]).then_inc(act_steps, st.step(f"sqa{i}"))
                    e.activation(jk[:, 512:1024], bank[4 + i][:], ACT.Square, accum_out=small[:, 17:18]).then_inc(act_steps, st.step(f"sqb{i}"))
                    e.wait_ge(vec_steps, after(hf, "post", "vec", f"ms{i}"))
                    e.activation(small[:, 20:21], small[:, 19:20], ACT.Sqrt).then_inc(act_steps, st.step(f"root{i}"))
                norm(hf, "fnorm", lambda i: hres[:, i, :])
                begin(e, hf, "up", "act")
                st = halves[hf]["up"]["act"]
                with e.Fori(0, PJ // 2) as g:
                    for n in range(2):
                        for m, k in enumerate("gv"):
                            u = 2 * n + m
                            split_hi(e, hf, "up", u, g, f"w{k}{n}", before("up", u, g, 4, 11))
                        for m, k in enumerate("gv"):
                            e.wait_ge(pe_steps, after(hf, "up", "pe", f"{k}{n}", g))
                            e.wait_ge(vec_steps, after(hf, "up", "vec", f"k{k}{n}", g - 1))
                            e.activation(cr[n][m][:, 2:2 + HALF], bank[2 * n + m][:], ACT.Copy).then_inc(act_steps, st.step(f"e{k}{n}"))
                        e.wait_ge(vec_steps, after(hf, "up", "vec", f"0g{n}", g))
                        e.wait_ge(vec_steps, after(hf, "up", "vec", f"m{1 - n}", g if n else g - 1))
                        e.activation(gl[:], cc[n][0][:], ACT.Gelu_apprx_tanh).then_inc(act_steps, st.step(f"ge{n}"))
                        e.wait_ge(vec_steps, after(hf, "up", "vec", f"m{n}", g))
                        e.activation(ghi[:, bass.ds(g * 2 + n, 1), :].rearrange("p a d -> p (a d)"),
                                             cc[n][0][:], ACT.Copy).then_inc(act_steps, st.step(f"hi{n}"))
                begin(e, hf, "down", "act")
                st = halves[hf]["down"]["act"]
                with e.Fori(0, 2) as n:
                    for u in range(11):
                        split_hi(e, hf, "down", u, n, f"u{u}", before("down", u, n, 11, 2))
                    e.wait_ge(pe_steps, after(hf, "down", "pe", "u10", n))
                    for i in range(2):
                        e.activation(fo[:, i, bass.ds(n * 512, 512)], bank[4 + i][:], ACT.Copy).then_inc(act_steps, st.step(f"f{i}"))
                begin(e, hf, "last", "act")
                st = halves[hf]["last"]["act"]
                for i in range(NT):
                    e.activation(fj[:], fo[:, i, :], ACT.Square, accum_out=small[:, i:i + 1]).then_inc(act_steps, st.step(f"sq{i}"))
                    e.wait_ge(vec_steps, after(hf, "last", "vec", f"ms{i}"))
                    e.activation(small[:, 8 + i:9 + i], small[:, 4 + i:5 + i], ACT.Sqrt).then_inc(act_steps, st.step(f"root{i}"))

        @block.vector
        def _(e):
            for n, cell in enumerate((shcar[:], cvcar[:], vA[:, 0, :], H[0][:])):
                e.memset(cell, 0.0).then_inc(sems["vec"], 1)
            e.wait_ge(const_in, 32)

            def mean_square(v, i, name="ms"):
                e.tensor_scalar(small[:, 4 + i:5 + i], small[:, i:i + 1], 1.0 / D, EPS, ALU.mult, ALU.add).then_inc(vec_steps, v.step(f"{name}{i}"))

            def norm(hf, ph, src, gains):
                begin(e, hf, ph, "vec")
                e.wait_ge(gain_in, 16 * gains)
                v = Pass(hf, ph)
                for i in range(NT):
                    e.wait_ge(act_steps, after(hf, ph, "act", f"sq{i}"))
                    mean_square(v, i)
                    e.wait_ge(act_steps, after(hf, ph, "act", f"root{i}"))
                    e.reciprocal(small[:, 12 + i:13 + i], small[:, 8 + i:9 + i]).then_inc(vec_steps, v.step(f"rstd{i}"))
                    if i >= 2:
                        e.wait_ge(pe_steps, after(hf, ph, "pe", f"tr{i - 2}_1"))
                    e.wait_ge(vec_steps, v.after(f"rstd{i}"))
                    e.scalar_tensor_tensor(xs[i % 2][:], src(i), small[:, 12 + i:13 + i], gain[:], ALU.mult, ALU.mult).then_inc(vec_steps, v.step(f"xs{i}"))
                    for b in range(2):
                        e.wait_ge(act_steps, after(hf, ph, "act", f"hi{i}_{b}"))
                        cols = (slice(None), slice(4 * b, 4 * b + 4), slice(P * i, P * i + P))
                        e.tensor_tensor(xlo[cols], bank[b][:].rearrange("p (k n) -> p k n", k=4), xhi[cols].bitcast(F32), ALU.subtract).then_inc(vec_steps, v.step(f"lo{i}_{b}"))

            def shift_tile(v, n, copied, mu, car, dst, four=True):
                s = shr[n % 2]
                e.tensor_copy(s[:, 0:1], car).then_inc(vec_steps, v.step(f"b{n}"))
                e.wait_ge(act_steps, copied)
                e.wait_ge(vec_steps, v.after(f"b{n}"))
                e.tensor_tensor(shd[:], s[:, 0:HALF], s[:, 1:1 + HALF], ALU.subtract).then_inc(vec_steps, v.step(f"d{n}"))
                e.wait_ge(vec_steps, v.after(f"d{n}"))
                x, y = shd[:], s[:, 1:1 + HALF]
                if four:
                    x, y = (z.rearrange("p (t n) -> p t n", t=NT) for z in (x, y))
                e.scalar_tensor_tensor(dst, x, mu, y, ALU.mult, ALU.add).then_inc(vec_steps, v.step(f"s{n}"))
                e.tensor_copy(car, s[:, HALF:HALF + 1]).then_inc(vec_steps, v.step(f"c{n}"))

            def mix_tile(hf, t):
                ph = "mix"
                v = Pass(hf, ph, t)

                def tile(x):
                    return x[:, bass.ds(t, 1), :].rearrange("p a d -> p (a d)")

                def four(x):
                    return x.rearrange("p (h n) -> p h n", h=4)

                def eight(x):
                    return x.rearrange("p (h n) -> p h n", h=HEADS)

                def over(x, n):
                    return x.unsqueeze(1).to_broadcast([P, n, x.shape[1]])

                def each(x):
                    return x.unsqueeze(2).to_broadcast([P, HEADS, CH])

                def masked(name, dst, odd, b, mask):
                    e.wait_ge(pe_steps, after(hf, ph, "pe", name, t))
                    e.tensor_tensor(dst[:].rearrange("p (a b) n -> p b a n", b=2)[:, odd], four(b[:]), over(mask, 4), ALU.mult).then_inc(vec_steps, v.step(name))

                def scores(j):
                    e.wait_ge(pe_steps, after(hf, ph, "pe", f"sc{j}", t))
                    h2 = slice(4 * (j % 2) + 2 * (j // 2), 4 * (j % 2) + 2 * (j // 2) + 2)
                    e.tensor_tensor(scb[:, h2, :], bank[6 + j % 2][:, 0:2 * WIN].rearrange("p (a n) -> p a n", a=2), table[:, h2, :], ALU.add).then_inc(vec_steps, v.step(f"sb{j}"))
                    e.wait_ge(vec_steps, v.after(f"sb{j}"))
                    e.tensor_reduce(den8[:, 0, h2], scb[:, h2, :], AX, ALU.max).then_inc(vec_steps, v.step(f"mx{j}"))

                def Y(lv):
                    e.wait_ge(pe_steps, after(hf, ph, "pe", f"Y{lv}", t))
                    e.tensor_tensor(Yst[:], eight(bank[2][:]), over(level[lv - 1], HEADS), ALU.mult).then_inc(vec_steps, v.step(f"Y{lv}"))

                def TT(lv):
                    e.wait_ge(pe_steps, after(hf, ph, "pe", f"TT{lv}", t))
                    e.tensor_tensor(Tt[:], eight(bank[3][:]), over(eye, HEADS) if lv == 1 else Tt[:], ALU.add).then_inc(vec_steps, v.step(f"TT{lv}"))

                def T(lv):
                    e.wait_ge(pe_steps, after(hf, ph, "pe", f"T{lv}", t))
                    if lv > 1:
                        e.wait_ge(act_steps, after(hf, ph, "act", f"Tb{lv - 1}b", t))
                    e.tensor_tensor(Tst[:], eight(bank[4][:]), over(eye, HEADS) if lv == 1 else Tst[:], ALU.add).then_inc(vec_steps, v.step(f"T{lv}"))

                e.wait_ge(act_steps, after(hf, ph, "act", "Y", t - 1))
                e.wait_ge(pe_steps, after(hf, ph, "pe", "YU", t - 1))
                e.wait_ge(pool_steps, after(hf, ph, "pool", "Wb", t - 1))
                e.tensor_tensor(Lp[:], tile(L), tile(sig), ALU.subtract).then_inc(vec_steps, v.step("Lp"))
                e.wait_ge(act_steps, after(hf, ph, "act", "Ep", t))
                e.scalar_tensor_tensor(AN[:], tile(kk), -1.0, Ep[:], ALU.mult, ALU.mult).then_inc(vec_steps, v.step("AN"))
                e.tensor_tensor(BT[:], tile(av), Ei[:], ALU.mult).then_inc(vec_steps, v.step("BT"))
                e.tensor_tensor(KTl[:], rkv[:, 1, bass.ds(t, 1), :].rearrange("p a d -> p (a d)"), Ei[:], ALU.mult).then_inc(vec_steps, v.step("KT"))
                e.tensor_tensor(RT[:], rkv[:, 0, bass.ds(t, 1), :].rearrange("p a d -> p (a d)"), E[:], ALU.mult).then_inc(vec_steps, v.step("RT"))
                e.tensor_copy(Vst[:], rkv[:, 2, bass.ds(t, 1), :].rearrange("p a d -> p (a d)")).then_inc(vec_steps, v.step("Vst"))
                masked("G0", G, 0, bank[2], lower)
                masked("G1", G, 1, bank[3], lower)
                e.wait_ge(pool_steps, after(hf, ph, "pool", "tab", t - 1))
                scores(0)
                scores(1)
                Y(1)
                TT(1)
                scores(2)
                T(1)
                scores(3)
                e.wait_ge(vec_steps, v.after("mx3"))
                e.tensor_tensor(den8[:, 5, :], den8[:, 0, :], sink, ALU.max).then_inc(vec_steps, v.step("m"))
                e.wait_ge(vec_steps, v.after("m"))
                e.tensor_scalar(den8[:, 1, :], den8[:, 5, :], -1.0, None, ALU.mult).then_inc(vec_steps, v.step("nm"))
                e.tensor_tensor(den8[:, 2, :], sink, den8[:, 5, :], ALU.subtract).then_inc(vec_steps, v.step("sd"))
                Y(2)
                TT(2)
                masked("MKA0", MKA, 0, bank[1], upper)
                T(2)
                masked("MKA1", MKA, 1, bank[5], upper)
                Y(3)
                masked("MRB0", MRB, 0, bank[0], uppeq)
                TT(3)
                masked("MRB1", MRB, 1, bank[1], uppeq)
                T(3)
                Y(4)
                masked("MRK0", MRK, 0, bank[5], uppeq)
                TT(4)
                T(4)
                masked("MRK1", MRK, 1, bank[0], uppeq)
                Y(5)
                TT(5)
                T(5)
                e.wait_ge(act_steps, after(hf, ph, "act", "esink", t))
                e.tensor_tensor(den8[:, 4, :], den8[:, 3, :], den8[:, 4, :], ALU.add).then_inc(vec_steps, v.step("den"))
                e.wait_ge(vec_steps, v.after("den"))
                e.reciprocal(den8[:, 0, :], den8[:, 4, :]).then_inc(vec_steps, v.step("rden"))
                Y(6)
                e.wait_ge(pe_steps, after(hf, ph, "pe", "PV", t))
                e.wait_ge(vec_steps, v.after("rden"))
                e.tensor_tensor(rows_a[:, bass.ds(t, 1), :].rearrange("p a (h n) -> p (a h) n", h=HEADS), eight(bank[6][:]), each(den8[:, 0, :]), ALU.mult).then_inc(vec_steps, v.step("PV"))
                TT(6)
                e.wait_ge(pe_steps, after(hf, ph, "pe", "bonus", t))
                e.tensor_copy(small[:, 32:40], bank[7][:, 0:8]).then_inc(vec_steps, v.step("bon"))
                for c in range(2):
                    nm = "ab"[c]
                    e.wait_ge(pe_steps, after(hf, ph, "pe", "HB" + nm, t))
                    e.wait_ge(pool_steps, after(hf, ph, "pool", "W" + nm, t))
                    b = bank[5] if c == 0 else bank[2]
                    e.tensor_tensor(H[1 - c][:], HW[:], b[:, 0:NP * HD].rearrange("p (a n) -> p a n", a=NP), ALU.add).then_inc(vec_steps, v.step("H" + nm))

            def last_of(hf):
                return 4 * hf

            for hf in range(HALVES):
                norm(hf, "norm", lambda i: xt[i % 2][:], 4 * hf + 1)
                begin(e, hf, "rkv", "vec")
                with e.Fori(0, 3) as g:
                    v = Pass(hf, "rkv", g)
                    for n in range(4):
                        shift_tile(v, n, after(hf, "rkv", "act", f"e{n}", g),
                                   par[:, bass.ds(g * 4 + n, 1)], shcar[:, bass.ds(g * 4 + n, 1)],
                                   rkv[:, bass.ds(g, 1), :, P * n:P * n + P].rearrange("p a t n -> p (a t) n"))
                v = Pass(hf, "lora")
                begin(e, hf, "lora", "vec")
                e.wait_ge(mix_in, 96 * (hf + 1))
                for n, dst in enumerate((wa, gd)):
                    shift_tile(v, n, after(hf, "lora", "act", f"e{n}"), par[:, 12 + n:13 + n],
                               shcar[:, 12 + n:13 + n], dst[:], four=False)
                for p in range(NP):
                    e.tensor_scalar(kk[:, :, P * p:P * p + P], rkv[:, 1, :, P * p:P * p + P], par[:, KK_ + p:KK_ + p + 1], None, ALU.mult).then_inc(vec_steps, v.step(f"kr{p}"))
                e.wait_ge(act_steps, after(hf, "lora", "act", "w_3"))
                for t in range(NT):
                    e.tensor_tensor_scan(L[:, t, :], chunks[:], sig[:, t, :], 0.0, ALU.mult, ALU.add).then_inc(vec_steps, v.step(f"scan{t}"))
                e.wait_ge(act_steps, after(hf, "lora", "act", "root"))
                e.tensor_scalar(rn[:, 1, :], rn[:, 0, :], 1e-12, None, ALU.max).then_inc(vec_steps, v.step("nmax"))
                e.wait_ge(vec_steps, v.after("nmax"))
                e.reciprocal(rn[:, 2, :], rn[:, 1, :]).then_inc(vec_steps, v.step("rn"))
                v = Pass(hf, "q")
                for p in range(NP):
                    part = (slice(None), slice(None), slice(P * p, P * p + P))
                    k_p = rkv[:, 1, :, P * p:P * p + P]
                    b4 = bank[4 + p][:].rearrange("p (t n) -> p t n", t=NT)
                    tmp = shd[:].rearrange("p (t n) -> p t n", t=NT)
                    e.wait_ge(pe_steps, after(hf, "q", "pe", f"bc{p}"))
                    e.tensor_tensor(kk[part], kk[part], b4, ALU.mult).then_inc(vec_steps, v.step(f"kn{p}"))
                    if p:
                        e.wait_ge(vec_steps, v.after(f"k{p - 1}"))
                    e.tensor_scalar(tmp, av[part], 1.0, par[:, KA + p:KA + p + 1], ALU.subtract, ALU.mult).then_inc(vec_steps, v.step(f"t{p}"))
                    e.wait_ge(vec_steps, v.after(f"t{p}"))
                    e.scalar_tensor_tensor(k_p, tmp, 1.0, k_p, ALU.add, ALU.mult).then_inc(vec_steps, v.step(f"k{p}"))
                    e.tensor_tensor(av[part], av[part], kk[part], ALU.mult).then_inc(vec_steps, v.step(f"b{p}"))
                begin(e, hf, "mix", "vec")
                with e.Fori(0, NT) as t:
                    mix_tile(hf, t)
                begin(e, hf, "gate", "vec")
                e.wait_ge(ln_in, 32 * (hf + 1))
                v = Pass(hf, "gate")
                g8 = gyn[:].rearrange("p (h n) -> p h n", h=HEADS)
                each = lambda x: x.unsqueeze(2).to_broadcast([P, HEADS, HD])
                for i in range(NT):
                    y8 = rows_y[:, i, :].rearrange("p (h n) -> p h n", h=HEADS)
                    e.tensor_reduce(den8[:, 0, :], y8, AX, ALU.add).then_inc(vec_steps, v.step(f"sum{i}"))
                    e.wait_ge(vec_steps, v.after(f"sum{i}"))
                    e.tensor_scalar(den8[:, 0, :], den8[:, 0, :], 1.0 / HD, None, ALU.mult).then_inc(vec_steps, v.step(f"mean{i}"))
                    e.wait_ge(vec_steps, v.after(f"mean{i}"))
                    e.tensor_tensor(g8, y8, each(den8[:, 0, :]), ALU.subtract).then_inc(vec_steps, v.step(f"yc{i}"))
                    e.wait_ge(act_steps, after(hf, "gate", "act", f"sq{i}"))
                    e.tensor_reduce(den8[:, 1, :], gsq[:].rearrange("p (h n) -> p h n", h=HEADS), AX, ALU.add).then_inc(vec_steps, v.step(f"ssq{i}"))
                    e.wait_ge(vec_steps, v.after(f"ssq{i}"))
                    e.tensor_scalar(den8[:, 1, :], den8[:, 1, :], 1.0 / HD, GN_EPS, ALU.mult, ALU.add).then_inc(vec_steps, v.step(f"var{i}"))
                    e.wait_ge(act_steps, after(hf, "gate", "act", f"root{i}"))
                    e.reciprocal(den8[:, 3, :], den8[:, 2, :]).then_inc(vec_steps, v.step(f"rstd{i}"))
                    e.wait_ge(vec_steps, v.after(f"rstd{i}"))
                    e.tensor_tensor(g8, g8, each(den8[:, 3, :]), ALU.mult).then_inc(vec_steps, v.step(f"yn{i}"))
                    e.wait_ge(vec_steps, v.after(f"yn{i}"))
                    e.tensor_tensor(gyn[:], gyn[:], lnw[:], ALU.mult).then_inc(vec_steps, v.step(f"lw{i}"))
                    e.wait_ge(vec_steps, v.after(f"lw{i}"))
                    e.tensor_tensor(gyn[:], gyn[:], lnb[:], ALU.add).then_inc(vec_steps, v.step(f"lb{i}"))
                    e.wait_ge(vec_steps, v.after(f"lb{i}"))
                    e.tensor_tensor(gyn[:], gyn[:], bv[:, i, :], ALU.add).then_inc(vec_steps, v.step(f"bv{i}"))
                    e.wait_ge(vec_steps, v.after(f"bv{i}"))
                    e.wait_ge(pe_steps, after(hf, "gate", "pe", f"g{i}"))
                    e.tensor_tensor(rows_y[:, i, :], gyn[:], bank[4 + i][:], ALU.mult).then_inc(vec_steps, v.step(f"g{i}"))
                    for b in range(2):
                        e.wait_ge(act_steps, after(hf, "gate", "act", f"h{b}_{i}"))
                        cols = (slice(None), slice(4 * b, 4 * b + 4), slice(P * i, P * i + P))
                        e.tensor_tensor(xlo[cols], bank[b][:].rearrange("p (k n) -> p k n", k=4), xhi[cols].bitcast(F32), ALU.subtract).then_inc(vec_steps, v.step(f"l{b}_{i}"))
                begin(e, hf, "post", "vec")
                e.wait_ge(gain_in, 16 * (4 * hf + 2))
                e.wait_ge(h_in, 16 * NT * (hf + 1))
                v = Pass(hf, "post")
                for i in range(NT):
                    e.wait_ge(act_steps, after(hf, "post", "act", f"sqb{i}"))
                    e.tensor_tensor(small[:, 18:19], small[:, 16:17], small[:, 17:18], ALU.add).then_inc(vec_steps, v.step(f"ss{i}"))
                    e.wait_ge(vec_steps, v.after(f"ss{i}"))
                    e.tensor_scalar(small[:, 19:20], small[:, 18:19], 1.0 / D, EPS, ALU.mult, ALU.add).then_inc(vec_steps, v.step(f"ms{i}"))
                    e.wait_ge(act_steps, after(hf, "post", "act", f"root{i}"))
                    e.reciprocal(small[:, 21:22], small[:, 20:21]).then_inc(vec_steps, v.step(f"rstd{i}"))
                    e.wait_ge(vec_steps, v.after(f"rstd{i}"))
                    e.scalar_tensor_tensor(xs[0][:, 0:512], bank[i][:], small[:, 21:22], gain[:, 0:512], ALU.mult, ALU.mult).then_inc(vec_steps, v.step(f"ma{i}"))
                    e.scalar_tensor_tensor(xs[0][:, 512:1024], bank[4 + i][:], small[:, 21:22], gain[:, 512:1024], ALU.mult, ALU.mult).then_inc(vec_steps, v.step(f"mb{i}"))
                    e.wait_ge(vec_steps, v.after(f"mb{i}"))
                    e.tensor_tensor(hres[:, i, :], hres[:, i, :], xs[0][:], ALU.add).then_inc(vec_steps, v.step(f"h{i}"))
                norm(hf, "fnorm", lambda i: hres[:, i, :], 4 * hf + 3)
                begin(e, hf, "up", "vec")
                with e.Fori(0, PJ // 2) as g:
                    v = Pass(hf, "up", g)
                    for n in range(2):
                        def col(first, m):
                            return par[:, bass.ds(g * 2 + (first + PJ * m + n), 1)]

                        gv = list(enumerate("gv"))
                        for m, k in gv:
                            e.tensor_copy(cr[n][m][:, 0:2], cvcar[:, bass.ds(g * 2 + (PJ * m + n), 1), :].rearrange("p a n -> p (a n)")).then_inc(vec_steps, v.step(f"i{k}{n}"))
                        for m, k in gv:
                            e.wait_ge(act_steps, after(hf, "up", "act", f"e{k}{n}", g))
                            if m == 0:
                                e.wait_ge(act_steps, after(hf, "up", "act", f"hi{n}", g - 1))
                            e.tensor_scalar(cc[n][m][:], cr[n][m][:, 2:2 + HALF], col(CW + 4 * PJ, m), col(CB, m), ALU.mult, ALU.add).then_inc(vec_steps, v.step(f"c{k}{n}"))
                        for tap in (1, 0):
                            for m, k in gv:
                                e.wait_ge(vec_steps, v.after(f"{'c' if tap else '1'}{k}{n}"))
                                e.scalar_tensor_tensor(cc[n][m][:], cr[n][m][:, tap:tap + HALF], col(CW + 2 * PJ * tap, m), cc[n][m][:], ALU.mult, ALU.add).then_inc(vec_steps, v.step(f"{tap}{k}{n}"))
                        for m, k in gv:
                            e.tensor_copy(cvcar[:, bass.ds(g * 2 + (PJ * m + n), 1), :].rearrange("p a n -> p (a n)"), cr[n][m][:, HALF:HALF + 2]).then_inc(vec_steps, v.step(f"k{k}{n}"))
                        e.wait_ge(act_steps, after(hf, "up", "act", f"ge{n}", g))
                        e.wait_ge(vec_steps, v.after(f"0v{n}"))
                        e.tensor_tensor(cc[n][0][:], gl[:], cc[n][1][:], ALU.mult).then_inc(vec_steps, v.step(f"m{n}"))
                        e.wait_ge(act_steps, after(hf, "up", "act", f"hi{n}", g))
                        sl = (slice(None), bass.ds(g * 2 + n, 1), slice(None))
                        e.tensor_tensor(glo[sl].rearrange("p a d -> p (a d)"), cc[n][0][:], ghi[sl].bitcast(F32).rearrange("p a d -> p (a d)"), ALU.subtract).then_inc(vec_steps, v.step(f"lo{n}"))
                begin(e, hf, "down", "vec")
                with e.Fori(0, 2) as n:
                    v = Pass(hf, "down", n)
                    e.wait_ge(pe_steps, after(hf, "down", "pe", "u10", n))
                    for i in (2, 3):
                        e.tensor_copy(fo[:, i, bass.ds(n * 512, 512)], bank[4 + i][:]).then_inc(vec_steps, v.step(f"f{i}"))
                begin(e, hf, "last", "vec")
                e.wait_ge(gain_in, 16 * (4 * hf + 4))
                v = Pass(hf, "last")
                for i in range(NT):
                    e.wait_ge(act_steps, after(hf, "last", "act", f"sq{i}"))
                    mean_square(v, i)
                    e.wait_ge(act_steps, after(hf, "last", "act", f"root{i}"))
                    e.reciprocal(small[:, 12 + i:13 + i], small[:, 8 + i:9 + i]).then_inc(vec_steps, v.step(f"rstd{i}"))
                    e.wait_ge(vec_steps, v.after(f"rstd{i}"))
                    e.scalar_tensor_tensor(fo[:, i, :], fo[:, i, :], small[:, 12 + i:13 + i], gain[:], ALU.mult, ALU.mult).then_inc(vec_steps, v.step(f"m{i}"))
                    e.wait_ge(vec_steps, v.after(f"m{i}"))
                    e.tensor_tensor(hres[:, i, :], hres[:, i, :], fo[:, i, :], ALU.add).then_inc(vec_steps, v.step(f"y{i}"))

        @block.gpsimd
        def _(e):
            for cell in (kT[:, 0:P], HW[:], rn[:, 0, :]):
                e.memset(cell, 0.0).then_inc(sems["pool"], 1)
            e.wait_ge(const_in, 32)

            def tt(hf, ph, name, dst, x, y, op):
                e.tensor_tensor(dst, x, y, op).then_inc(pool_steps, halves[hf][ph]["pool"].step(name))

            def mix_tile(hf, t):
                ph = "mix"
                c8 = lambda x: x[:].rearrange("p (c n) -> p c n", c=8)
                tile = lambda x, n: x[:, n, bass.ds(t, 1), :].rearrange("p a d -> p (a d)")
                wc = c8(E)[:, :, CH - 1:CH].to_broadcast([P, 8, CH])
                e.wait_ge(vec_steps, after(hf, ph, "vec", "KT", t))
                tt(hf, ph, "KP", c8(KP), c8(KTl), wc, ALU.mult)
                tt(hf, ph, "BP", c8(BP), c8(BT), wc, ALU.mult)
                tt(hf, ph, "RK", RKp[:], tile(rkv, 0), tile(rkv, 1), ALU.mult)
                e.wait_ge(vec_steps, after(hf, ph, "vec", "sb3", t))
                e.nop(nofuse=True)
                e.tensor_copy(table[:, :, 0:CH], edge[:]).then_inc(pool_steps, halves[hf][ph]["pool"].step("tab"))

                def decayed(c):
                    w = E[:].rearrange("p (a c n) -> p a c n", a=NP, c=2)[:, :, c, CH - 1:CH].to_broadcast([P, NP, HD])
                    tt(hf, ph, "W" + "ab"[c], HW[:], H[c][:], w, ALU.mult)

                decayed(0)
                e.wait_ge(act_steps, after(hf, ph, "act", "trV", t))
                e.wait_ge(vec_steps, after(hf, ph, "vec", "bon", t))
                tt(hf, ph, "BV", bv[:, bass.ds(t, 1), :].rearrange("p a (h n) -> p (a h) n", h=HEADS), c8(Vt),
                   small[:, 32:40].unsqueeze(2).to_broadcast([P, HEADS, HD]), ALU.mult)
                e.wait_ge(vec_steps, after(hf, ph, "vec", "Ha", t))
                decayed(1)

            for hf in range(HALVES):
                begin(e, hf, "rkv", "pool")
                with e.Fori(0, 3) as g:
                    for u in range(4):
                        split_lo(e, hf, "rkv", u, g, f"w{u}")
                begin(e, hf, "lora", "pool")
                for u in range(4):
                    split_lo(e, hf, "lora", u, 0, f"w{u}")
                for u in range(4):
                    split_lo(e, hf, "q", u, 0, f"w{u}")
                e.wait_ge(pe_steps, after(hf, "q", "pe", "bc3"))
                e.wait_ge(vec_steps, after(hf, "q", "vec", "k3"))
                st = halves[hf]["q"]["pool"]
                e.memset(Ybd[:], 0.0).then_inc(pool_steps, st.step("zy"))
                e.memset(Tbd[:], 0.0).then_inc(pool_steps, st.step("zt"))
                e.memset(pr[:, :, 0:CH], 0.0).then_inc(pool_steps, st.step("zp"))
                begin(e, hf, "mix", "pool")
                e.wait_ge(mix_in, 96 * (hf + 1))
                with e.Fori(0, NT) as t:
                    mix_tile(hf, t)
                begin(e, hf, "gate", "pool")
                st = halves[hf]["gate"]["pool"]
                e.tensor_copy(kT[:, 0:P], kT[:, HALF:HALF + P]).then_inc(pool_steps, st.step("kT"))
                e.tensor_copy(vA[:, 0, :], vA[:, NT, :]).then_inc(pool_steps, st.step("vA"))
                begin(e, hf, "out", "pool")
                for u in range(8):
                    split_lo(e, hf, "out", u, 0, f"u{u}")
                begin(e, hf, "up", "pool")
                with e.Fori(0, PJ // 2) as g:
                    for n in range(2):
                        for m, k in enumerate("gv"):
                            split_lo(e, hf, "up", 2 * n + m, g, f"w{k}{n}")
                begin(e, hf, "down", "pool")
                with e.Fori(0, 2) as n:
                    for u in range(11):
                        split_lo(e, hf, "down", u, n, f"u{u}")


def constants():
    f = np.float32
    i = np.arange(P)
    same = (i[:, None] // CH) == (i[None, :] // CH)
    eye = np.eye(P, dtype=f)
    lower = (same & (i[:, None] > i[None, :])).astype(f)
    stack = np.concatenate([np.eye(CH, dtype=f)] * 2)
    r, c = np.arange(CH)[:, None], np.arange(CH)[None, :]
    levels = []
    for b in LEVELS:
        m = (r // (2 * b) == c // (2 * b)) & (r // b % 2 == 0) & (c // b % 2 == 1)
        levels.append(np.concatenate([m.astype(f)] * 2))
    ones8 = np.zeros((P, NP, 8), f)
    spread = np.zeros((8, NP, P), f)
    for p in range(NP):
        for e in range(2):
            ones8[HD * e:HD * e + HD, p, 2 * p + e] = 1
            spread[2 * p + e, p, HD * e:HD * e + HD] = 1
    key = np.arange(WIN)
    dist = np.abs(i[:, None] + CH - key[None, :]).astype(f)
    seen = (key[None, :] // CH == i[:, None] // CH) | (key[None, :] // CH == i[:, None] // CH + 1)
    slopes = np.exp2(-8.0 * np.arange(1, HEADS + 1, dtype=f) / HEADS).astype(f)
    alibi = np.stack([np.where(seen, -slopes[h] * dist, -HID) for h in range(HEADS)], 1).astype(f)
    first = alibi.copy()
    first[:, :, 0:CH] = -HID
    chunks = np.ones((P, 512), f)
    chunks[:, ::CH] = 0
    return eye, lower, lower.T, lower.T + eye, stack, levels, ones8, spread, alibi, first, chunks


def kernel(**inputs):
    import concourse.bacc as bacc
    from concourse.bass_utils import run_bass_kernel_spmd

    x = {n: np.asarray(v) for n, v in inputs.items()}
    f = np.float32
    eye, lower, upper, uppeq, stack, levels, ones8, spread, alibi, first, chunks = constants()

    def tall(v):
        return np.ascontiguousarray(v.reshape(-1, P).T)

    def wide(v):
        return np.ascontiguousarray(np.broadcast_to(v.reshape(1, -1), (P, v.size)))

    bonus = np.zeros((P, 8), f)
    rk = x["rwkv_r_k"][0]
    for h in range(HEADS):
        bonus[HD * (h % 2):HD * (h % 2) + HD, h] = rk[h]
    par = np.concatenate([tall(x["rwkv_mu"][0]), tall(x["rwkv_w0"][0]), tall(x["rwkv_a0"][0]), tall(x["rwkv_k_k"][0]),
                          tall(x["rwkv_k_a"][0])] + [tall(x["ffn_conv_w"][0, n]) for n in range(3)]
                         + [tall(x["ffn_conv_b"][0]), bonus], 1)
    cst = np.concatenate([eye, lower, upper, uppeq, stack, *levels, ones8.reshape(P, -1),
                          wide(x["attn_sinks"])], 1)
    feed = {
        "x": x["x"][0], "w_in": x["w_in"][0], "w_out": x["w_out"][0], "ffn_w_up": x["ffn_w_up"][0],
        "ffn_w_down": x["ffn_w_down"][0], "par": par, "cst": cst, "spread": spread, "alibi": alibi, "first": first,
        "edge": np.ascontiguousarray(alibi[:, :, 0:CH]),
        "chunks": chunks, "lora": np.concatenate([x["rwkv_w_w2"][0], x["rwkv_w_a2"][0]], 0),
        "wg2": x["rwkv_w_g2"][0], "ln_w": wide(x["rwkv_ln_w"]), "ln_b": wide(x["rwkv_ln_b"]),
        "g_mix_pre": wide(x["norm_mix_pre"]), "g_mix_post": wide(x["norm_mix_post"]),
        "g_ffn_pre": wide(x["norm_ffn_pre"]), "g_ffn_post": wide(x["norm_ffn_post"]),
    }
    nc = bacc.Bacc("TRN2", target_bir_lowering=False, num_devices=1)
    arrays, aps = {}, {}
    for name, v in feed.items():
        v = np.ascontiguousarray(v)
        arrays[f"in_{name}"] = v
        aps[name] = nc.dram_tensor(f"in_{name}", v.shape, mybir.dt.from_np(v.dtype), kind="ExternalInput").ap()
    out = nc.dram_tensor("out", (SEQ, D), F32, kind="ExternalOutput").ap()
    build(nc, aps, out)
    r = run_bass_kernel_spmd(nc, [arrays], core_ids=[0])
    return r.results[0]["out"].reshape(1, SEQ, D)
```

```python
from contextlib import ExitStack

import numpy as np

import concourse.bass as bass
from concourse import mybir

P = 128
D, SEQ, HALF, FF = 1024, 1024, 512, 2816
HALVES, NT = SEQ // HALF, HALF // P
KT = D // P
CH, HD, HEADS, NP = 64, 64, 8, 4
PJ = FF // P
WIN = 3 * CH
LEVELS = (1, 2, 4, 8, 16, 32)
RAWS, SPLITS = 4, 2
DECAY = float(np.exp(-0.5))
EPS, GN_EPS = 1e-6, HD * 1e-5
ATT = 768
HID = 1e30

F32, F32R = mybir.dt.float32, mybir.dt.float32r
ALU, ACT, AX = mybir.AluOpType, mybir.ActivationFunctionType, mybir.AxisListType.X

MU, W0, A0, KK_, KA, CW, CB, RK = 0, 14, 18, 22, 26, 30, 30 + 6 * PJ, 30 + 8 * PJ
NPAR = RK + 8


class Steps:

    def __init__(self, sem, names, base, times):
        assert len(set(names)) == len(names)
        self.sem, self.names, self.base, self.times, self.at = sem, names, base, times, 0

    def after(self, name, it=0):
        return self.base + self.names.index(name) + 1 + it * len(self.names)

    def end(self):
        return self.base + len(self.names) * self.times

    def step(self, name):
        assert self.names[self.at % len(self.names)] == name, (self.names[self.at % len(self.names)], name)
        self.at += 1
        return 1


def norm_steps():
    pe = [f"tr{i}_{b}" for i in range(NT) for b in range(2)]
    act, vec = [], []
    for i in range(NT):
        act += [f"sq{i}", f"root{i}", f"hi{i}_0", f"hi{i}_1"]
        vec += [f"ms{i}", f"rstd{i}", f"xs{i}", f"lo{i}_0", f"lo{i}_1"]
    return pe, act, vec


def loop_steps():
    pe = ["G0", "G1", "trA", "trV", "sc0", "sc1", "Y1", "trK", "TT1", "sc2", "T1", "sc3",
          "Y2", "trB", "TT2", "MKA0", "T2", "MKA1", "Y3", "MRB0", "TT3", "MRB1", "T3", "PT0",
          "Y4", "MRK0", "TT4", "PT1", "T4", "MRK1", "Y5", "PT2", "TT5", "X1", "T5", "PT3",
          "Y6", "PV", "TT6", "bonus", "Z", "TAT", "UAa", "HVa", "RHa", "HBa", "UAb", "HVb", "RHb",
          "HBb", "YU"]
    act = ["E", "Ei", "Ep", "qs", "kw", "trA", "trV", "Yb1a", "Yb1b", "trK", "Tb1a", "Tb1b",
           "Yb2a", "Yb2b", "trB", "Tb2a", "Tb2b", "ex0", "ex1", "ex2", "ex3",
           "Yb3a", "Yb3b", "ex4", "ex5", "ex6", "ex7", "Tb3a", "Tb3b", "esink",
           "Yb4a", "Yb4b", "PT0", "Tb4a", "Tb4b", "PT1", "Yb5a", "Yb5b", "PT2", "Tb5a", "Tb5b",
           "X1", "PT3", "Tb6a", "Tb6b", "TAT", "Ua0", "Ua1", "Ub0", "Ub1", "Y0", "Y"]
    vec = ["Lp", "AN", "BT", "KT", "RT", "Vst", "G0", "G1", "sb0", "mx0", "sb1", "mx1",
           "Y1", "TT1", "sb2", "mx2", "T1", "sb3", "mx3", "m", "nm", "sd", "Y2", "TT2", "MKA0",
           "T2", "MKA1", "Y3", "MRB0", "TT3", "MRB1", "T3", "Y4", "MRK0", "TT4", "T4", "MRK1",
           "Y5", "TT5", "T5", "den", "rden", "Y6", "PV", "TT6", "bon", "Ha", "Hb"]
    pool = ["KP", "BP", "RK", "tab", "Wa", "BV", "Wb"]
    return pe, act, vec, pool


def plan(sems):
    npe, nact, nvec = norm_steps()
    lpe, lact, lvec, lpool = loop_steps()
    units = [f"u{u}" for u in range(20)]
    shift = [f"{k}{n}" for n in range(4) for k in "bdsc"]
    both = [f"{k}{n}" for n in range(4) for k in "se"]
    first = ["s0", "s1"]
    phases = {
        "norm": (npe, nact[:12] + first + nact[12:], nvec, [], 1),
        "rkv": (units[:4], both, shift, units[:4], 3),
        "lora": (units[:4], both, shift[:8] + [f"kr{p}" for p in range(NP)], units[:4], 1),
        "q": (units[:4] + ["ss", "vt"] + [f"{k}{p}" for p in range(NP) for k in "wa"] + [f"bc{p}" for p in range(NP)],
              ["s0", "e0", "th", "sg", "s1", "e1", "sq0", "sq1", "e2", "sq2", "sq3", "e3", "root"]
              + [f"{k}{p}" for p in range(NP) for k in ("w_", "a_")] + ["vt"],
              ["nmax", "rn"] + [f"{k}{p}" for p in range(NP) for k in ("kn", "t", "k", "b")]
              + ["scan0", "scan1", "scan2", "scan3"],
              units[:4] + ["zy", "zt", "zp"], 1),
        "mix": (lpe, lact, lvec, lpool, NT),
        "gate": ([f"g{i}" for i in range(NT)] + [f"tr{b}_{i}" for i in range(NT) for b in range(2)],
                 [f"{k}{i}" for i in range(2) for k in ("sq", "root", "h0_", "h1_")] + first
                 + [f"{k}{i}" for i in range(2, NT) for k in ("sq", "root", "h0_", "h1_")],
                 [f"{k}{i}" for i in range(NT) for k in
                  ("sum", "mean", "yc", "ssq", "var", "rstd", "yn", "lw", "lb", "bv", "g", "l0_", "l1_")],
                 ["kT", "vA"], 1),
        "out": (units[:8], [f"s{u}" for u in range(8)], [], units[:8], 1),
        "post": ([], [f"{k}{i}" for i in range(NT) for k in ("sqa", "sqb", "root")],
                 [f"{k}{i}" for i in range(NT) for k in ("ss", "ms", "rstd", "ma", "mb", "h")], [], 1),
        "fnorm": (npe, nact, nvec, [], 1),
        "up": (units[:4], ["s0", "eg0", "s1", "ev0", "ge0", "s2", "eg1", "s3", "ev1", "ge1"],
               [f"{k}{n}" for n in range(2) for k in
                ("ig", "iv", "cg", "1g", "0g", "kg", "cv", "1v", "0v", "kv", "m", "hi", "lo")],
               units[:4], PJ // 2),
        "down": (units[:11], [f"s0_{u}" for u in range(11)] + ["f0_0", "f1_0"]
                 + [f"s1_{u}" for u in range(9)] + ["f0_1", "f1_1"],
                 ["f2", "f3"], units[:11], 2),
        "last": ([], [f"{k}{i}" for i in range(NT) for k in ("sq", "root")],
                 [f"{k}{i}" for i in range(NT) for k in ("ms", "rstd", "m", "y")], [], 1),
    }
    base = dict(pe=0, act=0, vec=4, pool=3)
    halves = []
    for _ in range(HALVES):
        half = {}
        for name, row in phases.items():
            half[name] = {}
            for eng, names in zip(("pe", "act", "vec", "pool"), row):
                once = name == "down" and eng == "act"
                s = Steps(sems[eng], names, base[eng], 1 if once else row[4])
                base[eng] = s.end()
                half[name][eng] = s
        halves.append(half)
    return halves, list(phases)


def build(nc, a, out):
    with ExitStack() as ctx:
        def sem(name):
            return ctx.enter_context(nc.semaphore(name))

        lo_end = (nc.sbuf_base + 31) // 32 * 32
        cursor = [lo_end]

        def sb(name, shape, dt=F32, at=None):
            size = int(np.prod(shape[1:])) * 4
            where = cursor[0] if at is None else at
            t = nc.alloc_sbuf_tensor_at("s_" + name, list(shape), dt, offset=where)
            if at is None:
                cursor[0] = where + (size + 31) // 32 * 32
            return t

        bank = [ctx.enter_context(nc.psum_tensor(f"bank{b}", [P, 512], F32)) for b in range(8)]

        par = sb("par", [P, NPAR])
        cst = sb("cst", [P, 128 * 4 + 64 * 7 + 32 + 8])
        ident, lower, upper, uppeq = (cst[:, 128 * n:128 * n + 128] for n in range(4))
        eye = cst[:, 512:576]
        level = [cst[:, 576 + 64 * n:640 + 64 * n] for n in range(6)]
        ones8 = cst[:, 960:992].rearrange("p (a b) -> p a b", a=NP)
        sink = cst[:, 992:1000]
        H = [sb(f"H{n}", [P, NP, HD]) for n in range(2)]
        HW = sb("HW", [P, NP, HD])
        shcar = sb("shcar", [P, 14])
        cvcar = sb("cvcar", [P, 2 * PJ, 2])
        kT = sb("kT", [P, P + HALF])
        vA = sb("vA", [P, NT + 1, P])
        gain = sb("gain", [P, D])
        small = sb("small", [P, 64])
        den8 = sb("den8", [P, 6, HEADS])
        ring_at = cursor[0]
        raw = [sb(f"raw{n}", [P, D]) for n in range(RAWS)]
        whi = [sb(f"whi{n}", [P, D], F32R) for n in range(SPLITS)]
        wlo = [sb(f"wlo{n}", [P, D], F32R) for n in range(SPLITS)]
        xhi_at = cursor[0]
        xhi = sb("xhi", [P, KT, HALF], F32R)
        xlo = sb("xlo", [P, KT, HALF], F32R)
        free = cursor[0]

        rkv = sb("rkv", [P, 3, NT, 512])
        sig = sb("sig", [P, NT, 512])
        L = sb("L", [P, NT, 512])
        av = sb("av", [P, NT, 512])
        kk = sb("kk", [P, NT, 512])
        qT = sb("qT", [P, NT, 512])
        rows_y, rows_a, bv = rkv[:, 0], rkv[:, 2], qT
        sg = sb("sg", [P, HALF])
        spread = sb("spread", [8, NP, P])
        edge = sb("edge", [P, HEADS, CH])
        table = sb("table", [P, HEADS, WIN])
        chunks = sb("chunks", [P, 512])
        lora = sb("lora", [P, 512])
        wg2 = sb("wg2", [P, 512])
        mid = cursor[0]
        wa = sb("wa", [P, HALF])
        gd = sb("gd", [P, HALF])
        vT = sb("vT", [P, HALF])
        th = sb("th", [HD, HALF])
        shr = [sb(f"shr{n}", [P, 1 + HALF]) for n in range(2)]
        shd = sb("shd", [P, HALF])
        rn = sb("rn", [8, 3, HALF])
        sq = [sb(f"sq{p}", [P, HALF]) for p in range(NP)]
        endB = cursor[0]

        cursor[0] = xhi_at
        pr = sb("pr", [P, HEADS, 2 * P])
        pT = sb("pT", [P, HEADS, 2, P])
        scb = sb("scb", [P, HEADS, WIN])
        qs = sb("qs", [P, NP, P])
        E, Ei, Ep, Lp = (sb(n, [P, 512]) for n in ("E", "Ei", "Ep", "Lp"))
        assert cursor[0] <= free
        cursor[0] = ring_at
        AN, BT, KTl, RT, Vst, KP, BP, RKp = (sb(n, [P, 512]) for n in ("AN", "BT", "KTl", "RT", "Vst", "KP", "BP", "RKp"))
        G, MKA, MRB, MRK = (sb(n, [P, HEADS, P]) for n in ("G", "MKA", "MRB", "MRK"))
        assert cursor[0] <= xhi_at
        cursor[0] = mid
        At, Kt, Bt, Vt = (sb(n, [P, 512]) for n in ("At", "Kt", "Bt", "Vt"))
        Tst, Tt, Yst = (sb(n, [P, HEADS, CH]) for n in ("Tst", "Tt", "Yst"))
        Ybd, Tbd = (sb(n, [P, HEADS, P]) for n in ("Ybd", "Tbd"))
        X1, U, TAT = (sb(n, [P, 512]) for n in ("X1", "U", "TAT"))
        kw = sb("kw", [P, WIN])
        endD = cursor[0]

        cursor[0] = free
        ghi = sb("ghi", [P, PJ, HALF], F32R)
        glo = sb("glo", [P, PJ, HALF], F32R)
        hres = sb("hres", [P, NT, D])
        fo_at = cursor[0]
        cr = [[sb(f"cr{n}{m}", [P, 2 + HALF]) for m in range(2)] for n in range(2)]
        cc = [[sb(f"cc{n}{m}", [P, HALF]) for m in range(2)] for n in range(2)]
        gl = sb("gl", [P, HALF])
        endF = cursor[0]
        xt_at = free
        cursor[0] = mid
        gyn = sb("gyn", [P, 512])
        gsq = sb("gsq", [P, 512])
        lnw, lnb = sb("lnw", [P, 512]), sb("lnb", [P, 512])
        xt = [nc.alloc_sbuf_tensor_at(f"s_xt{n}", [P, D], F32, offset=xt_at + 4096 * n) for n in range(2)]
        xs = [nc.alloc_sbuf_tensor_at(f"s_xs{n}", [P, D], F32, offset=xt_at + 8192 + 4096 * n) for n in range(2)]
        jk = nc.alloc_sbuf_tensor_at("s_jk", [P, D], F32, offset=xt_at + 16384)
        mxo = nc.alloc_sbuf_tensor_at("s_mxo", [P, NT, D], F32, offset=xt_at + 20480)
        fo = nc.alloc_sbuf_tensor_at("s_fo", [P, NT, D], F32, offset=fo_at)
        fj = nc.alloc_sbuf_tensor_at("s_fj", [P, D], F32, offset=xhi_at + 16384)
        assert max(endB, endD, endF, cursor[0]) <= nc.sbuf_usable_end

        sems = {e: sem(f"{e}_steps") for e in ("pe", "act", "vec", "pool")}
        const_in, mix_in = sem("const_in"), sem("mix_in")
        w_in_ = [sem(f"w_raw{n}") for n in range(RAWS)]
        x_in = [sem(f"x_in{n}") for n in range(2)]
        gain_in, ln_in, h_in, y_out = sem("gain_in"), sem("ln_in"), sem("h_in"), sem("y_out")
        halves, order = plan(sems)

        pe_steps, act_steps, vec_steps, pool_steps = (sems[n] for n in ("pe", "act", "vec", "pool"))

        def after(hf, phase, eng, name, it=0):
            return halves[hf][phase][eng].after(name, it)

        class Pass:

            def __init__(self, hf, ph, it=0):
                self.steps, self.it = halves[hf][ph]["vec"], it
                self.step = self.steps.step

            def after(self, name):
                return self.steps.after(name, self.it)

        def begin(e, hf, phase, me):
            steps = halves[hf][phase]
            if hf or phase != "norm":
                e.wait_ge(pe_steps, steps["pe"].base)
                e.wait_ge(act_steps, steps["act"].base)
            e.wait_ge(vec_steps, steps["vec"].base)
            e.wait_ge(pool_steps, steps["pool"].base)

        w1 = a["w_in"].rearrange("(k p) n -> p k n", p=P)
        wo = a["w_out"]
        wu = a["ffn_w_up"].rearrange("(k p) n -> p k n", p=P)
        wd = a["ffn_w_down"].rearrange("(k p) n -> p k n", p=P)
        UNITS = {"rkv": (4, 3), "lora": (4, 1), "q": (4, 1), "out": (8, 1), "up": (4, PJ // 2), "down": (11, 2)}

        def loads(ph, u):
            return 2 if ph == "q" else 1

        ub, yb = (bank[0], bank[3]), (bank[1], bank[4])

        count = [0] * RAWS
        first = {}
        for hf in range(HALVES):
            for ph, (n, times) in UNITS.items():
                per = [sum(loads(ph, u) for u in range(s, n, RAWS)) for s in range(RAWS)]
                first[hf, ph] = (list(count), per)
                count = [c + p_ * times for c, p_ in zip(count, per)]

        def landed(hf, ph, u, it=0):
            base, per = first[hf, ph]
            return 16 * (base[u % RAWS] + sum(loads(ph, v) for v in range(u % RAWS, u + 1, RAWS)) + per[u % RAWS] * it)

        def last_in(ph, u, ring):
            return max(v for v in range(UNITS[ph][0]) if v % ring == u % ring)

        def slot_before(hf, ph, u, it, ring):
            if u >= ring:
                return hf, ph, u - ring, it
            if not (isinstance(it, int) and it == 0):
                return hf, ph, last_in(ph, u, ring), it - 1
            if ph == "out" or (hf, ph) == (0, "rkv"):
                return None
            stream = list(UNITS)
            before = stream[stream.index(ph) - 1]
            return hf - (ph == "rkv"), before, last_in(before, u, ring), UNITS[before][1] - 1

        def hi_done(hf, ph, u, it):
            if ph == "down" and (u >= SPLITS or it):
                return after(hf, ph, "act", f"s{it}_{u - SPLITS}" if u >= SPLITS else f"s0_{9 + u}")
            if u >= SPLITS:
                return after(hf, ph, "act", f"s{u - SPLITS}", it)
            if not (isinstance(it, int) and it == 0):
                return after(hf, ph, "act", f"s{u + 2}", it - 1)
            where, name, last = {"rkv": ("norm", u, 0), "lora": ("rkv", u + 2, 2), "q": ("lora", u + 2, 0),
                                 "out": ("gate", u, 0), "up": ("out", u + 6, 0),
                                 "down": ("up", u + 2, PJ // 2 - 1)}[ph]
            return after(hf, where, "act", f"s{name}", last)

        def split_hi(e, hf, ph, u, it, st, name):
            e.wait_ge(w_in_[u % RAWS], landed(hf, ph, u, it))
            used = slot_before(hf, ph, u, it, SPLITS)
            if used:
                e.wait_ge(pe_steps, after(used[0], used[1], "pe", f"u{used[2]}", used[3]))
            e.activation(whi[u % SPLITS][:], raw[u % RAWS][:], ACT.Copy).then_inc(act_steps, st.step(name))

        def split_lo(e, hf, ph, u, it):
            e.wait_ge(act_steps, hi_done(hf, ph, u, it))
            e.tensor_tensor(wlo[u % SPLITS][:], raw[u % RAWS][:], whi[u % SPLITS][:].bitcast(F32),
                            ALU.subtract).then_inc(pool_steps, halves[hf][ph]["pool"].step(f"u{u}"))

        block = ctx.enter_context(nc.Block())

        @block.sync
        def _(e):
            for dst, src in ((par, "par"), (cst, "cst")):
                e.dma_start(dst[:], a[src]).then_inc(const_in, 16)

            def load(hf, ph, u, it, src, dst=None):
                used = slot_before(hf, ph, u, it, RAWS)
                if used:
                    e.wait_ge(pool_steps, after(used[0], used[1], "pool", f"u{used[2]}", used[3]))
                slot = raw[u % RAWS][:] if dst is None else dst
                e.dma_start(slot, src).then_inc(w_in_[u % RAWS], 16)

            r3 = [raw[s][:].rearrange("p (k n) -> p k n", k=KT) for s in range(RAWS)]
            r2 = [raw[s][:].rearrange("p (k n) -> p k n", k=2) for s in range(RAWS)]
            for hf in range(HALVES):
                xrow = a["x"].rearrange("(t p) d -> p t d", p=P)
                if hf:
                    for u in range(4):
                        load(hf, "rkv", u, 0, w1[:, :, ATT + P * u:ATT + P * u + P], r3[u])
                    for eng in ("vec", "act"):
                        e.wait_ge(sems[eng], halves[hf]["norm"][eng].base)
                e.dma_start(gain[:], a["g_mix_pre"]).then_inc(gain_in, 16)
                for i in range(NT):
                    if i >= 2:
                        e.wait_ge(vec_steps, after(hf, "norm", "vec", f"xs{i - 2}"))
                        e.wait_ge(act_steps, after(hf, "norm", "act", f"sq{i - 2}"))
                    elif hf:
                        e.wait_ge(y_out, 16 * NT * hf)
                    if i == 0:
                        for dst, src in ((spread, "spread"), (edge, "edge"), (table, "alibi" if hf else "first"),
                                         (chunks, "chunks"), (lora, "lora"), (wg2, "wg2")):
                            e.dma_start(dst[:], a[src]).then_inc(mix_in, 16)
                    e.dma_start(xt[i % 2][:], xrow[:, hf * NT + i, :]).then_inc(x_in[i % 2], 16)
                if not hf:
                    for u in range(4):
                        load(hf, "rkv", u, 0, w1[:, :, ATT + P * u:ATT + P * u + P], r3[u])
                with e.Fori(1, 3) as g:
                    for u in range(4):
                        load(hf, "rkv", u, g, w1[:, :, bass.ds(g * 512 + (ATT + P * u), P)], r3[u])
                for u, c in enumerate((2304, 2432, 512, 640)):
                    load(hf, "lora", u, 0, w1[:, :, c:c + P], r3[u])
                for u in range(4):
                    load(hf, "q", u, 0, w1[:, :, HD * u:HD * u + HD], r3[u][:, :, 0:HD])
                    e.dma_start(r3[u][:, :, HD:P], w1[:, :, 256 + HD * u:320 + HD * u]).then_inc(w_in_[u], 16)
                e.wait_ge(act_steps, after(hf, "mix", "act", "Y", NT - 1))
                e.wait_ge(vec_steps, after(hf, "mix", "vec", "Hb", NT - 1))
                e.wait_ge(sems["pe"], halves[hf]["mix"]["pe"].end())
                e.dma_start(lnw[:], a["ln_w"]).then_inc(ln_in, 16)
                e.dma_start(lnb[:], a["ln_b"]).then_inc(ln_in, 16)
                e.dma_start(gain[:], a["g_mix_post"]).then_inc(gain_in, 16)
                for u in range(8):
                    if u == 6:
                        e.wait_ge(pe_steps, halves[hf]["gate"]["pe"].end())
                        e.wait_ge(act_steps, halves[hf]["gate"]["act"].end())
                        e.wait_ge(vec_steps, halves[hf]["gate"]["vec"].end())
                        for i in range(NT):
                            e.dma_start(hres[:, i, :], xrow[:, hf * NT + i, :]).then_inc(h_in, 16)
                    n, k = u // 4, 2 * (u % 4)
                    c = slice(512 * n, 512 * n + 512)
                    load(hf, "out", u, 0, wo.rearrange("(k p) n -> p k n", p=P)[:, k:k + 2, c], r2[u % RAWS])
                for u in range(4):
                    c = (u % 2) * FF + P * (u // 2)
                    load(hf, "up", u, 0, wu[:, :, c:c + P], r3[u])
                e.wait_ge(vec_steps, halves[hf]["post"]["vec"].end())
                e.dma_start(gain[:], a["g_ffn_pre"]).then_inc(gain_in, 16)
                with e.Fori(1, PJ // 2) as g:
                    for u in range(4):
                        load(hf, "up", u, g, wu[:, :, bass.ds(g * 256 + ((u % 2) * FF + P * (u // 2)), P)], r3[u])
                e.wait_ge(vec_steps, halves[hf]["fnorm"]["vec"].end())
                e.dma_start(gain[:], a["g_ffn_post"]).then_inc(gain_in, 16)
                for n in range(2):
                    for u in range(11):
                        load(hf, "down", u, n, wd[:, 2 * u:2 * u + 2, 512 * n:512 * n + 512], r2[u % RAWS])
                yrow = out.rearrange("(t p) d -> p t d", p=P)
                for i in range(NT):
                    e.wait_ge(vec_steps, after(hf, "last", "vec", f"y{i}"))
                    e.dma_start(yrow[:, hf * NT + i, :], hres[:, i, :]).then_inc(y_out, 16)
            e.wait_ge(y_out, 16 * NT * HALVES)

        @block.tensor
        def _(e):
            e.wait_ge(const_in, 32)

            def turn(hf, ph, name, dst, pieces):
                for n, src in enumerate(pieces):
                    m = e.transpose(dst[:, P * n:P * n + P], src, ident)
                m.then_inc(pe_steps, halves[hf][ph]["pe"].step(name))

            def norm(hf, ph):
                begin(e, hf, ph, "pe")
                for i in range(NT):
                    e.wait_ge(vec_steps, after(hf, ph, "vec", f"xs{i}"))
                    for b in range(2):
                        if i:
                            e.wait_ge(vec_steps, after(hf, ph, "vec", f"lo{i - 1}_{b}"))
                        turn(hf, ph, f"tr{i}_{b}", bank[b],
                             [xs[i % 2][:, P * k:P * k + P] for k in range(4 * b, 4 * b + 4)])

            def columns(hf, ph, u, it, dst):
                e.wait_ge(pool_steps, after(hf, ph, "pool", f"u{u}", it))
                hi = whi[u % SPLITS][:].rearrange("p (k n) -> p k n", k=KT)
                lo = wlo[u % SPLITS][:].rearrange("p (k n) -> p k n", k=KT)
                for k in range(KT):
                    e.matmul(dst[:], hi[:, k, :], xhi[:, k, :], start=k == 0, stop=False)
                    e.matmul(dst[:], hi[:, k, :], xlo[:, k, :], start=False, stop=False)
                    m = e.matmul(dst[:], lo[:, k, :], xhi[:, k, :], start=False, stop=k == KT - 1)
                m.then_inc(pe_steps, halves[hf][ph]["pe"].step(f"u{u}"))

            def rows(hf, ph, u, it, lhs_hi, lhs_lo, k0, banks, first_k, last_k):
                e.wait_ge(pool_steps, after(hf, ph, "pool", f"u{u}", it))
                hi = whi[u % SPLITS][:].rearrange("p (k n) -> p k n", k=2)
                lo = wlo[u % SPLITS][:].rearrange("p (k n) -> p k n", k=2)
                for kk_ in range(2):
                    k = k0 + kk_
                    for i in range(NT):
                        ts = slice(P * i, P * i + P)
                        e.matmul(banks[i][:], lhs_hi[:, k, ts], hi[:, kk_, :], start=k == first_k, stop=False)
                        e.matmul(banks[i][:], lhs_hi[:, k, ts], lo[:, kk_, :], start=False, stop=False)
                        m = e.matmul(banks[i][:], lhs_lo[:, k, ts], hi[:, kk_, :], start=False, stop=k == last_k)
                m.then_inc(pe_steps, halves[hf][ph]["pe"].step(f"u{u}"))

            def lora_tiles(hf):
                ph = "q"
                st = halves[hf][ph]["pe"]
                e.wait_ge(act_steps, after(hf, ph, "act", "sq3"))
                for p in range(NP):
                    m = e.matmul(bank[6][0:8, :], ones8[:, p, :], sq[p][:], start=p == 0, stop=p == NP - 1)
                m.then_inc(pe_steps, st.step("ss"))
                turn(hf, ph, "vt", bank[7], [vT[:, P * i:P * i + P] for i in range(NT)])
                for p in range(NP):
                    if p:
                        e.wait_ge(act_steps, after(hf, ph, "act", f"w_{p - 1}"))
                    ps = slice(P * p, P * p + P)
                    e.matmul(bank[4][:], lora[0:HD, ps], th[:], start=True, stop=True).then_inc(pe_steps, st.step(f"w{p}"))
                    if p:
                        e.wait_ge(act_steps, after(hf, ph, "act", f"a_{p - 1}"))
                    e.matmul(bank[5][:], lora[HD:P, ps], wa[HD:P, :], start=True, stop=True).then_inc(pe_steps, st.step(f"a{p}"))
                e.wait_ge(vec_steps, after(hf, ph, "vec", "rn"))
                e.wait_ge(act_steps, after(hf, ph, "act", "e3"))
                for p in range(NP):
                    e.matmul(bank[p][:], spread[:, p, :], rn[:, 2, :], start=True, stop=True).then_inc(pe_steps, st.step(f"bc{p}"))

            def mix_tile(hf, t):
                ph = "mix"
                st = halves[hf][ph]["pe"]

                def rows_of(e_):
                    return slice(HD * e_, HD * e_ + HD)

                def settle():
                    e.nop(nofuse=True)

                def pair(x, h):
                    return x[rows_of(h % 2), P * (h // 2):P * (h // 2) + P]

                def products(name, odd, dst, left, right):
                    for n in range(4):
                        h = 2 * n + odd
                        m = e.matmul(dst[:, P * n:P * n + P], pair(left, h), pair(right, h), start=n == 0,
                                     stop=n == 3, skip_group_check=True)
                    m.then_inc(pe_steps, st.step(name))

                def scores(j):
                    if j >= 2:
                        e.wait_ge(vec_steps, after(hf, ph, "vec", f"sb{j - 2}", t))
                    b = bank[6 + j % 2]
                    for n in range(2):
                        m = e.matmul(b[:, WIN * n:WIN * n + WIN], qs[rows_of(j % 2), 2 * (j // 2) + n, :],
                                     kw[rows_of(j % 2), :], start=n == 0, stop=n == 1,
                                     skip_group_check=True)
                    m.then_inc(pe_steps, st.step(f"sc{j}"))

                def per_head(name, dst, left, right, start, stop=False):
                    for h in range(HEADS):
                        m = e.matmul(dst[:, CH * h:CH * h + CH], left(h), right(h), start=start and h == 0,
                                     stop=stop and h == HEADS - 1, skip_group_check=True)
                    m.then_inc(pe_steps, st.step(name))

                def Y(lv):
                    if lv == 1:
                        e.wait_ge(vec_steps, after(hf, ph, "vec", "G1", t))
                    else:
                        e.wait_ge(vec_steps, after(hf, ph, "vec", f"TT{lv - 1}", t))
                    per_head(f"Y{lv}", bank[2], lambda h: G[:, h, :],
                             (lambda h: eye) if lv == 1 else (lambda h: Tt[:, h, :]), True, True)

                def TT(lv):
                    e.wait_ge(vec_steps, after(hf, ph, "vec", f"Y{lv}", t))
                    if lv > 1:
                        e.wait_ge(act_steps, after(hf, ph, "act", f"Tb{lv - 1}b", t))
                    per_head(f"TT{lv}", bank[3], (lambda h: ident) if lv == 1 else (lambda h: Tbd[:, h, :]),
                             lambda h: Yst[:, h, :], True, True)

                def T(lv):
                    e.wait_ge(act_steps, after(hf, ph, "act", f"Yb{lv}b", t))
                    per_head(f"T{lv}", bank[4], lambda h: Ybd[:, h, :],
                             (lambda h: eye) if lv == 1 else (lambda h: Tst[:, h, :]), True, True)

                def probs(n):
                    e.wait_ge(act_steps, after(hf, ph, "act", f"ex{2 * n + 1}", t))
                    if n < 2:
                        e.wait_ge(vec_steps, after(hf, ph, "vec", f"sb{n + 2}", t))
                    else:
                        e.wait_ge(act_steps, after(hf, ph, "act", f"PT{n - 2}", t))
                    turn(hf, ph, f"PT{n}", bank[6 + n % 2],
                         [pr[:, 2 * n + i // 2, P * (i % 2):P * (i % 2) + P] for i in range(4)])

                e.wait_ge(vec_steps, after(hf, ph, "vec", "BT", t))
                e.wait_ge(vec_steps, after(hf, ph, "vec", "Hb", t - 1))
                products("G0", 0, bank[2], AN, BT)
                products("G1", 1, bank[3], AN, BT)
                turn(hf, ph, "trA", bank[0], [AN[:, P * p:P * p + P] for p in range(NP)])
                e.wait_ge(vec_steps, after(hf, ph, "vec", "Vst", t))
                e.wait_ge(act_steps, after(hf, ph, "act", "Y", t - 1))
                turn(hf, ph, "trV", bank[1], [Vst[:, P * p:P * p + P] for p in range(NP)])
                e.wait_ge(act_steps, after(hf, ph, "act", "kw", t))
                scores(0)
                scores(1)
                Y(1)
                e.wait_ge(pool_steps, after(hf, ph, "pool", "KP", t))
                turn(hf, ph, "trK", bank[5], [KP[:, P * p:P * p + P] for p in range(NP)])
                TT(1)
                scores(2)
                T(1)
                scores(3)
                Y(2)
                e.wait_ge(pool_steps, after(hf, ph, "pool", "BP", t))
                e.wait_ge(act_steps, after(hf, ph, "act", "trA", t))
                turn(hf, ph, "trB", bank[0], [BP[:, P * p:P * p + P] for p in range(NP)])
                TT(2)
                e.wait_ge(vec_steps, after(hf, ph, "vec", "RT", t))
                e.wait_ge(act_steps, after(hf, ph, "act", "trV", t))
                products("MKA0", 0, bank[1], KTl, AN)
                T(2)
                e.wait_ge(act_steps, after(hf, ph, "act", "trK", t))
                products("MKA1", 1, bank[5], KTl, AN)
                Y(3)
                e.wait_ge(act_steps, after(hf, ph, "act", "trB", t))
                products("MRB0", 0, bank[0], BT, RT)
                TT(3)
                e.wait_ge(vec_steps, after(hf, ph, "vec", "MKA0", t))
                products("MRB1", 1, bank[1], BT, RT)
                T(3)
                probs(0)
                Y(4)
                e.wait_ge(vec_steps, after(hf, ph, "vec", "MKA1", t))
                products("MRK0", 0, bank[5], KTl, RT)
                TT(4)
                probs(1)
                T(4)
                e.wait_ge(vec_steps, after(hf, ph, "vec", "MRB0", t))
                products("MRK1", 1, bank[0], KTl, RT)
                Y(5)
                probs(2)
                TT(5)
                e.wait_ge(vec_steps, after(hf, ph, "vec", "MRB1", t))
                per_head("X1", bank[1], lambda h: MKA[:, h, :], lambda h: Vt[:, CH * h:CH * h + CH], True, True)
                T(5)
                probs(3)
                Y(6)
                e.wait_ge(act_steps, after(hf, ph, "act", "PT3", t))
                for h in range(HEADS):
                    for n in range(2):
                        m = e.matmul(bank[6][:, CH * h:CH * h + CH], pT[:, h, n, :],
                                     vA[:, bass.ds(t + n, 1), HD * (h // 4):HD * (h // 4) + HD].rearrange("p a d -> p (a d)"),
                                     start=h == 0 and n == 0, stop=h == HEADS - 1 and n == 1,
                                     skip_group_check=True)
                m.then_inc(pe_steps, st.step("PV"))
                TT(6)
                e.wait_ge(pool_steps, after(hf, ph, "pool", "RK", t))
                for p in range(NP):
                    m = e.matmul(bank[7][:, 2 * p:2 * p + 2], RKp[:, P * p:P * p + P],
                                 par[:, RK + 2 * p:RK + 2 * p + 2], start=p == 0, stop=p == 3,
                                 skip_group_check=True)
                m.then_inc(pe_steps, st.step("bonus"))
                e.wait_ge(act_steps, after(hf, ph, "act", "Tb6b", t))
                e.wait_ge(vec_steps, after(hf, ph, "vec", "MRK1", t))
                for h in range(HEADS):
                    m = e.matmul(ub[h % 2][:, CH * (h // 2):CH * (h // 2) + CH], Tbd[:, h, :],
                                 X1[:, CH * h:CH * h + CH], start=h < 2, stop=False, skip_group_check=True)
                m.then_inc(pe_steps, st.step("Z"))
                for h in range(HEADS):
                    m = e.matmul(bank[5][rows_of(h % 2), P * (h // 2):P * (h // 2) + P],
                                 At[:, CH * h:CH * h + CH], Tbd[:, h, :], start=h < 2, stop=h >= 6,
                                 skip_group_check=True)
                m.then_inc(pe_steps, st.step("TAT"))

                def chunk(c):
                    cs, nm = rows_of(c), "ab"[c]
                    state = H[c]
                    hps = bank[5] if c == 0 else bank[2]
                    if c == 0:
                        e.wait_ge(act_steps, after(hf, ph, "act", "TAT", t))
                        e.wait_ge(vec_steps, after(hf, ph, "vec", "Hb", t - 1))
                    else:
                        e.wait_ge(vec_steps, after(hf, ph, "vec", "Ha", t))
                    settle()
                    for h in range(HEADS):
                        m = e.matmul(ub[h % 2][cs, CH * (h // 2):CH * (h // 2) + CH],
                                     TAT[rows_of(h % 2), P * (h // 2) + CH * c:P * (h // 2) + CH * c + CH],
                                     state[rows_of(h % 2), h // 2, :], start=False, stop=h == 7,
                                     skip_group_check=True)
                    m.then_inc(pe_steps, st.step("UA" + nm))
                    for h in range(HEADS):
                        m = e.matmul(hps[rows_of(h % 2), HD * (h // 2):HD * (h // 2) + HD],
                                     Kt[cs, HD * h:HD * h + HD], Vt[cs, HD * h:HD * h + HD],
                                     start=h < 2, stop=False, skip_group_check=True)
                    m.then_inc(pe_steps, st.step("HV" + nm))
                    if c == 0:
                        for h in range(HEADS):
                            e.matmul(yb[h % 2][:, CH * (h // 2):CH * (h // 2) + CH], MRK[:, h, :],
                                     Vt[:, CH * h:CH * h + CH], start=h < 2, stop=False, skip_group_check=True)
                    for h in range(HEADS):
                        m = e.matmul(yb[h % 2][cs, CH * (h // 2):CH * (h // 2) + CH],
                                     RT[rows_of(h % 2), P * (h // 2) + CH * c:P * (h // 2) + CH * c + CH],
                                     state[rows_of(h % 2), h // 2, :], start=False, stop=False,
                                     skip_group_check=True)
                    m.then_inc(pe_steps, st.step("RH" + nm))
                    e.wait_ge(act_steps, after(hf, ph, "act", "U" + nm + "1", t))
                    settle()
                    for h in range(HEADS):
                        m = e.matmul(hps[rows_of(h % 2), HD * (h // 2):HD * (h // 2) + HD],
                                     Bt[cs, HD * h:HD * h + HD], U[cs, HD * h:HD * h + HD],
                                     start=False, stop=h >= 6, skip_group_check=True)
                    m.then_inc(pe_steps, st.step("HB" + nm))

                chunk(0)
                chunk(1)
                for h in range(HEADS):
                    m = e.matmul(yb[h % 2][:, CH * (h // 2):CH * (h // 2) + CH], MRB[:, h, :],
                                 U[:, CH * h:CH * h + CH], start=False, stop=h >= 6, skip_group_check=True)
                m.then_inc(pe_steps, st.step("YU"))

            for hf in range(HALVES):
                norm(hf, "norm")
                begin(e, hf, "rkv", "pe")
                with e.Fori(0, 3) as g:
                    for u in range(4):
                        if u < 4:
                            e.wait_ge(act_steps, after(hf, "rkv", "act", f"e{u}", g - 1))
                        columns(hf, "rkv", u, g, bank[u])
                e.wait_ge(mix_in, 96 * (hf + 1))
                for u in range(4):
                    e.wait_ge(act_steps, after(hf, "rkv", "act", f"e{u}", 2))
                    columns(hf, "lora", u, 0, bank[u])
                for u in range(4):
                    e.wait_ge(act_steps, after(hf, "lora", "act", f"e{u}"))
                    columns(hf, "q", u, 0, bank[u])
                lora_tiles(hf)
                begin(e, hf, "mix", "pe")
                with e.Fori(0, NT) as t:
                    mix_tile(hf, t)
                begin(e, hf, "gate", "pe")

                def g_tile(i):
                    e.matmul(bank[4 + i][:], sg[:, P * i:P * i + P], wg2[:], start=True, stop=True).then_inc(pe_steps, halves[hf]["gate"]["pe"].step(f"g{i}"))

                for i in range(NT):
                    g_tile(i)
                for i in range(NT):
                    for b in range(2):
                        e.wait_ge(vec_steps, after(hf, "gate", "vec", f"g{i}"))
                        if i:
                            e.wait_ge(vec_steps, after(hf, "gate", "vec", f"l{b}_{i - 1}"))
                        turn(hf, "gate", f"tr{b}_{i}", bank[b], [(rows_y if b else rows_a)[:, i, P * k:P * k + P] for k in range(4)])
                begin(e, hf, "out", "pe")
                for u in range(8):
                    n = u // 4
                    rows(hf, "out", u, 0, xhi, xlo, 2 * (u % 4), bank[4 * n:4 * n + 4], 0, KT - 1)
                norm(hf, "fnorm")
                begin(e, hf, "up", "pe")
                with e.Fori(0, PJ // 2) as g:
                    for u in range(4):
                        e.wait_ge(act_steps, after(hf, "up", "act", f"e{'gv'[u % 2]}{u // 2}", g - 1))
                        columns(hf, "up", u, g, bank[u])
                e.wait_ge(vec_steps, after(hf, "up", "vec", "lo1", PJ // 2 - 2))
                with e.Fori(0, 2) as n:
                    e.wait_ge(act_steps, after(hf, "down", "act", "f1_0", n - 1))
                    e.wait_ge(vec_steps, after(hf, "down", "vec", "f3", n - 1))
                    for u in range(11):
                        if u == 10:
                            e.wait_ge(vec_steps, after(hf, "up", "vec", "lo1", PJ // 2 - 1))
                        rows(hf, "down", u, n, ghi, glo, 2 * u, bank[4:8], 0, PJ - 1)

        @block.scalar
        def _(e):
            e.wait_ge(const_in, 32)

            def norm(hf, ph, src):
                begin(e, hf, ph, "act")
                st = halves[hf][ph]["act"]
                for i in range(NT):
                    if ph == "norm" and i == 3:
                        for u in range(2):
                            split_hi(e, hf, "rkv", u, 0, st, f"s{u}")
                    if ph == "norm":
                        e.wait_ge(x_in[i % 2], 16 * (2 * hf + i // 2 + 1))
                    e.activation(jk[:], src(i), ACT.Square, accum_out=small[:, i:i + 1]).then_inc(act_steps, st.step(f"sq{i}"))
                    e.wait_ge(vec_steps, after(hf, ph, "vec", f"ms{i}"))
                    e.activation(small[:, 8 + i:9 + i], small[:, 4 + i:5 + i], ACT.Sqrt).then_inc(act_steps, st.step(f"root{i}"))
                    for b in range(2):
                        e.wait_ge(pe_steps, after(hf, ph, "pe", f"tr{i}_{b}"))
                        e.activation(xhi[:, 4 * b:4 * b + 4, P * i:P * i + P],
                                             bank[b][:].rearrange("p (k n) -> p k n", k=4), ACT.Copy).then_inc(act_steps, st.step(f"hi{i}_{b}"))

            def mix_tile(hf, t):
                ph = "mix"
                st = halves[hf][ph]["act"]

                def act(name, dst, src, fn=ACT.Copy, **kw):
                    e.activation(dst, src, fn, **kw).then_inc(act_steps, st.step(name))

                def tile(x):
                    return x[:, bass.ds(t, 1), :].rearrange("p a d -> p (a d)")

                def parity(x, odd):
                    return x.rearrange("p (a b n) -> p b a n", b=2, n=CH)[:, odd]

                def parity_bank(x):
                    return x[:, 0:4 * CH].rearrange("p (a n) -> p a n", a=4)

                def blocks(name, dst, src):
                    for c in range(2):
                        cs = slice(CH * c, CH * c + CH)
                        act(f"{name}{'ab'[c]}", dst[cs, :, cs], src[cs, :, :])

                def Yb(lv):
                    e.wait_ge(vec_steps, after(hf, ph, "vec", f"Y{lv}", t))
                    blocks(f"Yb{lv}", Ybd, Yst)

                def Tb(lv):
                    e.wait_ge(vec_steps, after(hf, ph, "vec", f"T{lv}" if lv < 6 else "TT6", t))
                    blocks(f"Tb{lv}", Tbd, Tst if lv < 6 else Tt)

                def out_of(name, dst, b, pe_name):
                    e.wait_ge(pe_steps, after(hf, ph, "pe", pe_name, t))
                    act(name, dst, b)

                def ex(h):
                    act(f"ex{h}", pr[:, h, CH:2 * P], scb[:, h, :], ACT.Exp, bias=den8[:, 1, h:h + 1],
                        accum_out=den8[:, 3, h:h + 1])

                def pt(n):
                    out_of(f"PT{n}", pT[:, 2 * n:2 * n + 2, :, :],
                           bank[6 + n % 2][:].rearrange("p (a b c) -> p a b c", a=2, b=2), f"PT{n}")

                e.wait_ge(vec_steps, after(hf, ph, "vec", "Hb", t - 1))
                e.wait_ge(pool_steps, after(hf, ph, "pool", "Wb", t - 1))
                act("E", E[:], tile(L), ACT.Exp, scale=-DECAY)
                act("Ei", Ei[:], tile(L), ACT.Exp, scale=DECAY)
                e.wait_ge(vec_steps, after(hf, ph, "vec", "Lp", t))
                act("Ep", Ep[:], Lp[:], ACT.Exp, scale=-DECAY)
                act("qs", qs[:], tile(qT).rearrange("p (j n) -> p j n", j=NP), scale=HD ** -0.5)
                act("kw", kw[:], kT[:, bass.ds(t * P + CH, WIN)])
                e.wait_ge(pe_steps, after(hf, ph, "pe", "YU", t - 1))
                e.wait_ge(pool_steps, after(hf, ph, "pool", "BV", t - 1))
                out_of("trA", At[:], bank[0][:], "trA")
                out_of("trV", Vt[:], bank[1][:], "trV")
                Yb(1)
                out_of("trK", Kt[:], bank[5][:], "trK")
                Tb(1)
                Yb(2)
                out_of("trB", Bt[:], bank[0][:], "trB")
                Tb(2)
                e.wait_ge(vec_steps, after(hf, ph, "vec", "nm", t))
                for h in range(4):
                    ex(h)
                Yb(3)
                for h in range(4, 8):
                    ex(h)
                Tb(3)
                e.wait_ge(vec_steps, after(hf, ph, "vec", "sd", t))
                act("esink", den8[:, 4, :], den8[:, 2, :], ACT.Exp)
                Yb(4)
                pt(0)
                Tb(4)
                pt(1)
                Yb(5)
                pt(2)
                Tb(5)
                out_of("X1", X1[:], bank[1][:], "X1")
                pt(3)
                Tb(6)
                out_of("TAT", TAT[:], bank[5][:], "TAT")
                for c in range(2):
                    cs, nm = slice(CH * c, CH * c + CH), "ab"[c]
                    for odd in range(2):
                        out_of(f"U{nm}{odd}", parity(U[cs, :], odd), parity_bank(ub[odd][cs, :]), "UA" + nm)
                e.wait_ge(pe_steps, after(hf, ph, "pe", "YU", t))
                for odd, nm in enumerate(("Y0", "Y")):
                    act(nm, parity(tile(rows_y), odd), parity_bank(yb[odd]))

            for hf in range(HALVES):
                norm(hf, "norm", lambda i: xt[i % 2][:])
                begin(e, hf, "rkv", "act")
                st = halves[hf]["rkv"]["act"]

                def project(g, last):
                    for n in range(4):
                        if n < 2:
                            split_hi(e, hf, "rkv", n + 2, g, st, f"s{n}")
                        elif last:
                            split_hi(e, hf, "lora", n - 2, 0, st, f"s{n}")
                        else:
                            split_hi(e, hf, "rkv", n - 2, g + 1, st, f"s{n}")
                        e.wait_ge(pe_steps, after(hf, "rkv", "pe", f"u{n}", g))
                        e.wait_ge(vec_steps, after(hf, "rkv", "vec", f"c{n - 2}" if n >= 2 else f"c{n + 2}", g if n >= 2 else g - 1))
                        e.activation(shr[n % 2][:, 1:1 + HALF], bank[n][:], ACT.Copy).then_inc(act_steps, st.step(f"e{n}"))

                with e.Fori(0, 2) as g:
                    project(g, False)
                project(2, True)
                st = halves[hf]["lora"]["act"]
                dst = [shr[0][:, 1:1 + HALF], shr[1][:, 1:1 + HALF], kT[:, P:P + HALF], vT[:]]
                for n in range(4):
                    if n < 2:
                        split_hi(e, hf, "lora", n + 2, 0, st, f"s{n}")
                        e.wait_ge(vec_steps, after(hf, "rkv", "vec", f"c{n + 2}", 2))
                    else:
                        split_hi(e, hf, "q", n - 2, 0, st, f"s{n}")
                    e.wait_ge(pe_steps, after(hf, "lora", "pe", f"u{n}"))
                    e.activation(dst[n], bank[n][:], ACT.Copy).then_inc(act_steps, st.step(f"e{n}"))
                st = halves[hf]["q"]["act"]

                def queries(n):
                    e.wait_ge(pe_steps, after(hf, "q", "pe", f"u{n}"))
                    e.activation(qT[:, :, P * n:P * n + P], bank[n][:].rearrange("p (t n) -> p t n", t=NT), ACT.Copy).then_inc(act_steps, st.step(f"e{n}"))

                def squares(p):
                    k_p = rkv[:, 1, :, P * p:P * p + P]
                    e.activation(sq[p][:].rearrange("p (t n) -> p t n", t=NT), k_p, ACT.Square,
                                 scale=par[:, KK_ + p:KK_ + p + 1]).then_inc(act_steps, st.step(f"sq{p}"))

                split_hi(e, hf, "q", 2, 0, st, "s0")
                queries(0)
                e.wait_ge(vec_steps, after(hf, "lora", "vec", "s1"))
                e.activation(th[:], wa[0:HD, :], ACT.Tanh).then_inc(act_steps, st.step("th"))
                e.activation(sg[:], gd[:], ACT.Sigmoid).then_inc(act_steps, st.step("sg"))
                split_hi(e, hf, "q", 3, 0, st, "s1")
                queries(1)
                squares(0)
                squares(1)
                queries(2)
                squares(2)
                squares(3)
                queries(3)
                e.wait_ge(pe_steps, after(hf, "q", "pe", "ss"))
                e.activation(rn[:, 0, :], bank[6][0:8, :], ACT.Sqrt).then_inc(act_steps, st.step("root"))
                for p in range(NP):
                    for nm, dst_, off, b in (("w", sig, W0, 4), ("a", av, A0, 5)):
                        e.wait_ge(pe_steps, after(hf, "q", "pe", f"{nm}{p}"))
                        e.activation(dst_[:, :, P * p:P * p + P],
                                     bank[b][:].rearrange("p (t n) -> p t n", t=NT), ACT.Sigmoid,
                                     bias=par[:, off + p:off + p + 1]).then_inc(act_steps, st.step(f"{nm}_{p}"))
                e.wait_ge(pe_steps, after(hf, "q", "pe", "vt"))
                e.activation(vA[:, 1:1 + NT, :], bank[7][:].rearrange("p (t n) -> p t n", t=NT), ACT.Copy).then_inc(act_steps, st.step("vt"))
                begin(e, hf, "mix", "act")
                with e.Fori(0, NT) as t:
                    mix_tile(hf, t)
                begin(e, hf, "gate", "act")
                st = halves[hf]["gate"]["act"]
                for i in range(NT):
                    if i == 2:
                        for u in range(2):
                            split_hi(e, hf, "out", u, 0, st, f"s{u}")
                    e.wait_ge(vec_steps, after(hf, "gate", "vec", f"yc{i}"))
                    e.activation(gsq[:], gyn[:], ACT.Square).then_inc(act_steps, st.step(f"sq{i}"))
                    e.wait_ge(vec_steps, after(hf, "gate", "vec", f"var{i}"))
                    e.activation(den8[:, 2, :], den8[:, 1, :], ACT.Sqrt).then_inc(act_steps, st.step(f"root{i}"))
                    for b in range(2):
                        e.wait_ge(pe_steps, after(hf, "gate", "pe", f"tr{b}_{i}"))
                        e.activation(xhi[:, 4 * b:4 * b + 4, P * i:P * i + P],
                                             bank[b][:].rearrange("p (k n) -> p k n", k=4), ACT.Copy).then_inc(act_steps, st.step(f"h{b}_{i}"))
                st = halves[hf]["out"]["act"]
                for u in range(8):
                    if u < 6:
                        split_hi(e, hf, "out", u + 2, 0, st, f"s{u}")
                    else:
                        split_hi(e, hf, "up", u - 6, 0, st, f"s{u}")
                begin(e, hf, "post", "act")
                st = halves[hf]["post"]["act"]
                for i in range(NT):
                    e.activation(jk[:, 0:512], bank[i][:], ACT.Square, accum_out=small[:, 16:17]).then_inc(act_steps, st.step(f"sqa{i}"))
                    e.activation(jk[:, 512:1024], bank[4 + i][:], ACT.Square, accum_out=small[:, 17:18]).then_inc(act_steps, st.step(f"sqb{i}"))
                    e.wait_ge(vec_steps, after(hf, "post", "vec", f"ms{i}"))
                    e.activation(small[:, 20:21], small[:, 19:20], ACT.Sqrt).then_inc(act_steps, st.step(f"root{i}"))
                norm(hf, "fnorm", lambda i: hres[:, i, :])
                begin(e, hf, "up", "act")
                st = halves[hf]["up"]["act"]

                def hidden(g, last):
                    for u in range(4):
                        n, m, k = u // 2, u % 2, "gv"[u % 2]
                        if u < 2:
                            split_hi(e, hf, "up", u + 2, g, st, f"s{u}")
                        elif last:
                            split_hi(e, hf, "down", u - 2, 0, st, f"s{u}")
                        else:
                            split_hi(e, hf, "up", u - 2, g + 1, st, f"s{u}")
                        e.wait_ge(pe_steps, after(hf, "up", "pe", f"u{u}", g))
                        e.wait_ge(vec_steps, after(hf, "up", "vec", f"k{k}{n}", g - 1))
                        e.activation(cr[n][m][:, 2:2 + HALF], bank[u][:], ACT.Copy).then_inc(act_steps, st.step(f"e{k}{n}"))
                        if m:
                            e.wait_ge(vec_steps, after(hf, "up", "vec", f"0g{n}", g))
                            e.wait_ge(vec_steps, after(hf, "up", "vec", f"m{1 - n}", g if n else g - 1))
                            e.activation(gl[:], cc[n][0][:], ACT.Gelu_apprx_tanh).then_inc(act_steps, st.step(f"ge{n}"))

                with e.Fori(0, PJ // 2 - 1) as g:
                    hidden(g, False)
                hidden(PJ // 2 - 1, True)
                st = halves[hf]["down"]["act"]
                for n in range(2):
                    for u in range(11):
                        if u < 9:
                            split_hi(e, hf, "down", u + 2, n, st, f"s{n}_{u}")
                        elif n == 0:
                            split_hi(e, hf, "down", u - 9, 1, st, f"s{n}_{u}")
                    e.wait_ge(pe_steps, after(hf, "down", "pe", "u10", n))
                    for i in range(2):
                        e.activation(fo[:, i, 512 * n:512 * n + 512], bank[4 + i][:], ACT.Copy).then_inc(act_steps, st.step(f"f{i}_{n}"))
                begin(e, hf, "last", "act")
                st = halves[hf]["last"]["act"]
                for i in range(NT):
                    e.activation(fj[:], fo[:, i, :], ACT.Square, accum_out=small[:, i:i + 1]).then_inc(act_steps, st.step(f"sq{i}"))
                    e.wait_ge(vec_steps, after(hf, "last", "vec", f"ms{i}"))
                    e.activation(small[:, 8 + i:9 + i], small[:, 4 + i:5 + i], ACT.Sqrt).then_inc(act_steps, st.step(f"root{i}"))

        @block.vector
        def _(e):
            for n, cell in enumerate((shcar[:], cvcar[:], vA[:, 0, :], H[0][:])):
                e.memset(cell, 0.0).then_inc(sems["vec"], 1)
            e.wait_ge(const_in, 32)

            def mean_square(v, i, name="ms"):
                e.tensor_scalar(small[:, 4 + i:5 + i], small[:, i:i + 1], 1.0 / D, EPS, ALU.mult, ALU.add).then_inc(vec_steps, v.step(f"{name}{i}"))

            def norm(hf, ph, src, gains):
                begin(e, hf, ph, "vec")
                e.wait_ge(gain_in, 16 * gains)
                v = Pass(hf, ph)
                for i in range(NT):
                    e.wait_ge(act_steps, after(hf, ph, "act", f"sq{i}"))
                    mean_square(v, i)
                    e.wait_ge(act_steps, after(hf, ph, "act", f"root{i}"))
                    e.reciprocal(small[:, 12 + i:13 + i], small[:, 8 + i:9 + i]).then_inc(vec_steps, v.step(f"rstd{i}"))
                    if i >= 2:
                        e.wait_ge(pe_steps, after(hf, ph, "pe", f"tr{i - 2}_1"))
                    e.wait_ge(vec_steps, v.after(f"rstd{i}"))
                    e.scalar_tensor_tensor(xs[i % 2][:], src(i), small[:, 12 + i:13 + i], gain[:], ALU.mult, ALU.mult).then_inc(vec_steps, v.step(f"xs{i}"))
                    for b in range(2):
                        e.wait_ge(act_steps, after(hf, ph, "act", f"hi{i}_{b}"))
                        cols = (slice(None), slice(4 * b, 4 * b + 4), slice(P * i, P * i + P))
                        e.tensor_tensor(xlo[cols], bank[b][:].rearrange("p (k n) -> p k n", k=4), xhi[cols].bitcast(F32), ALU.subtract).then_inc(vec_steps, v.step(f"lo{i}_{b}"))

            def shift_tile(v, n, copied, mu, car, dst, four=True):
                s = shr[n % 2]
                e.tensor_copy(s[:, 0:1], car).then_inc(vec_steps, v.step(f"b{n}"))
                e.wait_ge(act_steps, copied)
                e.wait_ge(vec_steps, v.after(f"b{n}"))
                e.tensor_tensor(shd[:], s[:, 0:HALF], s[:, 1:1 + HALF], ALU.subtract).then_inc(vec_steps, v.step(f"d{n}"))
                e.wait_ge(vec_steps, v.after(f"d{n}"))
                x, y = shd[:], s[:, 1:1 + HALF]
                if four:
                    x, y = (z.rearrange("p (t n) -> p t n", t=NT) for z in (x, y))
                e.scalar_tensor_tensor(dst, x, mu, y, ALU.mult, ALU.add).then_inc(vec_steps, v.step(f"s{n}"))
                e.tensor_copy(car, s[:, HALF:HALF + 1]).then_inc(vec_steps, v.step(f"c{n}"))

            def mix_tile(hf, t):
                ph = "mix"
                v = Pass(hf, ph, t)

                def tile(x):
                    return x[:, bass.ds(t, 1), :].rearrange("p a d -> p (a d)")

                def four(x):
                    return x.rearrange("p (h n) -> p h n", h=4)

                def eight(x):
                    return x.rearrange("p (h n) -> p h n", h=HEADS)

                def over(x, n):
                    return x.unsqueeze(1).to_broadcast([P, n, x.shape[1]])

                def each(x):
                    return x.unsqueeze(2).to_broadcast([P, HEADS, CH])

                def masked(name, dst, odd, b, mask):
                    e.wait_ge(pe_steps, after(hf, ph, "pe", name, t))
                    e.tensor_tensor(dst[:].rearrange("p (a b) n -> p b a n", b=2)[:, odd], four(b[:]), over(mask, 4), ALU.mult).then_inc(vec_steps, v.step(name))

                def scores(j):
                    e.wait_ge(pe_steps, after(hf, ph, "pe", f"sc{j}", t))
                    h2 = slice(4 * (j % 2) + 2 * (j // 2), 4 * (j % 2) + 2 * (j // 2) + 2)
                    e.tensor_tensor(scb[:, h2, :], bank[6 + j % 2][:, 0:2 * WIN].rearrange("p (a n) -> p a n", a=2), table[:, h2, :], ALU.add).then_inc(vec_steps, v.step(f"sb{j}"))
                    e.wait_ge(vec_steps, v.after(f"sb{j}"))
                    e.tensor_reduce(den8[:, 0, h2], scb[:, h2, :], AX, ALU.max).then_inc(vec_steps, v.step(f"mx{j}"))

                def Y(lv):
                    e.wait_ge(pe_steps, after(hf, ph, "pe", f"Y{lv}", t))
                    e.tensor_tensor(Yst[:], eight(bank[2][:]), over(level[lv - 1], HEADS), ALU.mult).then_inc(vec_steps, v.step(f"Y{lv}"))

                def TT(lv):
                    e.wait_ge(pe_steps, after(hf, ph, "pe", f"TT{lv}", t))
                    e.tensor_tensor(Tt[:], eight(bank[3][:]), over(eye, HEADS) if lv == 1 else Tt[:], ALU.add).then_inc(vec_steps, v.step(f"TT{lv}"))

                def T(lv):
                    e.wait_ge(pe_steps, after(hf, ph, "pe", f"T{lv}", t))
                    if lv > 1:
                        e.wait_ge(act_steps, after(hf, ph, "act", f"Tb{lv - 1}b", t))
                    e.tensor_tensor(Tst[:], eight(bank[4][:]), over(eye, HEADS) if lv == 1 else Tst[:], ALU.add).then_inc(vec_steps, v.step(f"T{lv}"))

                e.wait_ge(act_steps, after(hf, ph, "act", "Y", t - 1))
                e.wait_ge(pe_steps, after(hf, ph, "pe", "YU", t - 1))
                e.wait_ge(pool_steps, after(hf, ph, "pool", "Wb", t - 1))
                e.tensor_tensor(Lp[:], tile(L), tile(sig), ALU.subtract).then_inc(vec_steps, v.step("Lp"))
                e.wait_ge(act_steps, after(hf, ph, "act", "Ep", t))
                e.scalar_tensor_tensor(AN[:], tile(kk), -1.0, Ep[:], ALU.mult, ALU.mult).then_inc(vec_steps, v.step("AN"))
                e.tensor_tensor(BT[:], tile(av), Ei[:], ALU.mult).then_inc(vec_steps, v.step("BT"))
                e.tensor_tensor(KTl[:], rkv[:, 1, bass.ds(t, 1), :].rearrange("p a d -> p (a d)"), Ei[:], ALU.mult).then_inc(vec_steps, v.step("KT"))
                e.tensor_tensor(RT[:], rkv[:, 0, bass.ds(t, 1), :].rearrange("p a d -> p (a d)"), E[:], ALU.mult).then_inc(vec_steps, v.step("RT"))
                e.tensor_copy(Vst[:], rkv[:, 2, bass.ds(t, 1), :].rearrange("p a d -> p (a d)")).then_inc(vec_steps, v.step("Vst"))
                masked("G0", G, 0, bank[2], lower)
                masked("G1", G, 1, bank[3], lower)
                e.wait_ge(pool_steps, after(hf, ph, "pool", "tab", t - 1))
                scores(0)
                scores(1)
                Y(1)
                TT(1)
                scores(2)
                T(1)
                scores(3)
                e.wait_ge(vec_steps, v.after("mx3"))
                e.tensor_tensor(den8[:, 5, :], den8[:, 0, :], sink, ALU.max).then_inc(vec_steps, v.step("m"))
                e.wait_ge(vec_steps, v.after("m"))
                e.tensor_scalar(den8[:, 1, :], den8[:, 5, :], -1.0, None, ALU.mult).then_inc(vec_steps, v.step("nm"))
                e.tensor_tensor(den8[:, 2, :], sink, den8[:, 5, :], ALU.subtract).then_inc(vec_steps, v.step("sd"))
                Y(2)
                TT(2)
                masked("MKA0", MKA, 0, bank[1], upper)
                T(2)
                masked("MKA1", MKA, 1, bank[5], upper)
                Y(3)
                masked("MRB0", MRB, 0, bank[0], uppeq)
                TT(3)
                masked("MRB1", MRB, 1, bank[1], uppeq)
                T(3)
                Y(4)
                masked("MRK0", MRK, 0, bank[5], uppeq)
                TT(4)
                T(4)
                masked("MRK1", MRK, 1, bank[0], uppeq)
                Y(5)
                TT(5)
                T(5)
                e.wait_ge(act_steps, after(hf, ph, "act", "esink", t))
                e.tensor_tensor(den8[:, 4, :], den8[:, 3, :], den8[:, 4, :], ALU.add).then_inc(vec_steps, v.step("den"))
                e.wait_ge(vec_steps, v.after("den"))
                e.reciprocal(den8[:, 0, :], den8[:, 4, :]).then_inc(vec_steps, v.step("rden"))
                Y(6)
                e.wait_ge(pe_steps, after(hf, ph, "pe", "PV", t))
                e.wait_ge(vec_steps, v.after("rden"))
                e.tensor_tensor(rows_a[:, bass.ds(t, 1), :].rearrange("p a (h n) -> p (a h) n", h=HEADS), eight(bank[6][:]), each(den8[:, 0, :]), ALU.mult).then_inc(vec_steps, v.step("PV"))
                TT(6)
                e.wait_ge(pe_steps, after(hf, ph, "pe", "bonus", t))
                e.tensor_copy(small[:, 32:40], bank[7][:, 0:8]).then_inc(vec_steps, v.step("bon"))
                for c in range(2):
                    nm = "ab"[c]
                    e.wait_ge(pe_steps, after(hf, ph, "pe", "HB" + nm, t))
                    e.wait_ge(pool_steps, after(hf, ph, "pool", "W" + nm, t))
                    b = bank[5] if c == 0 else bank[2]
                    e.tensor_tensor(H[1 - c][:], HW[:], b[:, 0:NP * HD].rearrange("p (a n) -> p a n", a=NP), ALU.add).then_inc(vec_steps, v.step("H" + nm))

            def last_of(hf):
                return 4 * hf

            for hf in range(HALVES):
                norm(hf, "norm", lambda i: xt[i % 2][:], 4 * hf + 1)
                begin(e, hf, "rkv", "vec")
                with e.Fori(0, 3) as g:
                    v = Pass(hf, "rkv", g)
                    for n in range(4):
                        shift_tile(v, n, after(hf, "rkv", "act", f"e{n}", g),
                                   par[:, bass.ds(g * 4 + n, 1)], shcar[:, bass.ds(g * 4 + n, 1)],
                                   rkv[:, bass.ds(g, 1), :, P * n:P * n + P].rearrange("p a t n -> p (a t) n"))
                v = Pass(hf, "lora")
                e.wait_ge(mix_in, 96 * (hf + 1))
                for n, dst in enumerate((wa, gd)):
                    shift_tile(v, n, after(hf, "lora", "act", f"e{n}"), par[:, 12 + n:13 + n],
                               shcar[:, 12 + n:13 + n], dst[:], four=False)
                for p in range(NP):
                    e.tensor_scalar(kk[:, :, P * p:P * p + P], rkv[:, 1, :, P * p:P * p + P], par[:, KK_ + p:KK_ + p + 1], None, ALU.mult).then_inc(vec_steps, v.step(f"kr{p}"))
                v = Pass(hf, "q")
                e.wait_ge(act_steps, after(hf, "q", "act", "root"))
                e.tensor_scalar(rn[:, 1, :], rn[:, 0, :], 1e-12, None, ALU.max).then_inc(vec_steps, v.step("nmax"))
                e.wait_ge(vec_steps, v.after("nmax"))
                e.reciprocal(rn[:, 2, :], rn[:, 1, :]).then_inc(vec_steps, v.step("rn"))
                for p in range(NP):
                    part = (slice(None), slice(None), slice(P * p, P * p + P))
                    k_p = rkv[:, 1, :, P * p:P * p + P]
                    b4 = bank[p][:].rearrange("p (t n) -> p t n", t=NT)
                    tmp = shd[:].rearrange("p (t n) -> p t n", t=NT)
                    e.wait_ge(pe_steps, after(hf, "q", "pe", f"bc{p}"))
                    e.tensor_tensor(kk[part], kk[part], b4, ALU.mult).then_inc(vec_steps, v.step(f"kn{p}"))
                    if p:
                        e.wait_ge(vec_steps, v.after(f"k{p - 1}"))
                    e.wait_ge(act_steps, after(hf, "q", "act", f"a_{p}"))
                    e.tensor_scalar(tmp, av[part], 1.0, par[:, KA + p:KA + p + 1], ALU.subtract, ALU.mult).then_inc(vec_steps, v.step(f"t{p}"))
                    e.wait_ge(vec_steps, v.after(f"t{p}"))
                    e.scalar_tensor_tensor(k_p, tmp, 1.0, k_p, ALU.add, ALU.mult).then_inc(vec_steps, v.step(f"k{p}"))
                    e.tensor_tensor(av[part], av[part], kk[part], ALU.mult).then_inc(vec_steps, v.step(f"b{p}"))
                e.wait_ge(act_steps, after(hf, "q", "act", "w_3"))
                for t in range(NT):
                    e.tensor_tensor_scan(L[:, t, :], chunks[:], sig[:, t, :], 0.0, ALU.mult, ALU.add).then_inc(vec_steps, v.step(f"scan{t}"))
                begin(e, hf, "mix", "vec")
                with e.Fori(0, NT) as t:
                    mix_tile(hf, t)
                begin(e, hf, "gate", "vec")
                e.wait_ge(ln_in, 32 * (hf + 1))
                v = Pass(hf, "gate")
                g8 = gyn[:].rearrange("p (h n) -> p h n", h=HEADS)
                each = lambda x: x.unsqueeze(2).to_broadcast([P, HEADS, HD])
                for i in range(NT):
                    y8 = rows_y[:, i, :].rearrange("p (h n) -> p h n", h=HEADS)
                    e.tensor_reduce(den8[:, 0, :], y8, AX, ALU.add).then_inc(vec_steps, v.step(f"sum{i}"))
                    e.wait_ge(vec_steps, v.after(f"sum{i}"))
                    e.tensor_scalar(den8[:, 0, :], den8[:, 0, :], 1.0 / HD, None, ALU.mult).then_inc(vec_steps, v.step(f"mean{i}"))
                    e.wait_ge(vec_steps, v.after(f"mean{i}"))
                    e.tensor_tensor(g8, y8, each(den8[:, 0, :]), ALU.subtract).then_inc(vec_steps, v.step(f"yc{i}"))
                    e.wait_ge(act_steps, after(hf, "gate", "act", f"sq{i}"))
                    e.tensor_reduce(den8[:, 1, :], gsq[:].rearrange("p (h n) -> p h n", h=HEADS), AX, ALU.add).then_inc(vec_steps, v.step(f"ssq{i}"))
                    e.wait_ge(vec_steps, v.after(f"ssq{i}"))
                    e.tensor_scalar(den8[:, 1, :], den8[:, 1, :], 1.0 / HD, GN_EPS, ALU.mult, ALU.add).then_inc(vec_steps, v.step(f"var{i}"))
                    e.wait_ge(act_steps, after(hf, "gate", "act", f"root{i}"))
                    e.reciprocal(den8[:, 3, :], den8[:, 2, :]).then_inc(vec_steps, v.step(f"rstd{i}"))
                    e.wait_ge(vec_steps, v.after(f"rstd{i}"))
                    e.tensor_tensor(g8, g8, each(den8[:, 3, :]), ALU.mult).then_inc(vec_steps, v.step(f"yn{i}"))
                    e.wait_ge(vec_steps, v.after(f"yn{i}"))
                    e.tensor_tensor(gyn[:], gyn[:], lnw[:], ALU.mult).then_inc(vec_steps, v.step(f"lw{i}"))
                    e.wait_ge(vec_steps, v.after(f"lw{i}"))
                    e.tensor_tensor(gyn[:], gyn[:], lnb[:], ALU.add).then_inc(vec_steps, v.step(f"lb{i}"))
                    e.wait_ge(vec_steps, v.after(f"lb{i}"))
                    e.tensor_tensor(gyn[:], gyn[:], bv[:, i, :], ALU.add).then_inc(vec_steps, v.step(f"bv{i}"))
                    e.wait_ge(vec_steps, v.after(f"bv{i}"))
                    e.wait_ge(pe_steps, after(hf, "gate", "pe", f"g{i}"))
                    e.tensor_tensor(rows_y[:, i, :], gyn[:], bank[4 + i][:], ALU.mult).then_inc(vec_steps, v.step(f"g{i}"))
                    for b in range(2):
                        e.wait_ge(act_steps, after(hf, "gate", "act", f"h{b}_{i}"))
                        cols = (slice(None), slice(4 * b, 4 * b + 4), slice(P * i, P * i + P))
                        e.tensor_tensor(xlo[cols], bank[b][:].rearrange("p (k n) -> p k n", k=4), xhi[cols].bitcast(F32), ALU.subtract).then_inc(vec_steps, v.step(f"l{b}_{i}"))
                begin(e, hf, "post", "vec")
                e.wait_ge(gain_in, 16 * (4 * hf + 2))
                e.wait_ge(h_in, 16 * NT * (hf + 1))
                v = Pass(hf, "post")
                for i in range(NT):
                    e.wait_ge(act_steps, after(hf, "post", "act", f"sqb{i}"))
                    e.tensor_tensor(small[:, 18:19], small[:, 16:17], small[:, 17:18], ALU.add).then_inc(vec_steps, v.step(f"ss{i}"))
                    e.wait_ge(vec_steps, v.after(f"ss{i}"))
                    e.tensor_scalar(small[:, 19:20], small[:, 18:19], 1.0 / D, EPS, ALU.mult, ALU.add).then_inc(vec_steps, v.step(f"ms{i}"))
                    e.wait_ge(act_steps, after(hf, "post", "act", f"root{i}"))
                    e.reciprocal(small[:, 21:22], small[:, 20:21]).then_inc(vec_steps, v.step(f"rstd{i}"))
                    e.wait_ge(vec_steps, v.after(f"rstd{i}"))
                    e.scalar_tensor_tensor(xs[0][:, 0:512], bank[i][:], small[:, 21:22], gain[:, 0:512], ALU.mult, ALU.mult).then_inc(vec_steps, v.step(f"ma{i}"))
                    e.scalar_tensor_tensor(xs[0][:, 512:1024], bank[4 + i][:], small[:, 21:22], gain[:, 512:1024], ALU.mult, ALU.mult).then_inc(vec_steps, v.step(f"mb{i}"))
                    e.wait_ge(vec_steps, v.after(f"mb{i}"))
                    e.tensor_tensor(hres[:, i, :], hres[:, i, :], xs[0][:], ALU.add).then_inc(vec_steps, v.step(f"h{i}"))
                norm(hf, "fnorm", lambda i: hres[:, i, :], 4 * hf + 3)
                begin(e, hf, "up", "vec")
                with e.Fori(0, PJ // 2) as g:
                    v = Pass(hf, "up", g)
                    for n in range(2):
                        def col(first, m):
                            return par[:, bass.ds(g * 2 + (first + PJ * m + n), 1)]

                        gv = list(enumerate("gv"))
                        for m, k in gv:
                            e.tensor_copy(cr[n][m][:, 0:2], cvcar[:, bass.ds(g * 2 + (PJ * m + n), 1), :].rearrange("p a n -> p (a n)")).then_inc(vec_steps, v.step(f"i{k}{n}"))
                        for m, k in gv:
                            e.wait_ge(act_steps, after(hf, "up", "act", f"e{k}{n}", g))
                            e.tensor_scalar(cc[n][m][:], cr[n][m][:, 2:2 + HALF], col(CW + 4 * PJ, m), col(CB, m), ALU.mult, ALU.add).then_inc(vec_steps, v.step(f"c{k}{n}"))
                            for tap in (1, 0):
                                e.wait_ge(vec_steps, v.after(f"{'c' if tap else '1'}{k}{n}"))
                                e.scalar_tensor_tensor(cc[n][m][:], cr[n][m][:, tap:tap + HALF], col(CW + 2 * PJ * tap, m), cc[n][m][:], ALU.mult, ALU.add).then_inc(vec_steps, v.step(f"{tap}{k}{n}"))
                            e.tensor_copy(cvcar[:, bass.ds(g * 2 + (PJ * m + n), 1), :].rearrange("p a n -> p (a n)"), cr[n][m][:, HALF:HALF + 2]).then_inc(vec_steps, v.step(f"k{k}{n}"))
                        e.wait_ge(act_steps, after(hf, "up", "act", f"ge{n}", g))
                        e.wait_ge(vec_steps, v.after(f"0v{n}"))
                        e.tensor_tensor(cc[n][0][:], gl[:], cc[n][1][:], ALU.mult).then_inc(vec_steps, v.step(f"m{n}"))
                        e.wait_ge(vec_steps, v.after(f"m{n}"))
                        part = ghi[:, bass.ds(g * 2 + n, 1), :].rearrange("p a d -> p (a d)")
                        e.tensor_copy(part, cc[n][0][:]).then_inc(vec_steps, v.step(f"hi{n}"))
                        e.wait_ge(vec_steps, v.after(f"hi{n}"))
                        e.tensor_tensor(glo[:, bass.ds(g * 2 + n, 1), :].rearrange("p a d -> p (a d)"), cc[n][0][:], part.bitcast(F32), ALU.subtract).then_inc(vec_steps, v.step(f"lo{n}"))
                with e.Fori(0, 2) as n:
                    v = Pass(hf, "down", n)
                    e.wait_ge(pe_steps, after(hf, "down", "pe", "u10", n))
                    for i in (2, 3):
                        e.tensor_copy(fo[:, i, bass.ds(n * 512, 512)], bank[4 + i][:]).then_inc(vec_steps, v.step(f"f{i}"))
                begin(e, hf, "last", "vec")
                e.wait_ge(gain_in, 16 * (4 * hf + 4))
                v = Pass(hf, "last")
                for i in range(NT):
                    e.wait_ge(act_steps, after(hf, "last", "act", f"sq{i}"))
                    mean_square(v, i)
                    e.wait_ge(act_steps, after(hf, "last", "act", f"root{i}"))
                    e.reciprocal(small[:, 12 + i:13 + i], small[:, 8 + i:9 + i]).then_inc(vec_steps, v.step(f"rstd{i}"))
                    e.wait_ge(vec_steps, v.after(f"rstd{i}"))
                    e.scalar_tensor_tensor(fo[:, i, :], fo[:, i, :], small[:, 12 + i:13 + i], gain[:], ALU.mult, ALU.mult).then_inc(vec_steps, v.step(f"m{i}"))
                    e.wait_ge(vec_steps, v.after(f"m{i}"))
                    e.tensor_tensor(hres[:, i, :], hres[:, i, :], fo[:, i, :], ALU.add).then_inc(vec_steps, v.step(f"y{i}"))

        @block.gpsimd
        def _(e):
            for cell in (kT[:, 0:P], HW[:], rn[:, 0, :]):
                e.memset(cell, 0.0).then_inc(sems["pool"], 1)
            e.wait_ge(const_in, 32)

            def tt(hf, ph, name, dst, x, y, op):
                e.tensor_tensor(dst, x, y, op).then_inc(pool_steps, halves[hf][ph]["pool"].step(name))

            def mix_tile(hf, t):
                ph = "mix"
                c8 = lambda x: x[:].rearrange("p (c n) -> p c n", c=8)
                tile = lambda x, n: x[:, n, bass.ds(t, 1), :].rearrange("p a d -> p (a d)")
                wc = c8(E)[:, :, CH - 1:CH].to_broadcast([P, 8, CH])
                e.wait_ge(vec_steps, after(hf, ph, "vec", "KT", t))
                tt(hf, ph, "KP", c8(KP), c8(KTl), wc, ALU.mult)
                tt(hf, ph, "BP", c8(BP), c8(BT), wc, ALU.mult)
                tt(hf, ph, "RK", RKp[:], tile(rkv, 0), tile(rkv, 1), ALU.mult)
                e.wait_ge(vec_steps, after(hf, ph, "vec", "sb3", t))
                e.nop(nofuse=True)
                e.tensor_copy(table[:, :, 0:CH], edge[:]).then_inc(pool_steps, halves[hf][ph]["pool"].step("tab"))

                def decayed(c):
                    w = E[:].rearrange("p (a c n) -> p a c n", a=NP, c=2)[:, :, c, CH - 1:CH].to_broadcast([P, NP, HD])
                    tt(hf, ph, "W" + "ab"[c], HW[:], H[c][:], w, ALU.mult)

                decayed(0)
                e.wait_ge(act_steps, after(hf, ph, "act", "trV", t))
                e.wait_ge(vec_steps, after(hf, ph, "vec", "bon", t))
                tt(hf, ph, "BV", bv[:, bass.ds(t, 1), :].rearrange("p a (h n) -> p (a h) n", h=HEADS), c8(Vt),
                   small[:, 32:40].unsqueeze(2).to_broadcast([P, HEADS, HD]), ALU.mult)
                e.wait_ge(vec_steps, after(hf, ph, "vec", "Ha", t))
                decayed(1)

            for hf in range(HALVES):
                for u in range(4):
                    split_lo(e, hf, "rkv", u, 0)
                with e.Fori(1, 3) as g:
                    for u in range(4):
                        split_lo(e, hf, "rkv", u, g)
                for ph in ("lora", "q"):
                    for u in range(4):
                        split_lo(e, hf, ph, u, 0)
                e.wait_ge(pe_steps, after(hf, "q", "pe", "bc3"))
                e.wait_ge(vec_steps, after(hf, "q", "vec", "k3"))
                st = halves[hf]["q"]["pool"]
                e.memset(Ybd[:], 0.0).then_inc(pool_steps, st.step("zy"))
                e.memset(Tbd[:], 0.0).then_inc(pool_steps, st.step("zt"))
                e.memset(pr[:, :, 0:CH], 0.0).then_inc(pool_steps, st.step("zp"))
                begin(e, hf, "mix", "pool")
                e.wait_ge(mix_in, 96 * (hf + 1))
                with e.Fori(0, NT) as t:
                    mix_tile(hf, t)
                begin(e, hf, "gate", "pool")
                st = halves[hf]["gate"]["pool"]
                e.tensor_copy(kT[:, 0:P], kT[:, HALF:HALF + P]).then_inc(pool_steps, st.step("kT"))
                e.tensor_copy(vA[:, 0, :], vA[:, NT, :]).then_inc(pool_steps, st.step("vA"))
                for u in range(8):
                    split_lo(e, hf, "out", u, 0)
                for u in range(4):
                    split_lo(e, hf, "up", u, 0)
                with e.Fori(1, PJ // 2) as g:
                    for u in range(4):
                        split_lo(e, hf, "up", u, g)
                for n in range(2):
                    for u in range(11):
                        split_lo(e, hf, "down", u, n)


def constants():
    f = np.float32
    i = np.arange(P)
    same = (i[:, None] // CH) == (i[None, :] // CH)
    eye = np.eye(P, dtype=f)
    lower = (same & (i[:, None] > i[None, :])).astype(f)
    stack = np.concatenate([np.eye(CH, dtype=f)] * 2)
    r, c = np.arange(CH)[:, None], np.arange(CH)[None, :]
    levels = []
    for b in LEVELS:
        m = (r // (2 * b) == c // (2 * b)) & (r // b % 2 == 0) & (c // b % 2 == 1)
        levels.append(np.concatenate([m.astype(f)] * 2))
    ones8 = np.zeros((P, NP, 8), f)
    spread = np.zeros((8, NP, P), f)
    for p in range(NP):
        for e in range(2):
            ones8[HD * e:HD * e + HD, p, 2 * p + e] = 1
            spread[2 * p + e, p, HD * e:HD * e + HD] = 1
    key = np.arange(WIN)
    dist = np.abs(i[:, None] + CH - key[None, :]).astype(f)
    seen = (key[None, :] // CH == i[:, None] // CH) | (key[None, :] // CH == i[:, None] // CH + 1)
    slopes = np.exp2(-8.0 * np.arange(1, HEADS + 1, dtype=f) / HEADS).astype(f)
    alibi = np.stack([np.where(seen, -slopes[h] * dist, -HID) for h in range(HEADS)], 1).astype(f)
    first = alibi.copy()
    first[:, :, 0:CH] = -HID
    chunks = np.ones((P, 512), f)
    chunks[:, ::CH] = 0
    return eye, lower, lower.T, lower.T + eye, stack, levels, ones8, spread, alibi, first, chunks


def kernel(**inputs):
    import concourse.bacc as bacc
    from concourse.bass_utils import run_bass_kernel_spmd

    x = {n: np.asarray(v) for n, v in inputs.items()}
    f = np.float32
    eye, lower, upper, uppeq, stack, levels, ones8, spread, alibi, first, chunks = constants()

    def tall(v):
        return np.ascontiguousarray(v.reshape(-1, P).T)

    def wide(v):
        return np.ascontiguousarray(np.broadcast_to(v.reshape(1, -1), (P, v.size)))

    bonus = np.zeros((P, 8), f)
    rk = x["rwkv_r_k"][0]
    for h in range(HEADS):
        bonus[HD * (h % 2):HD * (h % 2) + HD, h] = rk[h]
    par = np.concatenate([tall(x["rwkv_mu"][0]), tall(x["rwkv_w0"][0]), tall(x["rwkv_a0"][0]), tall(x["rwkv_k_k"][0]),
                          tall(x["rwkv_k_a"][0])] + [tall(x["ffn_conv_w"][0, n]) for n in range(3)]
                         + [tall(x["ffn_conv_b"][0]), bonus], 1)
    cst = np.concatenate([eye, lower, upper, uppeq, stack, *levels, ones8.reshape(P, -1),
                          wide(x["attn_sinks"])], 1)
    feed = {
        "x": x["x"][0], "w_in": x["w_in"][0], "w_out": x["w_out"][0], "ffn_w_up": x["ffn_w_up"][0],
        "ffn_w_down": x["ffn_w_down"][0], "par": par, "cst": cst, "spread": spread, "alibi": alibi, "first": first,
        "edge": np.ascontiguousarray(alibi[:, :, 0:CH]),
        "chunks": chunks, "lora": np.concatenate([x["rwkv_w_w2"][0], x["rwkv_w_a2"][0]], 0),
        "wg2": x["rwkv_w_g2"][0], "ln_w": wide(x["rwkv_ln_w"]), "ln_b": wide(x["rwkv_ln_b"]),
        "g_mix_pre": wide(x["norm_mix_pre"]), "g_mix_post": wide(x["norm_mix_post"]),
        "g_ffn_pre": wide(x["norm_ffn_pre"]), "g_ffn_post": wide(x["norm_ffn_post"]),
    }
    nc = bacc.Bacc("TRN2", target_bir_lowering=False, num_devices=1)
    arrays, aps = {}, {}
    for name, v in feed.items():
        v = np.ascontiguousarray(v)
        arrays[f"in_{name}"] = v
        aps[name] = nc.dram_tensor(f"in_{name}", v.shape, mybir.dt.from_np(v.dtype), kind="ExternalInput").ap()
    out = nc.dram_tensor("out", (SEQ, D), F32, kind="ExternalOutput").ap()
    build(nc, aps, out)
    r = run_bass_kernel_spmd(nc, [arrays], core_ids=[0])
    return r.results[0]["out"].reshape(1, SEQ, D)
```

```python
from contextlib import ExitStack

import numpy as np

import concourse.bass as bass
from concourse import mybir

P = 128
D, SEQ, HALF, FF = 1024, 1024, 512, 2816
HALVES, NT = SEQ // HALF, HALF // P
KT = D // P
CH, HD, HEADS, NP = 64, 64, 8, 4
PJ = FF // P
WIN = 3 * CH
LEVELS = (1, 2, 4, 8, 16, 32)
RAWS, SPLITS = 4, 2
DECAY = float(np.exp(-0.5))
EPS, GN_EPS = 1e-6, HD * 1e-5
ATT = 768
HID = 1e30

F32, F32R = mybir.dt.float32, mybir.dt.float32r
ALU, ACT, AX = mybir.AluOpType, mybir.ActivationFunctionType, mybir.AxisListType.X

MU, W0, A0, KK_, KA, CW, CB, RK = 0, 14, 18, 22, 26, 30, 30 + 6 * PJ, 30 + 8 * PJ
NPAR = RK + 8


TURNS = [f"a{i}" for i in range(NT)] + [f"y{i}" for i in range(NT)]


class Steps:

    def __init__(self, sem, names, base, times):
        assert len(set(names)) == len(names)
        self.sem, self.names, self.base, self.times, self.at = sem, names, base, times, 0

    def after(self, name, it=0):
        return self.base + self.names.index(name) + 1 + it * len(self.names)

    def end(self):
        return self.base + len(self.names) * self.times

    def step(self, name):
        assert self.names[self.at % len(self.names)] == name, (self.names[self.at % len(self.names)], name)
        self.at += 1
        return 1


def norm_steps():
    pe = [f"tr{i}_{b}" for i in range(NT) for b in range(2)]
    act = [f"sq{i}" for i in range(NT)] + ["root"] + [f"hi{i}_{b}" for i in range(NT) for b in range(2)]
    vec = ["ms", "rstd", "xs0"] + [n for i in range(NT) for n in ([f"xs{i + 1}"] if i < 3 else []) + [f"lo{i}_0", f"lo{i}_1"]]
    return pe, act, vec


def gate_steps(on):
    return (["gsum", "gmean", "gyc"], ["gssq", "gvar"], ["grstd", "gyn"]) if on else ([], [], [])


def loop_steps(more, gated):
    g0, g1, g2 = gate_steps(gated)
    lv = [[f"Y{v}_0", f"Y{v}_1"] for v in range(7)]
    tt = [[f"TT{v}_0", f"TT{v}_1"] for v in range(7)]
    tr = [[f"T{v}_0", f"T{v}_1"] for v in range(7)]
    pe = (["G0", "G1", "trA", "trV"] + lv[1] + ["sc0", "sc1", "trK", "MKA0"] + tr[1]
          + lv[2] + ["sc2"] + tt[2] + ["sc3", "MKA1"] + tr[2]
          + lv[3] + ["MRB0"] + tt[3] + ["trB"] + (["gp"] if gated else []) + tr[3]
          + lv[4] + ["MRB1"] + tt[4] + ["PT0"] + tr[4]
          + lv[5] + ["MRK0"] + tt[5] + ["PT1", "MRK1"] + tr[5]
          + lv[6] + ["X1"] + tt[6] + ["PT2", "PT3", "Z", "TAT", "bonus",
          "UAa", "HVa", "RHa", "HBa", "PV", "UAb", "HVb", "RHb", "HBb", "YU"])
    ready = ["E", "Ei", "Ep", "qs", "kw"]
    act = (["trA", "trV", "trK"] + (["gt"] if gated else []) + tr[1] + tr[2] + ["ex0", "ex1", "ex2", "ex3", "trB"] + (["gsq"] if gated else []) + tr[3]
           + (["gb"] if gated else [])
           + ["ex4", "ex5", "ex6", "ex7", "esink", "PT0"] + tr[4] + (["groot"] if gated else []) + ["PT1"] + tr[5]
           + ["X1", "PT2", "PT3", "TAT", "Ua0", "Ua1"] + (ready if more else []) + ["Ub0", "Ub1", "Y0", "Y"])
    vec = (["RT", "wend", "G0", "G1", "Y1_0", "TT1_0", "Y1_1", "TT1_1", "sb0", "sb1", "MKA0", "mx0", "mx1"]
           + lv[2] + ["sb2"] + tt[2] + ["mx2", "sb3", "mx3", "m", "nm", "sd", "MKA1"] + g0
           + lv[3] + ["MRB0"] + tt[3] + g1 + lv[4] + ["MRB1"] + tt[4] + lv[5] + ["MRK0"] + tt[5] + g2 + ["MRK1", "den", "rden"]
           + lv[6] + tt[6] + (["Lp"] if more else []) + ["bon", "Ha", "PV"]
           + (["AN", "BT", "KT", "Vst"] if more else []) + ["Hb"])
    pool = ["RK", "tab", "Wa"] + (["glw", "glb", "gbv", "gg"] if gated else []) + ["BV", "Wb"] + (["KP", "BP"] if more else [])
    return pe, act, vec, pool


def plan(sems):
    npe, nact, nvec = norm_steps()
    units = [f"u{u}" for u in range(20)]
    shift = [f"{k}{n}" for n in range(4) for k in "bdsc"]
    both = [f"{k}{n}" for n in range(4) for k in "se"]
    first = ["s0", "s1"]
    phases = {
        "norm": (npe, nact + first, nvec, [], 1),
        "rkv": (units[:4], both, shift, units[:4], 3),
        "lora": (units[:4], ["s0", "e0", "sq0", "s1", "e1", "sq1", "s2", "e2", "th", "sq2", "s3", "sq3", "e3", "sg"],
                 shift[:8] + [f"kr{p}" for p in range(NP)], units[:4], 1),
        "q": (["ss", "w0", "a0", "vt"] + [f"{k}{p}" for p in range(1, NP) for k in "wa"] + [f"bc{p}" for p in range(NP)]
              + units[:4],
              ["root", "w_0", "a_0", "vt"] + [f"{k}{p}" for p in range(1, NP) for k in ("w_", "a_")]
              + ["s0", "e0", "s1", "e1"],
              ["nmax", "rn"] + [f"{k}{p}" for p in range(NP) for k in "tk"] + ["scan0"]
              + [f"{k}{p}" for p in range(NP) for k in ("kn", "b")],
              units[:4] + ["zp"], 1),
        "prep": ([], ["E", "Ei", "Ep", "e2", "e3", "qs", "kw"], ["Lp", "AN", "BT", "KT", "Vst", "scan1", "scan2", "scan3"],
                 ["KP", "BP"], 1),
        "mix_first": (*loop_steps(True, False), 1),
        "mix": (*loop_steps(True, True), NT - 2),
        "mix_end": (*loop_steps(False, True), 1),
        "gate": (["gp"] + [f"tr_{n}" for n in TURNS],
                 ["gb", "hi_a0", "gsq", "hi_a1"] + first + ["groot"] + [f"hi_{n}" for n in TURNS[2:]],
                 gate_steps(True)[0] + ["lo_a0"] + gate_steps(True)[1] + ["lo_a1"] + gate_steps(True)[2]
                 + [f"lo_{n}" for n in TURNS[2:]],
                 ["kT", "vA", "glw", "glb", "gbv", "gg"], 1),
        "out": (units[:8], [f"s{u}" for u in range(5)] + [f"qa{i}" for i in range(NT)] + ["s5", "s6", "s7"],
                [], units[:8], 1),
        "post": (npe, [f"qb{i}" for i in range(NT)] + ["proot", "sq0", "root0", "sq1", "root1", "hi0_0", "hi0_1",
                       "sq2", "root2", "sq3", "root3"] + [f"hi{i}_{b}" for i in range(1, NT) for b in range(2)],
                 ["ss", "pms", "prstd", "ma0", "mb0", "h0", "ma1", "mb1", "ma2", "mb2", "h2", "ms0", "rstd0", "xs0",
                  "ma3", "mb3", "h3", "ms1", "rstd1", "xs1", "lo0_0", "lo0_1", "ms2", "rstd2", "xs2",
                  "ms3", "rstd3", "xs3", "lo1_0", "lo1_1", "lo2_0", "lo2_1", "lo3_0", "lo3_1"],
                 ["h1"], 1),
        "up": (units[:4], ["s0", "eg0", "s1", "ev0", "ge0", "s2", "eg1", "s3", "ev1", "ge1"],
               [f"{k}{n}" for n in range(2) for k in
                ("ig", "iv", "cg", "1g", "0g", "kg", "cv", "1v", "0v", "kv", "m", "hi", "lo")],
               units[:4], PJ // 2),
        "down0": (units[:11], [f"s{u}" for u in range(11)] + ["f0", "f1"], ["f2", "f3"], units[:11], 1),
        "down1": (units[:11], [f"s{u}" for u in range(9)] + ["f0", "f1"], ["f2", "f3"], units[:11], 1),
        "last": ([], [f"sq{i}" for i in range(NT)] + ["root"],
                 ["ms", "rstd"] + [f"{k}{i}" for i in range(NT) for k in ("m", "y")], [], 1),
    }
    base = dict(pe=0, act=0, vec=4, pool=3)
    s11 = phases["down0"][1]
    early = {"norm": ([], [], [], [], 1),
             "down0": (units[:5] + [n for i in range(NT) for n in [f"tr{i}_0", f"tr{i}_1", f"u{5 + i}"]] + units[9:11],
                       s11[:3] + ["sq0", "sq1", s11[3], "sq2", "sq3", s11[4], "root"]
                       + [n for i in range(NT) for n in (s11[5 + i], f"hi{i}_0", f"hi{i}_1")] + s11[9:],
                       nvec + ["f2", "f3"], units[:11], 1),
             "down1": (units[:11], s11, ["f2", "f3"], units[:11], 1)}
    halves = []
    for hf in range(HALVES):
        half = {}
        for name, row in phases.items():
            if name == "norm" and hf:
                row = early["norm"]
            elif name in ("down0", "down1") and hf + 1 < HALVES:
                row = early[name]
            half[name] = {}
            for eng, names in zip(("pe", "act", "vec", "pool"), row):
                s = Steps(sems[eng], names, base[eng], row[4])
                base[eng] = s.end()
                half[name][eng] = s
        halves.append(half)
    return halves, list(phases)


def build(nc, a, out):
    with ExitStack() as ctx:
        def sem(name):
            return ctx.enter_context(nc.semaphore(name))

        lo_end = (nc.sbuf_base + 31) // 32 * 32
        cursor = [lo_end]

        def sb(name, shape, dt=F32, at=None):
            size = int(np.prod(shape[1:])) * 4
            where = cursor[0] if at is None else at
            t = nc.alloc_sbuf_tensor_at("s_" + name, list(shape), dt, offset=where)
            if at is None:
                cursor[0] = where + (size + 31) // 32 * 32
            return t

        bank = [ctx.enter_context(nc.psum_tensor(f"bank{b}", [P, 512], F32)) for b in range(8)]

        par = sb("par", [P, NPAR])
        cst = sb("cst", [P, 128 * 10 + 32 + 8])
        ident, lower, upper, uppeq = (cst[:, 128 * n:128 * n + 128] for n in range(4))
        level = [cst[:, 512 + 128 * n:640 + 128 * n] for n in range(6)]
        ones8 = cst[:, 1280:1312].rearrange("p (a b) -> p a b", a=NP)
        sink = cst[:, 1312:1320]
        H = [sb(f"H{n}", [P, NP, HD]) for n in range(2)]
        HW = sb("HW", [P, NP, HD])
        shcar = sb("shcar", [P, 14])
        cvcar = sb("cvcar", [P, 2 * PJ, 2])
        kT = sb("kT", [P, P + HALF])
        vA = sb("vA", [P, NT + 1, P])
        gain = sb("gain", [P, D])
        small = sb("small", [P, 64])
        wend = sb("wend", [P, HEADS])
        den8 = sb("den8", [P, 9, HEADS])
        ring_at = cursor[0]
        raw = [sb(f"raw{n}", [P, D]) for n in range(RAWS)]
        whi = [sb(f"whi{n}", [P, D], F32R) for n in range(SPLITS)]
        wlo = [sb(f"wlo{n}", [P, D], F32R) for n in range(SPLITS)]
        xhi_at = cursor[0]
        xhi = sb("xhi", [P, KT, HALF], F32R)
        xlo = sb("xlo", [P, KT, HALF], F32R)
        free = cursor[0]

        rkv = sb("rkv", [P, 3, NT, 512])
        sig = sb("sig", [P, NT, 512])
        L = sb("L", [P, NT, 512])
        av = sb("av", [P, NT, 512])
        kk = sb("kk", [P, NT, 512])
        qT = sb("qT", [P, NT, 512])
        rows_y, rows_a, bv = rkv[:, 0], rkv[:, 2], qT
        sg = sb("sg", [P, HALF])
        spread = sb("spread", [8, NP, P])
        edge = sb("edge", [P, HEADS, CH])
        table = sb("table", [P, HEADS, WIN])
        chunks = sb("chunks", [P, 512])
        lora = sb("lora", [P, 512])
        wg2 = sb("wg2", [P, 512])
        mid = cursor[0]
        wa = sb("wa", [P, HALF])
        gd = sb("gd", [P, HALF])
        vT = sb("vT", [P, HALF])
        th = sb("th", [HD, HALF])
        shr = [sb(f"shr{n}", [P, 1 + HALF]) for n in range(2)]
        shd = sb("shd", [P, HALF])
        rn = sb("rn", [8, 3, HALF])
        sq = [sb(f"sq{p}", [P, HALF]) for p in range(NP)]
        endB = cursor[0]

        cursor[0] = xhi_at
        pr = sb("pr", [P, HEADS, 2 * P])
        pT = sb("pT", [P, HEADS, 2, P])
        scb = sb("scb", [P, HEADS, WIN])
        qs = sb("qs", [P, NP, P])
        Ep, Lp = (sb(n, [P, 512]) for n in ("Ep", "Lp"))
        assert cursor[0] <= free
        cursor[0] = ring_at
        AN, BT, KTl, RT, Vst, KP, BP, RKp = (sb(n, [P, 512]) for n in ("AN", "BT", "KTl", "RT", "Vst", "KP", "BP", "RKp"))
        G, MKA, MRB, MRK = (sb(n, [P, 2, NP, P]) for n in ("G", "MKA", "MRB", "MRK"))
        assert cursor[0] <= xhi_at
        cursor[0] = mid
        At, Kt, Bt, Vt = (sb(n, [P, 512]) for n in ("At", "Kt", "Bt", "Vt"))
        Yb, Tb, Tt = (sb(n, [P, 2, NP, P]) for n in ("Yb", "Tb", "Tt"))
        X1, U, TAT = (sb(n, [P, 512]) for n in ("X1", "U", "TAT"))
        kw = sb("kw", [P, WIN])
        cursor[0] = max(cursor[0], endB)
        gyn, gsq, gb, lnw, lnb = (sb(n, [P, 512]) for n in ("gyn", "gsq", "gb", "lnw", "lnb"))
        gt = sb("gt", [P, P])
        E, Ei = (sb(n, [P, 512]) for n in ("E", "Ei"))
        endD = cursor[0]
        endD = cursor[0]

        cursor[0] = free
        ghi = sb("ghi", [P, PJ, HALF], F32R)
        glo = sb("glo", [P, PJ, HALF], F32R)
        hres = sb("hres", [P, NT, D])
        fo_at = cursor[0]
        cr = [[sb(f"cr{n}{m}", [P, 2 + HALF]) for m in range(2)] for n in range(2)]
        cc = [[sb(f"cc{n}{m}", [P, HALF]) for m in range(2)] for n in range(2)]
        gl = sb("gl", [P, HALF])
        endF = cursor[0]
        xt_at = free
        xn = nc.alloc_sbuf_tensor_at("s_xn", [P, NT, D], F32, offset=xt_at)
        jk = nc.alloc_sbuf_tensor_at("s_jk", [P, D], F32, offset=xhi_at + KT * HALF * 4)
        gain2 = nc.alloc_sbuf_tensor_at("s_gain2", [P, D], F32, offset=xt_at + 4096 * NT)
        pj = nc.alloc_sbuf_tensor_at("s_pj", [P, D], F32, offset=fo_at)
        fj = nc.alloc_sbuf_tensor_at("s_fj", [P, D], F32, offset=xt_at)
        xr, fo = (nc.alloc_sbuf_tensor_at(f"s_{n}", [P, NT, D], F32, offset=fo_at) for n in ("xr", "fo"))
        assert max(endB, endD, endF, cursor[0]) <= nc.sbuf_usable_end

        sems = {e: sem(f"{e}_steps") for e in ("pe", "act", "vec", "pool")}
        const_in, mix_in = sem("const_in"), sem("mix_in")
        w_in_ = [sem(f"w_raw{n}") for n in range(RAWS)]
        x_in = [sem(f"x_in{i}") for i in range(NT)]
        gain_in, h_in, y_out = sem("gain_in"), sem("h_in"), sem("y_out")
        halves, order = plan(sems)

        pe_steps, act_steps, vec_steps, pool_steps = (sems[n] for n in ("pe", "act", "vec", "pool"))

        def after(hf, phase, eng, name, it=0):
            return halves[hf][phase][eng].after(name, it)

        def tile_pass(ph, t):
            return t - 1 if ph == "mix" else 0

        def tile_counts(hf, ph, t):
            def done(eng, name):
                return after(hf, ph, eng, name, tile_pass(ph, t))

            def last(eng, name):
                if ph == "mix_first":
                    return halves[hf][ph][eng].base
                return after(hf, "mix", eng, name, tile_pass("mix", t - 1))

            return done, last

        class Pass:

            def __init__(self, hf, ph, it=0):
                self.steps, self.it = halves[hf][ph]["vec"], it
                self.step = self.steps.step

            def after(self, name):
                return self.steps.after(name, self.it)

        def begin(e, hf, phase, me):
            steps = halves[hf][phase]
            if hf or phase != "norm":
                e.wait_ge(pe_steps, steps["pe"].base)
                e.wait_ge(act_steps, steps["act"].base)
            e.wait_ge(vec_steps, steps["vec"].base)
            e.wait_ge(pool_steps, steps["pool"].base)

        w1 = a["w_in"].rearrange("(k p) n -> p k n", p=P)
        wo = a["w_out"]
        wu = a["ffn_w_up"].rearrange("(k p) n -> p k n", p=P)
        wd = a["ffn_w_down"].rearrange("(k p) n -> p k n", p=P)
        UNITS = {"rkv": (4, 3), "lora": (4, 1), "q": (4, 1), "out": (8, 1), "up": (4, PJ // 2), "down0": (11, 1), "down1": (11, 1)}

        def loads(ph, u):
            return 2 if ph == "q" else 1

        ub, yb = (bank[0], bank[3]), (bank[1], bank[4])

        norms = (bank[6], bank[7], bank[4], bank[5])

        count = [0] * RAWS
        first = {}
        for hf in range(HALVES):
            for ph, (n, times) in UNITS.items():
                per = [sum(loads(ph, u) for u in range(s, n, RAWS)) for s in range(RAWS)]
                first[hf, ph] = (list(count), per)
                count = [c + p_ * times for c, p_ in zip(count, per)]

        def landed(hf, ph, u, it=0):
            base, per = first[hf, ph]
            return 16 * (base[u % RAWS] + sum(loads(ph, v) for v in range(u % RAWS, u + 1, RAWS)) + per[u % RAWS] * it)

        def last_in(ph, u, ring):
            return max(v for v in range(UNITS[ph][0]) if v % ring == u % ring)

        def slot_before(hf, ph, u, it, ring):
            if u >= ring:
                return hf, ph, u - ring, it
            if not (isinstance(it, int) and it == 0):
                return hf, ph, last_in(ph, u, ring), it - 1
            if ph == "out" or (hf, ph) == (0, "rkv"):
                return None
            stream = list(UNITS)
            before = stream[stream.index(ph) - 1]
            return hf - (ph == "rkv"), before, last_in(before, u, ring), UNITS[before][1] - 1

        def hi_done(hf, ph, u, it):
            if u >= SPLITS:
                return after(hf, ph, "act", f"s{u - SPLITS}", it)
            if not (isinstance(it, int) and it == 0):
                return after(hf, ph, "act", f"s{u + 2}", it - 1)
            where, name, last = {"rkv": ("norm", u, 0), "lora": ("rkv", u + 2, 2), "q": ("lora", u + 2, 0),
                                 "out": ("gate", u, 0), "up": ("out", u + 6, 0),
                                 "down0": ("up", u + 2, PJ // 2 - 1), "down1": ("down0", u + 9, 0)}[ph]
            if ph == "rkv" and hf:
                return after(hf - 1, "down1", "act", f"s{u + 9}")
            return after(hf, where, "act", f"s{name}", last)

        def split_hi(e, hf, ph, u, it, st, name):
            e.wait_ge(w_in_[u % RAWS], landed(hf, ph, u, it))
            used = slot_before(hf, ph, u, it, SPLITS)
            if used:
                e.wait_ge(pe_steps, after(used[0], used[1], "pe", f"u{used[2]}", used[3]))
            e.activation(whi[u % SPLITS][:], raw[u % RAWS][:], ACT.Copy).then_inc(act_steps, st.step(name))

        def split_lo(e, hf, ph, u, it):
            e.wait_ge(act_steps, hi_done(hf, ph, u, it))
            e.tensor_tensor(wlo[u % SPLITS][:], raw[u % RAWS][:], whi[u % SPLITS][:].bitcast(F32),
                            ALU.subtract).then_inc(pool_steps, halves[hf][ph]["pool"].step(f"u{u}"))

        block = ctx.enter_context(nc.Block())

        @block.sync
        def _(e):
            def load(hf, ph, u, it, src, dst=None):
                used = slot_before(hf, ph, u, it, RAWS)
                if used:
                    e.wait_ge(pool_steps, after(used[0], used[1], "pool", f"u{used[2]}", used[3]))
                slot = raw[u % RAWS][:] if dst is None else dst
                e.dma_start(slot, src).then_inc(w_in_[u % RAWS], 16)

            r3 = [raw[s][:].rearrange("p (k n) -> p k n", k=KT) for s in range(RAWS)]
            r2 = [raw[s][:].rearrange("p (k n) -> p k n", k=2) for s in range(RAWS)]
            xrow = a["x"].rearrange("(t p) d -> p t d", p=P)
            yrow = out.rearrange("(t p) d -> p t d", p=P)

            def x_tiles(hf):
                for i in range(NT):
                    e.dma_start(xr[:, i, :], xrow[:, hf * NT + i, :]).then_inc(x_in[i], 16)
                e.dma_start(gain[:], a["g_mix_pre"]).then_inc(gain_in, 16)

            def first_units(hf):
                for u in range(4):
                    load(hf, "rkv", u, 0, w1[:, :, ATT + P * u:ATT + P * u + P], r3[u])

            x_tiles(0)
            for dst, src in ((par, "par"), (cst, "cst")):
                e.dma_start(dst[:], a[src]).then_inc(const_in, 16)
            first_units(0)
            for hf in range(HALVES):
                for dst, src in ((spread, "spread"), (edge, "edge"), (table, "alibi" if hf else "first"),
                                 (chunks, "chunks"), (lora, "lora"), (wg2, "wg2")):
                    e.dma_start(dst[:], a[src]).then_inc(mix_in, 16)
                with e.Fori(1, 3) as g:
                    for u in range(4):
                        load(hf, "rkv", u, g, w1[:, :, bass.ds(g * 512 + (ATT + P * u), P)], r3[u])
                before = halves[hf - 1]["last"] if hf else halves[hf]["norm"]
                e.wait_ge(pe_steps, before["pe"].end())
                e.wait_ge(act_steps, before["act"].end())
                e.wait_ge(vec_steps, before["vec"].end())
                for dst, src in ((lnw, "ln_w"), (lnb, "ln_b")):
                    e.dma_start(dst[:], a[src]).then_inc(mix_in, 16)
                for u, c in enumerate((2304, 2432, 512, 640)):
                    load(hf, "lora", u, 0, w1[:, :, c:c + P], r3[u])
                for u in range(4):
                    load(hf, "q", u, 0, w1[:, :, HD * u:HD * u + HD], r3[u][:, :, 0:HD])
                    e.dma_start(r3[u][:, :, HD:P], w1[:, :, 256 + HD * u:320 + HD * u]).then_inc(w_in_[u], 16)
                e.wait_ge(act_steps, after(hf, "mix_end", "act", "Y"))
                e.wait_ge(vec_steps, after(hf, "mix_end", "vec", "Hb"))
                e.wait_ge(sems["pe"], halves[hf]["mix_end"]["pe"].end())
                e.dma_start(gain[:], a["g_mix_post"]).then_inc(gain_in, 16)
                for u in range(8):
                    if u == 6:
                        e.wait_ge(pe_steps, halves[hf]["gate"]["pe"].end())
                        e.wait_ge(act_steps, halves[hf]["gate"]["act"].end())
                        e.wait_ge(vec_steps, halves[hf]["gate"]["vec"].end())
                        e.wait_ge(pool_steps, halves[hf]["gate"]["pool"].end())
                        for i in range(NT):
                            e.dma_start(hres[:, i, :], xrow[:, hf * NT + i, :]).then_inc(h_in, 16)
                        e.dma_start(gain2[:], a["g_ffn_pre"]).then_inc(h_in, 16)
                    n, k = u // 4, 2 * (u % 4)
                    c = slice(512 * n, 512 * n + 512)
                    load(hf, "out", u, 0, wo.rearrange("(k p) n -> p k n", p=P)[:, k:k + 2, c], r2[u % RAWS])
                for u in range(4):
                    c = (u % 2) * FF + P * (u // 2)
                    load(hf, "up", u, 0, wu[:, :, c:c + P], r3[u])
                with e.Fori(1, PJ // 2) as g:
                    for u in range(4):
                        load(hf, "up", u, g, wu[:, :, bass.ds(g * 256 + ((u % 2) * FF + P * (u // 2)), P)], r3[u])
                for n in range(2):
                    for u in range(11):
                        if u == 5 and n == 0 and hf + 1 < HALVES:
                            e.wait_ge(vec_steps, halves[hf]["up"]["vec"].end())
                            e.wait_ge(act_steps, halves[hf]["up"]["act"].end())
                            x_tiles(hf + 1)
                        if u == 5 and n == 1:
                            e.wait_ge(vec_steps, halves[hf]["down0"]["vec"].end())
                            e.dma_start(gain[:], a["g_ffn_post"]).then_inc(gain_in, 16)
                        load(hf, f"down{n}", u, 0, wd[:, 2 * u:2 * u + 2, 512 * n:512 * n + 512], r2[u % RAWS])
                if hf + 1 < HALVES:
                    first_units(hf + 1)
                    e.wait_ge(pe_steps, halves[hf]["down1"]["pe"].end())
                for i in range(NT):
                    e.wait_ge(vec_steps, after(hf, "last", "vec", f"y{i}"))
                    e.dma_start(yrow[:, hf * NT + i, :], hres[:, i, :]).then_inc(y_out, 16)
            e.wait_ge(y_out, 16 * NT * HALVES)

        @block.tensor
        def _(e):
            e.wait_ge(const_in, 32)

            def turn(hf, ph, name, dst, pieces):
                for n, src in enumerate(pieces):
                    m = e.transpose(dst[:, P * n:P * n + P], src, ident)
                m.then_inc(pe_steps, halves[hf][ph]["pe"].step(name))

            def norm_tile(hf, ph, i, src):
                e.wait_ge(vec_steps, after(hf, ph, "vec", f"xs{i}"))
                for b in range(2):
                    if i >= 2:
                        e.wait_ge(vec_steps, after(hf, ph, "vec", f"lo{i - 2}_{b}"))
                    turn(hf, ph, f"tr{i}_{b}", bank[2 * (i % 2) + b], [src[:, i, P * k:P * k + P] for k in range(4 * b, 4 * b + 4)])

            def columns(hf, ph, u, it, dst):
                e.wait_ge(pool_steps, after(hf, ph, "pool", f"u{u}", it))
                hi = whi[u % SPLITS][:].rearrange("p (k n) -> p k n", k=KT)
                lo = wlo[u % SPLITS][:].rearrange("p (k n) -> p k n", k=KT)
                for k in range(KT):
                    e.matmul(dst[:], hi[:, k, :], xhi[:, k, :], start=k == 0, stop=False)
                    e.matmul(dst[:], hi[:, k, :], xlo[:, k, :], start=False, stop=False)
                    m = e.matmul(dst[:], lo[:, k, :], xhi[:, k, :], start=False, stop=k == KT - 1)
                m.then_inc(pe_steps, halves[hf][ph]["pe"].step(f"u{u}"))

            def rows(hf, ph, u, it, lhs_hi, lhs_lo, k0, banks, first_k, last_k):
                e.wait_ge(pool_steps, after(hf, ph, "pool", f"u{u}", it))
                hi = whi[u % SPLITS][:].rearrange("p (k n) -> p k n", k=2)
                lo = wlo[u % SPLITS][:].rearrange("p (k n) -> p k n", k=2)
                for kk_ in range(2):
                    k = k0 + kk_
                    for i in range(NT):
                        ts = slice(P * i, P * i + P)
                        e.matmul(banks[i][:], lhs_hi[:, k, ts], hi[:, kk_, :], start=k == first_k, stop=False)
                        e.matmul(banks[i][:], lhs_hi[:, k, ts], lo[:, kk_, :], start=False, stop=False)
                        m = e.matmul(banks[i][:], lhs_lo[:, k, ts], hi[:, kk_, :], start=False, stop=k == last_k)
                m.then_inc(pe_steps, halves[hf][ph]["pe"].step(f"u{u}"))

            def lora_tiles(hf):
                ph = "q"
                st = halves[hf][ph]["pe"]
                e.wait_ge(act_steps, after(hf, "lora", "act", "sq3"))
                for p in range(NP):
                    m = e.matmul(bank[6][0:8, :], ones8[:, p, :], sq[p][:], start=p == 0, stop=p == NP - 1)
                m.then_inc(pe_steps, st.step("ss"))
                for p in range(NP):
                    if p:
                        e.wait_ge(act_steps, after(hf, ph, "act", f"w_{p - 1}"))
                    ps = slice(P * p, P * p + P)
                    e.matmul(bank[4][:], lora[0:HD, ps], th[:], start=True, stop=True).then_inc(pe_steps, st.step(f"w{p}"))
                    if p:
                        e.wait_ge(act_steps, after(hf, ph, "act", f"a_{p - 1}"))
                    e.matmul(bank[5][:], lora[HD:P, ps], wa[HD:P, :], start=True, stop=True).then_inc(pe_steps, st.step(f"a{p}"))
                    if p == 0:
                        e.wait_ge(act_steps, after(hf, "lora", "act", "e3"))
                        turn(hf, ph, "vt", bank[7], [vT[:, P * i:P * i + P] for i in range(NT)])
                e.wait_ge(vec_steps, after(hf, ph, "vec", "rn"))
                for p in range(NP):
                    if p >= 2:
                        e.wait_ge(act_steps, after(hf, ph, "act", f"{'wa'[p - 2]}_3"))
                    e.matmul(norms[p][:], spread[:, p, :], rn[:, 2, :], start=True, stop=True).then_inc(pe_steps, st.step(f"bc{p}"))

            def mix_tile(hf, ph, t):
                st = halves[hf][ph]["pe"]
                done, last = tile_counts(hf, ph, t)

                def rows_of(e_):
                    return slice(HD * e_, HD * e_ + HD)

                def block(x, h):
                    return x[:, h % 2, h // 2, :]

                def settle():
                    e.nop(nofuse=True)

                def pair(x, h):
                    return x[rows_of(h % 2), P * (h // 2):P * (h // 2) + P]

                def products(name, odd, dst, left, right):
                    for n in range(4):
                        h = 2 * n + odd
                        m = e.matmul(dst[:, P * n:P * n + P], pair(left, h), pair(right, h), start=n == 0,
                                     stop=n == 3, skip_group_check=True)
                    m.then_inc(pe_steps, st.step(name))

                def scores(j):
                    if j >= 2:
                        e.wait_ge(vec_steps, done("vec", f"sb{j - 2}"))
                    b = bank[6 + j % 2]
                    for n in range(2):
                        m = e.matmul(b[:, WIN * n:WIN * n + WIN], qs[rows_of(j % 2), 2 * (j // 2) + n, :],
                                     kw[rows_of(j % 2), :], start=n == 0, stop=n == 1,
                                     skip_group_check=True)
                    m.then_inc(pe_steps, st.step(f"sc{j}"))

                def parity_products(name, odd, dst, left, right):
                    for n in range(NP):
                        m = e.matmul(dst[:, P * n:P * n + P], left[:, odd, n, :], right[:, odd, n, :],
                                     start=n == 0, stop=n == 3, skip_group_check=True)
                    m.then_inc(pe_steps, st.step(name))

                def Y(lv):
                    for odd in range(2):
                        e.wait_ge(vec_steps, done("vec", f"TT{lv - 1}_{odd}"))
                        parity_products(f"Y{lv}_{odd}", odd, bank[2 + odd], G, Tt)

                def TT(lv):
                    for odd in range(2):
                        e.wait_ge(vec_steps, done("vec", f"Y{lv}_{odd}"))
                        e.wait_ge(act_steps, done("act", f"T{lv - 1}_{odd}"))
                        parity_products(f"TT{lv}_{odd}", odd, bank[4 + odd], Tb, Yb)

                def T(lv):
                    for odd in range(2):
                        e.wait_ge(vec_steps, done("vec", f"TT{lv}_{odd}"))
                        turn(hf, ph, f"T{lv}_{odd}", bank[4 + odd], [Tt[:, odd, n, :] for n in range(NP)])

                def probs(n):
                    e.wait_ge(act_steps, done("act", f"ex{2 * n + 1}"))
                    if n == 0 and ph != "mix_first":
                        e.wait_ge(act_steps, done("act", "gb"))
                    if n < 2:
                        e.wait_ge(vec_steps, done("vec", f"sb{n + 2}"))
                    else:
                        e.wait_ge(act_steps, done("act", f"PT{n - 2}"))
                    turn(hf, ph, f"PT{n}", bank[6 + n % 2],
                         [pr[:, 2 * n + i // 2, P * (i % 2):P * (i % 2) + P] for i in range(4)])

                e.wait_ge(vec_steps, last("vec", "Hb"))
                products("G0", 0, bank[2], AN, BT)
                e.wait_ge(act_steps, last("act", "Ub1"))
                products("G1", 1, bank[3], AN, BT)
                turn(hf, ph, "trA", bank[0], [AN[:, P * p:P * p + P] for p in range(NP)])
                e.wait_ge(act_steps, last("act", "Y"))
                turn(hf, ph, "trV", bank[1], [Vst[:, P * p:P * p + P] for p in range(NP)])
                for odd in range(2):
                    e.wait_ge(vec_steps, done("vec", f"G{odd}"))
                    turn(hf, ph, f"Y1_{odd}", bank[4 + odd], [G[:, odd, n, :] for n in range(NP)])
                scores(0)
                scores(1)
                e.wait_ge(pool_steps, last("pool", "BP"))
                e.wait_ge(act_steps, done("act", "trA"))
                turn(hf, ph, "trK", bank[0], [KP[:, P * p:P * p + P] for p in range(NP)])
                e.wait_ge(act_steps, done("act", "trV"))
                products("MKA0", 0, bank[1], KTl, AN)
                T(1)
                Y(2)
                scores(2)
                TT(2)
                scores(3)
                e.wait_ge(act_steps, done("act", "trK"))
                products("MKA1", 1, bank[0], KTl, AN)
                T(2)
                Y(3)
                e.wait_ge(vec_steps, done("vec", "MKA0"))
                products("MRB0", 0, bank[1], BT, RT)
                TT(3)
                e.wait_ge(vec_steps, done("vec", "MKA1"))
                turn(hf, ph, "trB", bank[0], [BP[:, P * p:P * p + P] for p in range(NP)])
                if ph != "mix_first":
                    e.wait_ge(vec_steps, done("vec", "sb2"))
                    e.wait_ge(act_steps, done("act", "gt"))
                    e.matmul(bank[6][:], gt[:], wg2[:], start=True, stop=True).then_inc(pe_steps, st.step("gp"))
                T(3)
                Y(4)
                e.wait_ge(act_steps, done("act", "trB"))
                products("MRB1", 1, bank[0], BT, RT)
                TT(4)
                probs(0)
                T(4)
                Y(5)
                e.wait_ge(vec_steps, done("vec", "MRB0"))
                products("MRK0", 0, bank[1], KTl, RT)
                TT(5)
                probs(1)
                e.wait_ge(vec_steps, done("vec", "MRB1"))
                products("MRK1", 1, bank[0], KTl, RT)
                T(5)
                Y(6)
                e.wait_ge(vec_steps, done("vec", "MRK0"))
                for h in range(HEADS):
                    m = e.matmul(bank[1][:, CH * h:CH * h + CH], block(MKA, h), Vt[:, CH * h:CH * h + CH],
                                 start=h == 0, stop=h == HEADS - 1, skip_group_check=True)
                m.then_inc(pe_steps, st.step("X1"))
                TT(6)
                probs(2)
                probs(3)
                e.wait_ge(act_steps, done("act", "X1"))
                e.wait_ge(vec_steps, done("vec", "TT6_1"))
                for h in range(HEADS):
                    m = e.matmul(ub[h % 2][:, CH * (h // 2):CH * (h // 2) + CH], block(Tt, h),
                                 X1[:, CH * h:CH * h + CH], start=h < 2, stop=False, skip_group_check=True)
                m.then_inc(pe_steps, st.step("Z"))
                for h in range(HEADS):
                    m = e.matmul(bank[5][rows_of(h % 2), P * (h // 2):P * (h // 2) + P],
                                 At[:, CH * h:CH * h + CH], block(Tt, h), start=h < 2, stop=h >= 6,
                                 skip_group_check=True)
                m.then_inc(pe_steps, st.step("TAT"))
                def values(heads):
                    for h in heads:
                        for n in range(2):
                            m = e.matmul(bank[6][:, CH * h:CH * h + CH], pT[:, h, n, :],
                                         vA[:, bass.ds(t + n, 1), HD * (h // 4):HD * (h // 4) + HD].rearrange("p a d -> p (a d)"),
                                         start=h == 0 and n == 0, stop=h == HEADS - 1 and n == 1,
                                         skip_group_check=True)
                    return m

                e.wait_ge(act_steps, done("act", "PT3"))
                values(range(4))
                e.wait_ge(pool_steps, done("pool", "RK"))
                for p in range(NP):
                    m = e.matmul(bank[7][:, 2 * p:2 * p + 2], RKp[:, P * p:P * p + P],
                                 par[:, RK + 2 * p:RK + 2 * p + 2], start=p == 0, stop=p == 3,
                                 skip_group_check=True)
                m.then_inc(pe_steps, st.step("bonus"))

                def chunk(c):
                    cs, nm = rows_of(c), "ab"[c]
                    state = H[c]
                    hps = bank[5] if c == 0 else bank[2]
                    if c == 0:
                        e.wait_ge(act_steps, done("act", "TAT"))
                    else:
                        e.wait_ge(vec_steps, done("vec", "Ha"))
                    settle()
                    for h in range(HEADS):
                        m = e.matmul(ub[h % 2][cs, CH * (h // 2):CH * (h // 2) + CH],
                                     TAT[rows_of(h % 2), P * (h // 2) + CH * c:P * (h // 2) + CH * c + CH],
                                     state[rows_of(h % 2), h // 2, :], start=False, stop=h == 7,
                                     skip_group_check=True)
                    m.then_inc(pe_steps, st.step("UA" + nm))
                    for h in range(HEADS):
                        m = e.matmul(hps[rows_of(h % 2), HD * (h // 2):HD * (h // 2) + HD],
                                     Kt[cs, HD * h:HD * h + HD], Vt[cs, HD * h:HD * h + HD],
                                     start=h < 2, stop=False, skip_group_check=True)
                    m.then_inc(pe_steps, st.step("HV" + nm))
                    if c == 0:
                        e.wait_ge(vec_steps, done("vec", "MRK1"))
                        for h in range(HEADS):
                            e.matmul(yb[h % 2][:, CH * (h // 2):CH * (h // 2) + CH], block(MRK, h),
                                     Vt[:, CH * h:CH * h + CH], start=h < 2, stop=False, skip_group_check=True)
                    for h in range(HEADS):
                        m = e.matmul(yb[h % 2][cs, CH * (h // 2):CH * (h // 2) + CH],
                                     RT[rows_of(h % 2), P * (h // 2) + CH * c:P * (h // 2) + CH * c + CH],
                                     state[rows_of(h % 2), h // 2, :], start=False, stop=False,
                                     skip_group_check=True)
                    m.then_inc(pe_steps, st.step("RH" + nm))
                    e.wait_ge(act_steps, done("act", "U" + nm + "1"))
                    settle()
                    for h in range(HEADS):
                        m = e.matmul(hps[rows_of(h % 2), HD * (h // 2):HD * (h // 2) + HD],
                                     Bt[cs, HD * h:HD * h + HD], U[cs, HD * h:HD * h + HD],
                                     start=False, stop=h >= 6, skip_group_check=True)
                    m.then_inc(pe_steps, st.step("HB" + nm))

                chunk(0)
                values(range(4, HEADS)).then_inc(pe_steps, st.step("PV"))
                chunk(1)
                for h in range(HEADS):
                    m = e.matmul(yb[h % 2][:, CH * (h // 2):CH * (h // 2) + CH], block(MRB, h),
                                 U[:, CH * h:CH * h + CH], start=False, stop=h >= 6, skip_group_check=True)
                m.then_inc(pe_steps, st.step("YU"))

            for hf in range(HALVES):
                if hf == 0:
                    begin(e, hf, "norm", "pe")
                    for i in range(NT):
                        norm_tile(hf, "norm", i, xr)
                    e.wait_ge(vec_steps, after(hf, "norm", "vec", "lo3_1"))
                else:
                    e.wait_ge(vec_steps, after(hf - 1, "down0", "vec", "lo3_1"))
                with e.Fori(0, 3) as g:
                    for u in range(4):
                        if u < 4:
                            e.wait_ge(act_steps, after(hf, "rkv", "act", f"e{u}", g - 1))
                        columns(hf, "rkv", u, g, bank[u])
                e.wait_ge(mix_in, 128 * (hf + 1))
                for u in range(4):
                    e.wait_ge(act_steps, after(hf, "rkv", "act", f"e{u}", 2))
                    columns(hf, "lora", u, 0, bank[u])
                lora_tiles(hf)
                for u in range(4):
                    e.wait_ge(act_steps, after(hf, "lora", "act", f"e{u}"))
                    columns(hf, "q", u, 0, bank[u])
                begin(e, hf, "mix_first", "pe")
                mix_tile(hf, "mix_first", 0)
                with e.Fori(1, NT - 1) as t:
                    mix_tile(hf, "mix", t)
                mix_tile(hf, "mix_end", NT - 1)
                begin(e, hf, "gate", "pe")

                st = halves[hf]["gate"]["pe"]
                e.matmul(bank[7][:], sg[:, P * (NT - 1):P * NT], wg2[:], start=True, stop=True).then_inc(pe_steps, st.step("gp"))
                for n, name in enumerate(TURNS):
                    i = n % NT
                    if n >= NT:
                        e.wait_ge(vec_steps, after(hf, "gate", "vec", f"lo_a{i}"))
                    if name == "y3":
                        e.wait_ge(pool_steps, after(hf, "gate", "pool", "gg"))
                    turn(hf, "gate", f"tr_{name}", bank[i], [(rows_y if n >= NT else rows_a)[:, i, P * k:P * k + P] for k in range(4)])
                begin(e, hf, "out", "pe")
                for u in range(8):
                    n = u // 4
                    rows(hf, "out", u, 0, xhi, xlo, 2 * (u % 4), bank[4 * n:4 * n + 4], 0, KT - 1)
                for i in range(NT):
                    norm_tile(hf, "post", i, xn)
                begin(e, hf, "up", "pe")
                with e.Fori(0, PJ // 2) as g:
                    for u in range(4):
                        e.wait_ge(act_steps, after(hf, "up", "act", f"e{'gv'[u % 2]}{u // 2}", g - 1))
                        columns(hf, "up", u, g, bank[u])
                e.wait_ge(vec_steps, after(hf, "up", "vec", "lo1", PJ // 2 - 2))
                for n in range(2):
                    if n:
                        e.wait_ge(act_steps, after(hf, "down0", "act", "f1"))
                        e.wait_ge(vec_steps, after(hf, "down0", "vec", "f3"))
                    for u in range(11):
                        if u == 10 and n == 0:
                            e.wait_ge(vec_steps, after(hf, "up", "vec", "lo1", PJ // 2 - 1))
                        if n == 0 and hf + 1 < HALVES and 5 <= u < 9:
                            norm_tile(hf, "down0", u - 5, xr)
                        rows(hf, f"down{n}", u, 0, ghi, glo, 2 * u, bank[4:8], 0, PJ - 1)

        @block.scalar
        def _(e):

            def square(hf, ph, i, src, junk=jk):
                if i:
                    e.wait_ge(act_steps, after(hf, ph, "act", f"sq{i - 1}"))
                e.activation(junk[:], src[:, i, :], ACT.Square, accum_out=small[:, i:i + 1]).then_inc(act_steps, halves[hf][ph]["act"].step(f"sq{i}"))

            def root(hf, ph):
                e.wait_ge(vec_steps, after(hf, ph, "vec", "ms"))
                e.activation(small[:, 8:12], small[:, 4:8], ACT.Sqrt).then_inc(act_steps, halves[hf][ph]["act"].step("root"))

            def columns_hi(hf, ph, i):
                for b in range(2):
                    e.wait_ge(pe_steps, after(hf, ph, "pe", f"tr{i}_{b}"))
                    e.activation(xhi[:, 4 * b:4 * b + 4, P * i:P * i + P],
                                 bank[2 * (i % 2) + b][:].rearrange("p (k n) -> p k n", k=4), ACT.Copy).then_inc(act_steps, halves[hf][ph]["act"].step(f"hi{i}_{b}"))

            def ready(hf, ph, t, between=None):
                st = halves[hf][ph]["act"]
                before, shifted = (gyn, gsq) if ph == "prep" else (Lp, Ep)

                def tile(x):
                    return x[:, bass.ds(t, 1), :].rearrange("p a d -> p (a d)")

                it = tile_pass(ph, t - 1)
                if ph != "prep":
                    e.wait_ge(vec_steps, after(hf, ph, "vec", "wend", it))
                    e.wait_ge(pool_steps, tile_counts(hf, ph, t - 1)[1]("pool", "BP"))
                e.activation(E[:], tile(L), ACT.Exp, scale=-DECAY).then_inc(act_steps, st.step("E"))
                e.activation(Ei[:], tile(L), ACT.Exp, scale=DECAY).then_inc(act_steps, st.step("Ei"))
                e.wait_ge(vec_steps, after(hf, ph, "vec", "Lp", it))
                e.activation(shifted[:], before[:], ACT.Exp, scale=-DECAY).then_inc(act_steps, st.step("Ep"))
                if between:
                    between()
                    e.wait_ge(act_steps, after(hf, "prep", "act", "e3"))
                e.activation(qs[:], tile(qT).rearrange("p (j n) -> p j n", j=NP), ACT.Copy, scale=HD ** -0.5).then_inc(act_steps, st.step("qs"))
                e.activation(kw[:], kT[:, bass.ds(t * P + CH, WIN)], ACT.Copy).then_inc(act_steps, st.step("kw"))

            def mix_tile(hf, ph, t):
                st = halves[hf][ph]["act"]
                done, last = tile_counts(hf, ph, t)

                def act(name, dst, src, fn=ACT.Copy, **kw):
                    e.activation(dst, src, fn, **kw).then_inc(act_steps, st.step(name))

                def tile(x):
                    return x[:, bass.ds(t, 1), :].rearrange("p a d -> p (a d)")

                def parity(x, odd):
                    return x.rearrange("p (a b n) -> p b a n", b=2, n=CH)[:, odd]

                def parity_bank(x):
                    return x[:, 0:4 * CH].rearrange("p (a n) -> p a n", a=4)

                def out_of(name, dst, b, pe_name):
                    e.wait_ge(pe_steps, done("pe", pe_name))
                    act(name, dst, b)

                def T(lv):
                    for odd in range(2):
                        out_of(f"T{lv}_{odd}", Tb[:, odd], bank[4 + odd][:].rearrange("p (a n) -> p a n", a=NP), f"T{lv}_{odd}")

                def ex(h):
                    act(f"ex{h}", pr[:, h, CH:2 * P], scb[:, h, :], ACT.Exp, bias=den8[:, 1, h:h + 1],
                        accum_out=den8[:, 3, h:h + 1])

                def pt(n):
                    out_of(f"PT{n}", pT[:, 2 * n:2 * n + 2, :, :],
                           bank[6 + n % 2][:].rearrange("p (a b c) -> p a b c", a=2, b=2), f"PT{n}")

                e.wait_ge(pool_steps, last("pool", "BV"))
                out_of("trA", At[:], bank[0][:], "trA")
                out_of("trV", Vt[:], bank[1][:], "trV")
                out_of("trK", Kt[:], bank[0][:], "trK")
                if ph != "mix_first":
                    act("gt", gt[:], sg[:, bass.ds((t - 1) * P, P)])
                T(1)
                T(2)
                e.wait_ge(vec_steps, done("vec", "nm"))
                for h in range(4):
                    ex(h)
                out_of("trB", Bt[:], bank[0][:], "trB")
                if ph != "mix_first":
                    e.wait_ge(vec_steps, done("vec", "gyc"))
                    act("gsq", gsq[:], gyn[:], ACT.Square)
                T(3)
                if ph != "mix_first":
                    out_of("gb", gb[:], bank[6][:], "gp")
                for h in range(4, 8):
                    ex(h)
                e.wait_ge(vec_steps, done("vec", "sd"))
                act("esink", den8[:, 4, :], den8[:, 2, :], ACT.Exp)
                pt(0)
                T(4)
                if ph != "mix_first":
                    e.wait_ge(vec_steps, done("vec", "gvar"))
                    act("groot", den8[:, 7, :], den8[:, 6, :], ACT.Sqrt)
                pt(1)
                T(5)
                out_of("X1", X1[:], bank[1][:], "X1")
                pt(2)
                pt(3)
                out_of("TAT", TAT[:], bank[5][:], "TAT")
                for c in range(2):
                    cs, nm = slice(CH * c, CH * c + CH), "ab"[c]
                    for odd in range(2):
                        out_of(f"U{nm}{odd}", parity(U[cs, :], odd), parity_bank(ub[odd][cs, :]), "UA" + nm)
                    if c == 0 and ph != "mix_end":
                        ready(hf, ph, t + 1)
                e.wait_ge(pe_steps, done("pe", "YU"))
                for odd, nm in enumerate(("Y0", "Y")):
                    act(nm, parity(tile(rows_y), odd), parity_bank(yb[odd]))

            for hf in range(HALVES):
                if hf == 0:
                    begin(e, hf, "norm", "act")
                    for i in range(NT):
                        e.wait_ge(x_in[i], 16)
                        square(hf, "norm", i, xr)
                    root(hf, "norm")
                    for i in range(NT):
                        columns_hi(hf, "norm", i)
                    for u in range(2):
                        split_hi(e, hf, "rkv", u, 0, halves[hf]["norm"]["act"], f"s{u}")
                    e.wait_ge(const_in, 32)
                st = halves[hf]["rkv"]["act"]

                def project(g, last):
                    for n in range(4):
                        if n < 2:
                            split_hi(e, hf, "rkv", n + 2, g, st, f"s{n}")
                        elif last:
                            split_hi(e, hf, "lora", n - 2, 0, st, f"s{n}")
                        else:
                            split_hi(e, hf, "rkv", n - 2, g + 1, st, f"s{n}")
                        if hf and n == 0:
                            e.wait_ge(y_out, 16 * NT * hf)
                        e.wait_ge(pe_steps, after(hf, "rkv", "pe", f"u{n}", g))
                        e.wait_ge(vec_steps, after(hf, "rkv", "vec", f"c{n - 2}" if n >= 2 else f"c{n + 2}", g if n >= 2 else g - 1))
                        e.activation(shr[n % 2][:, 1:1 + HALF], bank[n][:], ACT.Copy).then_inc(act_steps, st.step(f"e{n}"))

                with e.Fori(0, 2) as g:
                    project(g, False)
                project(2, True)
                st = halves[hf]["lora"]["act"]
                dst = [shr[0][:, 1:1 + HALF], shr[1][:, 1:1 + HALF], kT[:, P:P + HALF], vT[:]]

                def squares(p):
                    k_p = rkv[:, 1, :, P * p:P * p + P]
                    e.activation(sq[p][:].rearrange("p (t n) -> p t n", t=NT), k_p, ACT.Square,
                                 scale=par[:, KK_ + p:KK_ + p + 1]).then_inc(act_steps, st.step(f"sq{p}"))

                for n in range(4):
                    if n < 2:
                        split_hi(e, hf, "lora", n + 2, 0, st, f"s{n}")
                        e.wait_ge(vec_steps, after(hf, "rkv", "vec", f"c{n + 2}", 2))
                    else:
                        split_hi(e, hf, "q", n - 2, 0, st, f"s{n}")
                    if n == 3:
                        squares(3)
                    e.wait_ge(pe_steps, after(hf, "lora", "pe", f"u{n}"))
                    e.activation(dst[n], bank[n][:], ACT.Copy).then_inc(act_steps, st.step(f"e{n}"))
                    if n == 2:
                        e.wait_ge(vec_steps, after(hf, "lora", "vec", "s0"))
                        e.activation(th[:], wa[0:HD, :], ACT.Tanh).then_inc(act_steps, st.step("th"))
                    if n < 3:
                        squares(n)
                e.wait_ge(vec_steps, after(hf, "lora", "vec", "s1"))
                e.activation(sg[:], gd[:], ACT.Sigmoid).then_inc(act_steps, st.step("sg"))
                st = halves[hf]["q"]["act"]
                e.wait_ge(pe_steps, after(hf, "q", "pe", "ss"))
                e.activation(rn[:, 0, :], bank[6][0:8, :], ACT.Sqrt).then_inc(act_steps, st.step("root"))
                for p in range(NP):
                    for nm, dst_, off, b in (("w", sig, W0, 4), ("a", av, A0, 5)):
                        e.wait_ge(pe_steps, after(hf, "q", "pe", f"{nm}{p}"))
                        e.activation(dst_[:, :, P * p:P * p + P],
                                     bank[b][:].rearrange("p (t n) -> p t n", t=NT), ACT.Sigmoid,
                                     bias=par[:, off + p:off + p + 1]).then_inc(act_steps, st.step(f"{nm}_{p}"))
                    if p == 0:
                        e.wait_ge(pe_steps, after(hf, "q", "pe", "vt"))
                        e.activation(vA[:, 1:1 + NT, :], bank[7][:].rearrange("p (t n) -> p t n", t=NT), ACT.Copy).then_inc(act_steps, st.step("vt"))

                def queries(n, st):
                    e.wait_ge(pe_steps, after(hf, "q", "pe", f"u{n}"))
                    e.activation(qT[:, :, P * n:P * n + P], bank[n][:].rearrange("p (t n) -> p t n", t=NT), ACT.Copy).then_inc(act_steps, st.step(f"e{n}"))

                for n in range(2):
                    split_hi(e, hf, "q", 2 + n, 0, st, f"s{n}")
                    queries(n, st)
                e.wait_ge(vec_steps, after(hf, "q", "vec", "scan0"))

                def last_queries():
                    for n in (2, 3):
                        queries(n, halves[hf]["prep"]["act"])

                ready(hf, "prep", 0, last_queries)
                begin(e, hf, "mix_first", "act")
                mix_tile(hf, "mix_first", 0)
                with e.Fori(1, NT - 1) as t:
                    mix_tile(hf, "mix", t)
                mix_tile(hf, "mix_end", NT - 1)
                begin(e, hf, "gate", "act")
                st = halves[hf]["gate"]["act"]

                def hi(name):
                    n = TURNS.index(name)
                    b, i = n // NT, n % NT
                    e.wait_ge(pe_steps, after(hf, "gate", "pe", f"tr_{name}"))
                    e.activation(xhi[:, 4 * b:4 * b + 4, P * i:P * i + P],
                                 bank[i][:].rearrange("p (k n) -> p k n", k=4), ACT.Copy).then_inc(act_steps, st.step(f"hi_{name}"))

                e.wait_ge(pe_steps, after(hf, "gate", "pe", "gp"))
                e.activation(gb[:], bank[7][:], ACT.Copy).then_inc(act_steps, st.step("gb"))
                hi("a0")
                e.wait_ge(vec_steps, after(hf, "gate", "vec", "gyc"))
                e.activation(gsq[:], gyn[:], ACT.Square).then_inc(act_steps, st.step("gsq"))
                hi("a1")
                for u in range(2):
                    split_hi(e, hf, "out", u, 0, st, f"s{u}")
                e.wait_ge(vec_steps, after(hf, "gate", "vec", "gvar"))
                e.activation(den8[:, 7, :], den8[:, 6, :], ACT.Sqrt).then_inc(act_steps, st.step("groot"))
                for name in TURNS[2:]:
                    hi(name)
                st = halves[hf]["out"]["act"]
                for u in range(8):
                    if u == 5:
                        e.wait_ge(pe_steps, after(hf, "out", "pe", "u3"))
                        for i in range(NT):
                            if i:
                                e.wait_ge(act_steps, after(hf, "out", "act", f"qa{i - 1}"))
                            e.activation(pj[:, 0:512], bank[i][:], ACT.Square, accum_out=small[:, 16 + i:17 + i]).then_inc(act_steps, st.step(f"qa{i}"))
                    if u < 6:
                        split_hi(e, hf, "out", u + 2, 0, st, f"s{u}")
                    else:
                        split_hi(e, hf, "up", u - 6, 0, st, f"s{u}")
                begin(e, hf, "post", "act")
                st = halves[hf]["post"]["act"]
                for i in range(NT):
                    if i:
                        e.wait_ge(act_steps, after(hf, "post", "act", f"qb{i - 1}"))
                    e.activation(pj[:, 0:512], bank[4 + i][:], ACT.Square, accum_out=small[:, 20 + i:21 + i]).then_inc(act_steps, st.step(f"qb{i}"))
                e.wait_ge(vec_steps, after(hf, "post", "vec", "pms"))
                e.activation(small[:, 28:32], small[:, 24:28], ACT.Sqrt).then_inc(act_steps, st.step("proot"))
                for i in range(NT):
                    if i == 1:
                        e.wait_ge(pool_steps, after(hf, "post", "pool", "h1"))
                    else:
                        e.wait_ge(vec_steps, after(hf, "post", "vec", f"h{i}"))
                    e.wait_ge(act_steps, after(hf, "post", "act", f"sq{i - 1}" if i else "qb3"))
                    e.activation(pj[:], hres[:, i, :], ACT.Square, accum_out=small[:, i:i + 1]).then_inc(act_steps, st.step(f"sq{i}"))
                    e.wait_ge(vec_steps, after(hf, "post", "vec", f"ms{i}"))
                    e.activation(small[:, 8 + i:9 + i], small[:, 4 + i:5 + i], ACT.Sqrt).then_inc(act_steps, st.step(f"root{i}"))
                    if i == 1:
                        columns_hi(hf, "post", 0)
                for i in range(1, NT):
                    columns_hi(hf, "post", i)
                begin(e, hf, "up", "act")
                st = halves[hf]["up"]["act"]

                def hidden(g, last):
                    for u in range(4):
                        n, m, k = u // 2, u % 2, "gv"[u % 2]
                        if u < 2:
                            split_hi(e, hf, "up", u + 2, g, st, f"s{u}")
                        elif last:
                            split_hi(e, hf, "down0", u - 2, 0, st, f"s{u}")
                        else:
                            split_hi(e, hf, "up", u - 2, g + 1, st, f"s{u}")
                        e.wait_ge(pe_steps, after(hf, "up", "pe", f"u{u}", g))
                        e.wait_ge(vec_steps, after(hf, "up", "vec", f"k{k}{n}", g - 1))
                        e.activation(cr[n][m][:, 2:2 + HALF], bank[u][:], ACT.Copy).then_inc(act_steps, st.step(f"e{k}{n}"))
                        if m:
                            e.wait_ge(vec_steps, after(hf, "up", "vec", f"0g{n}", g))
                            e.wait_ge(vec_steps, after(hf, "up", "vec", f"m{1 - n}", g if n else g - 1))
                            e.activation(gl[:], cc[n][0][:], ACT.Gelu_apprx_tanh).then_inc(act_steps, st.step(f"ge{n}"))

                with e.Fori(0, PJ // 2 - 1) as g:
                    hidden(g, False)
                hidden(PJ // 2 - 1, True)
                for n in range(2):
                    ph = f"down{n}"
                    st = halves[hf][ph]["act"]
                    for u in range(11):
                        if u < 9:
                            split_hi(e, hf, ph, u + 2, 0, st, f"s{u}")
                        elif n == 0:
                            split_hi(e, hf, "down1", u - 9, 0, st, f"s{u}")
                        elif hf + 1 < HALVES:
                            split_hi(e, hf + 1, "rkv", u - 9, 0, st, f"s{u}")
                        if n == 0 and hf + 1 < HALVES:
                            if u in (2, 3):
                                for i in range(NT):
                                    e.wait_ge(x_in[i], 16 * (hf + 2))
                                e.wait_ge(pe_steps, halves[hf]["up"]["pe"].end())
                                square(hf, ph, 2 * u - 4, xr)
                                square(hf, ph, 2 * u - 3, xr)
                            elif u == NT:
                                root(hf, ph)
                            elif 0 <= u - NT - 1 < NT:
                                columns_hi(hf, ph, u - NT - 1)
                    e.wait_ge(pe_steps, after(hf, ph, "pe", "u10"))
                    for i in range(2):
                        e.activation(fo[:, i, 512 * n:512 * n + 512], bank[4 + i][:], ACT.Copy).then_inc(act_steps, st.step(f"f{i}"))
                begin(e, hf, "last", "act")
                for i in range(NT):
                    square(hf, "last", i, fo, fj)
                root(hf, "last")

        @block.vector
        def _(e):
            for n, cell in enumerate((shcar[:], cvcar[:], vA[:, 0, :], H[0][:])):
                e.memset(cell, 0.0).then_inc(sems["vec"], 1)

            def rstd(v, hf, ph):
                e.wait_ge(act_steps, after(hf, ph, "act", "sq3"))
                e.tensor_scalar(small[:, 4:8], small[:, 0:4], 1.0 / D, EPS, ALU.mult, ALU.add).then_inc(vec_steps, v.step("ms"))
                e.wait_ge(act_steps, after(hf, ph, "act", "root"))
                e.reciprocal(small[:, 12:16], small[:, 8:12]).then_inc(vec_steps, v.step("rstd"))
                e.wait_ge(vec_steps, v.after("rstd"))

            def columns_lo(v, hf, ph, i):
                for b in range(2):
                    e.wait_ge(act_steps, after(hf, ph, "act", f"hi{i}_{b}"))
                    cols = (slice(None), slice(4 * b, 4 * b + 4), slice(P * i, P * i + P))
                    e.tensor_tensor(xlo[cols], bank[2 * (i % 2) + b][:].rearrange("p (k n) -> p k n", k=4), xhi[cols].bitcast(F32), ALU.subtract).then_inc(vec_steps, v.step(f"lo{i}_{b}"))

            def norm(v, hf, ph, src, dst, gains):
                rstd(v, hf, ph)
                e.wait_ge(gain_in, 16 * gains)

                def scaled(i):
                    e.scalar_tensor_tensor(dst[:, i, :], src[:, i, :], small[:, 12 + i:13 + i], gain[:], ALU.mult, ALU.mult).then_inc(vec_steps, v.step(f"xs{i}"))

                scaled(0)
                for i in range(NT):
                    if i + 1 < NT:
                        scaled(i + 1)
                    columns_lo(v, hf, ph, i)

            def shift_tile(v, n, copied, mu, car, dst, four=True):
                s = shr[n % 2]
                e.tensor_copy(s[:, 0:1], car).then_inc(vec_steps, v.step(f"b{n}"))
                e.wait_ge(act_steps, copied)
                e.wait_ge(vec_steps, v.after(f"b{n}"))
                e.tensor_tensor(shd[:], s[:, 0:HALF], s[:, 1:1 + HALF], ALU.subtract).then_inc(vec_steps, v.step(f"d{n}"))
                e.wait_ge(vec_steps, v.after(f"d{n}"))
                x, y = shd[:], s[:, 1:1 + HALF]
                if four:
                    x, y = (z.rearrange("p (t n) -> p t n", t=NT) for z in (x, y))
                e.scalar_tensor_tensor(dst, x, mu, y, ALU.mult, ALU.add).then_inc(vec_steps, v.step(f"s{n}"))
                e.tensor_copy(car, s[:, HALF:HALF + 1]).then_inc(vec_steps, v.step(f"c{n}"))

            def ready(hf, ph, t, part=2):
                v = Pass(hf, ph, tile_pass(ph, t - 1))
                before, shifted = (gyn, gsq) if ph == "prep" else (Lp, Ep)

                def tile(x):
                    return x[:, bass.ds(t, 1), :].rearrange("p a d -> p (a d)")

                if part != 1:
                    e.tensor_tensor(before[:], tile(L), tile(sig), ALU.subtract).then_inc(vec_steps, v.step("Lp"))
                if part != 0:
                    e.wait_ge(act_steps, after(hf, ph, "act", "Ep", v.it))
                    e.scalar_tensor_tensor(AN[:], tile(kk), -1.0, shifted[:], ALU.mult, ALU.mult).then_inc(vec_steps, v.step("AN"))
                    e.tensor_tensor(BT[:], tile(av), Ei[:], ALU.mult).then_inc(vec_steps, v.step("BT"))
                    e.tensor_tensor(KTl[:], tile(rkv[:, 1]), Ei[:], ALU.mult).then_inc(vec_steps, v.step("KT"))
                    e.tensor_copy(Vst[:], tile(rkv[:, 2])).then_inc(vec_steps, v.step("Vst"))

            def centre(v, t):
                rows = rows_y[:, bass.ds(t, 1), :].rearrange("p a (h n) -> p (a h) n", h=HEADS)
                e.tensor_reduce(den8[:, 8, :], rows, AX, ALU.add).then_inc(vec_steps, v.step("gsum"))
                e.wait_ge(vec_steps, v.after("gsum"))
                e.tensor_scalar(den8[:, 8, :], den8[:, 8, :], 1.0 / HD, None, ALU.mult).then_inc(vec_steps, v.step("gmean"))
                e.wait_ge(vec_steps, v.after("gmean"))
                e.tensor_tensor(gyn[:].rearrange("p (h n) -> p h n", h=HEADS), rows,
                                den8[:, 8, :].unsqueeze(2).to_broadcast([P, HEADS, HD]), ALU.subtract).then_inc(vec_steps, v.step("gyc"))

            def variance(v, squared):
                e.wait_ge(act_steps, squared)
                e.tensor_reduce(den8[:, 6, :], gsq[:].rearrange("p (h n) -> p h n", h=HEADS), AX, ALU.add).then_inc(vec_steps, v.step("gssq"))
                e.wait_ge(vec_steps, v.after("gssq"))
                e.tensor_scalar(den8[:, 6, :], den8[:, 6, :], 1.0 / HD, GN_EPS, ALU.mult, ALU.add).then_inc(vec_steps, v.step("gvar"))

            def scale(v, root):
                e.wait_ge(act_steps, root)
                e.reciprocal(den8[:, 8, :], den8[:, 7, :]).then_inc(vec_steps, v.step("grstd"))
                e.wait_ge(vec_steps, v.after("grstd"))
                g8 = gyn[:].rearrange("p (h n) -> p h n", h=HEADS)
                e.tensor_tensor(g8, g8, den8[:, 8, :].unsqueeze(2).to_broadcast([P, HEADS, HD]), ALU.mult).then_inc(vec_steps, v.step("gyn"))

            def mix_tile(hf, ph, t):
                v = Pass(hf, ph, tile_pass(ph, t))
                done, last = tile_counts(hf, ph, t)

                def tile(x):
                    return x[:, bass.ds(t, 1), :].rearrange("p a d -> p (a d)")

                def four(x):
                    return x.rearrange("p (h n) -> p h n", h=4)

                def over(x):
                    return x.unsqueeze(1).to_broadcast([P, NP, P])

                def masked(name, dst, odd, b, mask, src=None):
                    e.wait_ge(pe_steps, done("pe", name))
                    e.tensor_tensor(dst[:, odd], four(b[:]), over(mask), ALU.mult).then_inc(vec_steps, v.step(name))

                def scores(j):
                    h2 = slice(4 * (j % 2) + 2 * (j // 2), 4 * (j % 2) + 2 * (j // 2) + 2)
                    e.wait_ge(pe_steps, done("pe", f"sc{j}"))
                    e.tensor_tensor(scb[:, h2, :], bank[6 + j % 2][:, 0:2 * WIN].rearrange("p (a n) -> p a n", a=2), table[:, h2, :], ALU.add).then_inc(vec_steps, v.step(f"sb{j}"))

                def highest(j):
                    h2 = slice(4 * (j % 2) + 2 * (j // 2), 4 * (j % 2) + 2 * (j // 2) + 2)
                    e.wait_ge(vec_steps, v.after(f"sb{j}"))
                    e.tensor_reduce(den8[:, 0, h2], scb[:, h2, :], AX, ALU.max).then_inc(vec_steps, v.step(f"mx{j}"))

                def Y(lv):
                    for odd in range(2):
                        masked(f"Y{lv}_{odd}", Yb, odd, bank[2 + odd], level[lv - 1])

                def TT(lv):
                    for odd in range(2):
                        e.wait_ge(pe_steps, done("pe", f"TT{lv}_{odd}"))
                        e.tensor_tensor(Tt[:, odd], four(bank[4 + odd][:]), Tt[:, odd], ALU.add).then_inc(vec_steps, v.step(f"TT{lv}_{odd}"))

                e.wait_ge(pe_steps, last("pe", "YU"))
                e.tensor_tensor(RT[:], tile(rkv[:, 0]), E[:], ALU.mult).then_inc(vec_steps, v.step("RT"))
                e.wait_ge(pool_steps, last("pool", "Wb"))
                e.tensor_copy(wend[:].unsqueeze(2), E[:].rearrange("p (c n) -> p c n", c=8)[:, :, CH - 1:CH]).then_inc(vec_steps, v.step("wend"))
                masked("G0", G, 0, bank[2], lower)
                masked("G1", G, 1, bank[3], lower)
                e.wait_ge(pool_steps, last("pool", "BV"))
                for odd in range(2):
                    masked(f"Y1_{odd}", Yb, odd, bank[4 + odd], level[0])
                    e.wait_ge(vec_steps, v.after(f"Y1_{odd}"))
                    e.tensor_tensor(Tt[:, odd], Yb[:, odd], over(ident), ALU.add).then_inc(vec_steps, v.step(f"TT1_{odd}"))
                scores(0)
                scores(1)
                masked("MKA0", MKA, 0, bank[1], upper)
                highest(0)
                highest(1)
                Y(2)
                scores(2)
                TT(2)
                highest(2)
                scores(3)
                highest(3)
                e.wait_ge(vec_steps, v.after("mx3"))
                e.tensor_tensor(den8[:, 5, :], den8[:, 0, :], sink, ALU.max).then_inc(vec_steps, v.step("m"))
                e.wait_ge(vec_steps, v.after("m"))
                e.tensor_scalar(den8[:, 1, :], den8[:, 5, :], -1.0, None, ALU.mult).then_inc(vec_steps, v.step("nm"))
                e.tensor_tensor(den8[:, 2, :], sink, den8[:, 5, :], ALU.subtract).then_inc(vec_steps, v.step("sd"))
                masked("MKA1", MKA, 1, bank[0], upper)
                if ph != "mix_first":
                    e.wait_ge(act_steps, last("act", "Y"))
                    e.wait_ge(pool_steps, last("pool", "BV"))
                    centre(v, t - 1)
                Y(3)
                masked("MRB0", MRB, 0, bank[1], uppeq)
                TT(3)
                if ph != "mix_first":
                    variance(v, done("act", "gsq"))
                Y(4)
                masked("MRB1", MRB, 1, bank[0], uppeq)
                TT(4)
                Y(5)
                masked("MRK0", MRK, 0, bank[1], uppeq)
                TT(5)
                if ph != "mix_first":
                    scale(v, done("act", "groot"))
                masked("MRK1", MRK, 1, bank[0], uppeq)
                e.wait_ge(act_steps, done("act", "esink"))
                e.tensor_tensor(den8[:, 4, :], den8[:, 3, :], den8[:, 4, :], ALU.add).then_inc(vec_steps, v.step("den"))
                e.wait_ge(vec_steps, v.after("den"))
                e.reciprocal(den8[:, 0, :], den8[:, 4, :]).then_inc(vec_steps, v.step("rden"))
                Y(6)
                TT(6)
                if ph != "mix_end":
                    ready(hf, ph, t + 1, 0)
                e.wait_ge(pe_steps, done("pe", "bonus"))
                e.tensor_copy(small[:, 32:40], bank[7][:, 0:8]).then_inc(vec_steps, v.step("bon"))
                for c in range(2):
                    nm = "ab"[c]
                    e.wait_ge(pe_steps, done("pe", "HB" + nm))
                    e.wait_ge(pool_steps, done("pool", "W" + nm))
                    b = bank[5] if c == 0 else bank[2]
                    e.tensor_tensor(H[1 - c][:], HW[:], b[:, 0:NP * HD].rearrange("p (a n) -> p a n", a=NP), ALU.add).then_inc(vec_steps, v.step("H" + nm))
                    if c == 0:
                        e.wait_ge(pe_steps, done("pe", "PV"))
                        e.wait_ge(vec_steps, v.after("rden"))
                        e.tensor_tensor(rows_a[:, bass.ds(t, 1), :].rearrange("p a (h n) -> p (a h) n", h=HEADS), bank[6][:].rearrange("p (h n) -> p h n", h=HEADS),
                                        den8[:, 0, :].unsqueeze(2).to_broadcast([P, HEADS, CH]), ALU.mult).then_inc(vec_steps, v.step("PV"))
                    if c == 0 and ph != "mix_end":
                        e.wait_ge(pool_steps, last("pool", "BP"))
                        ready(hf, ph, t + 1, 1)

            for hf in range(HALVES):
                if hf == 0:
                    begin(e, hf, "norm", "vec")
                    norm(Pass(hf, "norm"), hf, "norm", xr, xr, 1)
                    e.wait_ge(const_in, 32)
                begin(e, hf, "rkv", "vec")
                if hf:
                    e.wait_ge(y_out, 16 * NT * hf)
                with e.Fori(0, 3) as g:
                    v = Pass(hf, "rkv", g)
                    for n in range(4):
                        shift_tile(v, n, after(hf, "rkv", "act", f"e{n}", g),
                                   par[:, bass.ds(g * 4 + n, 1)], shcar[:, bass.ds(g * 4 + n, 1)],
                                   rkv[:, bass.ds(g, 1), :, P * n:P * n + P].rearrange("p a t n -> p (a t) n"))
                v = Pass(hf, "lora")
                e.wait_ge(mix_in, 128 * (hf + 1))
                for n, dst in enumerate((wa, gd)):
                    shift_tile(v, n, after(hf, "lora", "act", f"e{n}"), par[:, 12 + n:13 + n],
                               shcar[:, 12 + n:13 + n], dst[:], four=False)
                for p in range(NP):
                    e.tensor_scalar(kk[:, :, P * p:P * p + P], rkv[:, 1, :, P * p:P * p + P], par[:, KK_ + p:KK_ + p + 1], None, ALU.mult).then_inc(vec_steps, v.step(f"kr{p}"))
                v = Pass(hf, "q")
                e.wait_ge(act_steps, after(hf, "q", "act", "root"))
                e.tensor_scalar(rn[:, 1, :], rn[:, 0, :], 1e-12, None, ALU.max).then_inc(vec_steps, v.step("nmax"))
                e.wait_ge(vec_steps, v.after("nmax"))
                e.reciprocal(rn[:, 2, :], rn[:, 1, :]).then_inc(vec_steps, v.step("rn"))
                for p in range(NP):
                    part = (slice(None), slice(None), slice(P * p, P * p + P))
                    k_p = rkv[:, 1, :, P * p:P * p + P]
                    tmp = shd[:].rearrange("p (t n) -> p t n", t=NT)
                    if p:
                        e.wait_ge(vec_steps, v.after(f"k{p - 1}"))
                    e.wait_ge(act_steps, after(hf, "q", "act", f"a_{p}"))
                    e.tensor_scalar(tmp, av[part], 1.0, par[:, KA + p:KA + p + 1], ALU.subtract, ALU.mult).then_inc(vec_steps, v.step(f"t{p}"))
                    e.wait_ge(vec_steps, v.after(f"t{p}"))
                    e.scalar_tensor_tensor(k_p, tmp, 1.0, k_p, ALU.add, ALU.mult).then_inc(vec_steps, v.step(f"k{p}"))

                def scan(v, t):
                    e.tensor_tensor_scan(L[:, t, :], chunks[:], sig[:, t, :], 0.0, ALU.mult, ALU.add).then_inc(vec_steps, v.step(f"scan{t}"))

                e.wait_ge(act_steps, after(hf, "q", "act", "w_3"))
                scan(v, 0)
                for p in range(NP):
                    part = (slice(None), slice(None), slice(P * p, P * p + P))
                    e.wait_ge(pe_steps, after(hf, "q", "pe", f"bc{p}"))
                    e.tensor_tensor(kk[part], kk[part], norms[p][:].rearrange("p (t n) -> p t n", t=NT), ALU.mult).then_inc(vec_steps, v.step(f"kn{p}"))
                    e.wait_ge(vec_steps, v.after(f"kn{p}"))
                    e.tensor_tensor(av[part], av[part], kk[part], ALU.mult).then_inc(vec_steps, v.step(f"b{p}"))
                e.wait_ge(vec_steps, v.after("scan0"))
                ready(hf, "prep", 0, 0)
                e.wait_ge(pool_steps, after(hf, "q", "pool", "u2"))
                ready(hf, "prep", 0, 1)
                for t in range(1, NT):
                    scan(Pass(hf, "prep"), t)
                begin(e, hf, "mix_first", "vec")
                mix_tile(hf, "mix_first", 0)
                with e.Fori(1, NT - 1) as t:
                    mix_tile(hf, "mix", t)
                mix_tile(hf, "mix_end", NT - 1)
                begin(e, hf, "gate", "vec")
                v = Pass(hf, "gate")

                def lo(name):
                    n = TURNS.index(name)
                    b, i = n // NT, n % NT
                    e.wait_ge(act_steps, after(hf, "gate", "act", f"hi_{name}"))
                    cols = (slice(None), slice(4 * b, 4 * b + 4), slice(P * i, P * i + P))
                    e.tensor_tensor(xlo[cols], bank[i][:].rearrange("p (k n) -> p k n", k=4), xhi[cols].bitcast(F32), ALU.subtract).then_inc(vec_steps, v.step(f"lo_{name}"))

                centre(v, NT - 1)
                lo("a0")
                variance(v, after(hf, "gate", "act", "gsq"))
                lo("a1")
                scale(v, after(hf, "gate", "act", "groot"))
                for name in TURNS[2:]:
                    lo(name)
                begin(e, hf, "post", "vec")
                v = Pass(hf, "post")
                e.wait_ge(act_steps, after(hf, "post", "act", "qb3"))
                e.tensor_tensor(small[:, 24:28], small[:, 16:20], small[:, 20:24], ALU.add).then_inc(vec_steps, v.step("ss"))
                e.wait_ge(vec_steps, v.after("ss"))
                e.tensor_scalar(small[:, 24:28], small[:, 24:28], 1.0 / D, EPS, ALU.mult, ALU.add).then_inc(vec_steps, v.step("pms"))
                e.wait_ge(act_steps, after(hf, "post", "act", "proot"))
                e.reciprocal(small[:, 40:44], small[:, 28:32]).then_inc(vec_steps, v.step("prstd"))
                e.wait_ge(vec_steps, v.after("prstd"))
                e.wait_ge(gain_in, 16 * (3 * hf + 2))
                e.wait_ge(h_in, 16 * (NT + 1) * (hf + 1))

                def mixture(i):
                    e.scalar_tensor_tensor(xn[:, i, 0:512], bank[i][:], small[:, 40 + i:41 + i], gain[:, 0:512], ALU.mult, ALU.mult).then_inc(vec_steps, v.step(f"ma{i}"))
                    e.scalar_tensor_tensor(xn[:, i, 512:1024], bank[4 + i][:], small[:, 40 + i:41 + i], gain[:, 512:1024], ALU.mult, ALU.mult).then_inc(vec_steps, v.step(f"mb{i}"))

                def residual(i):
                    e.wait_ge(vec_steps, v.after(f"mb{i}"))
                    e.tensor_tensor(hres[:, i, :], hres[:, i, :], xn[:, i, :], ALU.add).then_inc(vec_steps, v.step(f"h{i}"))

                def normalised(i):
                    e.wait_ge(act_steps, after(hf, "post", "act", f"sq{i}"))
                    e.tensor_scalar(small[:, 4 + i:5 + i], small[:, i:i + 1], 1.0 / D, EPS, ALU.mult, ALU.add).then_inc(vec_steps, v.step(f"ms{i}"))
                    e.wait_ge(act_steps, after(hf, "post", "act", f"root{i}"))
                    e.reciprocal(small[:, 12 + i:13 + i], small[:, 8 + i:9 + i]).then_inc(vec_steps, v.step(f"rstd{i}"))
                    e.wait_ge(vec_steps, v.after(f"rstd{i}"))
                    e.scalar_tensor_tensor(xn[:, i, :], hres[:, i, :], small[:, 12 + i:13 + i], gain2[:], ALU.mult, ALU.mult).then_inc(vec_steps, v.step(f"xs{i}"))

                mixture(0)
                residual(0)
                mixture(1)
                mixture(2)
                residual(2)
                normalised(0)
                mixture(3)
                residual(3)
                normalised(1)
                columns_lo(v, hf, "post", 0)
                normalised(2)
                normalised(3)
                columns_lo(v, hf, "post", 1)
                columns_lo(v, hf, "post", 2)
                columns_lo(v, hf, "post", 3)
                begin(e, hf, "up", "vec")
                with e.Fori(0, PJ // 2) as g:
                    v = Pass(hf, "up", g)
                    for n in range(2):
                        def col(first, m):
                            return par[:, bass.ds(g * 2 + (first + PJ * m + n), 1)]

                        gv = list(enumerate("gv"))
                        for m, k in gv:
                            e.tensor_copy(cr[n][m][:, 0:2], cvcar[:, bass.ds(g * 2 + (PJ * m + n), 1), :].rearrange("p a n -> p (a n)")).then_inc(vec_steps, v.step(f"i{k}{n}"))
                        for m, k in gv:
                            e.wait_ge(act_steps, after(hf, "up", "act", f"e{k}{n}", g))
                            e.tensor_scalar(cc[n][m][:], cr[n][m][:, 2:2 + HALF], col(CW + 4 * PJ, m), col(CB, m), ALU.mult, ALU.add).then_inc(vec_steps, v.step(f"c{k}{n}"))
                            for tap in (1, 0):
                                e.wait_ge(vec_steps, v.after(f"{'c' if tap else '1'}{k}{n}"))
                                e.scalar_tensor_tensor(cc[n][m][:], cr[n][m][:, tap:tap + HALF], col(CW + 2 * PJ * tap, m), cc[n][m][:], ALU.mult, ALU.add).then_inc(vec_steps, v.step(f"{tap}{k}{n}"))
                            e.tensor_copy(cvcar[:, bass.ds(g * 2 + (PJ * m + n), 1), :].rearrange("p a n -> p (a n)"), cr[n][m][:, HALF:HALF + 2]).then_inc(vec_steps, v.step(f"k{k}{n}"))
                        e.wait_ge(act_steps, after(hf, "up", "act", f"ge{n}", g))
                        e.wait_ge(vec_steps, v.after(f"0v{n}"))
                        e.tensor_tensor(cc[n][0][:], gl[:], cc[n][1][:], ALU.mult).then_inc(vec_steps, v.step(f"m{n}"))
                        e.wait_ge(vec_steps, v.after(f"m{n}"))
                        part = ghi[:, bass.ds(g * 2 + n, 1), :].rearrange("p a d -> p (a d)")
                        e.tensor_copy(part, cc[n][0][:]).then_inc(vec_steps, v.step(f"hi{n}"))
                        e.wait_ge(vec_steps, v.after(f"hi{n}"))
                        e.tensor_tensor(glo[:, bass.ds(g * 2 + n, 1), :].rearrange("p a d -> p (a d)"), cc[n][0][:], part.bitcast(F32), ALU.subtract).then_inc(vec_steps, v.step(f"lo{n}"))
                for n in range(2):
                    ph = f"down{n}"
                    v = Pass(hf, ph)
                    if n == 0 and hf + 1 < HALVES:
                        norm(v, hf, ph, xr, xr, 3)
                    e.wait_ge(pe_steps, after(hf, ph, "pe", "u10"))
                    for i in (2, 3):
                        e.tensor_copy(fo[:, i, 512 * n:512 * n + 512], bank[4 + i][:]).then_inc(vec_steps, v.step(f"f{i}"))
                begin(e, hf, "last", "vec")
                v = Pass(hf, "last")
                rstd(v, hf, "last")
                e.wait_ge(gain_in, 16 * (4 + 2 * hf))
                for i in range(NT):
                    e.scalar_tensor_tensor(fo[:, i, :], fo[:, i, :], small[:, 12 + i:13 + i], gain[:], ALU.mult, ALU.mult).then_inc(vec_steps, v.step(f"m{i}"))
                    e.wait_ge(vec_steps, v.after(f"m{i}"))
                    e.tensor_tensor(hres[:, i, :], hres[:, i, :], fo[:, i, :], ALU.add).then_inc(vec_steps, v.step(f"y{i}"))

        @block.gpsimd
        def _(e):
            for cell in (kT[:, 0:P], HW[:], rn[:, 0, :]):
                e.memset(cell, 0.0).then_inc(sems["pool"], 1)
            e.wait_ge(const_in, 32)

            def tt(hf, ph, name, dst, x, y, op):
                e.tensor_tensor(dst, x, y, op).then_inc(pool_steps, halves[hf][ph]["pool"].step(name))

            def ready(hf, ph, t):
                it = tile_pass(ph, t - 1)
                c8 = lambda x: x[:].rearrange("p (c n) -> p c n", c=8)
                wc = c8(E)[:, :, CH - 1:CH].to_broadcast([P, 8, CH])
                e.wait_ge(vec_steps, after(hf, ph, "vec", "KT", it))
                tt(hf, ph, "KP", c8(KP), c8(KTl), wc, ALU.mult)
                tt(hf, ph, "BP", c8(BP), c8(BT), wc, ALU.mult)

            def gate(hf, ph, t, scaled, gated):
                steps = halves[hf][ph]["pool"]
                it = tile_pass(ph, t + 1)
                row = lambda x: x[:, bass.ds(t, 1), :].rearrange("p a d -> p (a d)")
                e.wait_ge(vec_steps, scaled)
                tt(hf, ph, "glw", gyn[:], gyn[:], lnw[:], ALU.mult)
                e.wait_ge(pool_steps, steps.after("glw", it))
                tt(hf, ph, "glb", gyn[:], gyn[:], lnb[:], ALU.add)
                e.wait_ge(pool_steps, steps.after("glb", it))
                tt(hf, ph, "gbv", gyn[:], gyn[:], row(bv), ALU.add)
                e.wait_ge(pool_steps, steps.after("gbv", it))
                e.wait_ge(act_steps, gated)
                tt(hf, ph, "gg", row(rows_y), gyn[:], gb[:], ALU.mult)

            def mix_tile(hf, ph, t):
                done, last = tile_counts(hf, ph, t)
                c8 = lambda x: x[:].rearrange("p (c n) -> p c n", c=8)
                tile = lambda x, n: x[:, n, bass.ds(t, 1), :].rearrange("p a d -> p (a d)")
                e.wait_ge(pe_steps, last("pe", "bonus"))
                tt(hf, ph, "RK", RKp[:], tile(rkv, 0), tile(rkv, 1), ALU.mult)
                e.wait_ge(vec_steps, done("vec", "sb3"))
                e.nop(nofuse=True)
                e.tensor_copy(table[:, :, 0:CH], edge[:]).then_inc(pool_steps, halves[hf][ph]["pool"].step("tab"))

                def decayed(c):
                    w = wend[:].rearrange("p (a c) -> p a c", a=NP)[:, :, c:c + 1].to_broadcast([P, NP, HD])
                    tt(hf, ph, "W" + "ab"[c], HW[:], H[c][:], w, ALU.mult)

                decayed(0)
                if ph != "mix_first":
                    gate(hf, ph, t - 1, done("vec", "gyn"), done("act", "gb"))
                e.wait_ge(act_steps, done("act", "trV"))
                e.wait_ge(vec_steps, done("vec", "bon"))
                tt(hf, ph, "BV", bv[:, bass.ds(t, 1), :].rearrange("p a (h n) -> p (a h) n", h=HEADS), c8(Vt),
                   small[:, 32:40].unsqueeze(2).to_broadcast([P, HEADS, HD]), ALU.mult)
                e.wait_ge(vec_steps, done("vec", "Ha"))
                decayed(1)
                if ph != "mix_end":
                    ready(hf, ph, t + 1)

            for hf in range(HALVES):
                for u in range(4):
                    split_lo(e, hf, "rkv", u, 0)
                with e.Fori(1, 3) as g:
                    for u in range(4):
                        split_lo(e, hf, "rkv", u, g)
                for ph in ("lora", "q"):
                    for u in range(4):
                        split_lo(e, hf, ph, u, 0)
                e.wait_ge(pe_steps, after(hf, "q", "pe", "u3"))
                st = halves[hf]["q"]["pool"]
                e.memset(pr[:, :, 0:CH], 0.0).then_inc(pool_steps, st.step("zp"))
                ready(hf, "prep", 0)
                begin(e, hf, "mix_first", "pool")
                e.wait_ge(mix_in, 128 * (hf + 1))
                mix_tile(hf, "mix_first", 0)
                with e.Fori(1, NT - 1) as t:
                    mix_tile(hf, "mix", t)
                mix_tile(hf, "mix_end", NT - 1)
                begin(e, hf, "gate", "pool")
                st = halves[hf]["gate"]["pool"]
                e.tensor_copy(kT[:, 0:P], kT[:, HALF:HALF + P]).then_inc(pool_steps, st.step("kT"))
                e.tensor_copy(vA[:, 0, :], vA[:, NT, :]).then_inc(pool_steps, st.step("vA"))
                gate(hf, "gate", NT - 1, after(hf, "gate", "vec", "gyn"), after(hf, "gate", "act", "gb"))
                for u in range(8):
                    split_lo(e, hf, "out", u, 0)
                e.wait_ge(vec_steps, after(hf, "post", "vec", "mb1"))
                tt(hf, "post", "h1", hres[:, 1, :], hres[:, 1, :], xn[:, 1, :], ALU.add)
                for u in range(4):
                    split_lo(e, hf, "up", u, 0)
                with e.Fori(1, PJ // 2) as g:
                    for u in range(4):
                        split_lo(e, hf, "up", u, g)
                for n in range(2):
                    for u in range(11):
                        split_lo(e, hf, f"down{n}", u, 0)


def constants():
    f = np.float32
    i = np.arange(P)
    same = (i[:, None] // CH) == (i[None, :] // CH)
    eye = np.eye(P, dtype=f)
    lower = (same & (i[:, None] > i[None, :])).astype(f)
    r, c = np.arange(CH)[:, None], np.arange(CH)[None, :]
    levels = []
    for b in LEVELS:
        m = (r // (2 * b) == c // (2 * b)) & (r // b % 2 == 0) & (c // b % 2 == 1)
        levels.append(np.kron(np.eye(2, dtype=f), m.astype(f)))
    ones8 = np.zeros((P, NP, 8), f)
    spread = np.zeros((8, NP, P), f)
    for p in range(NP):
        for e in range(2):
            ones8[HD * e:HD * e + HD, p, 2 * p + e] = 1
            spread[2 * p + e, p, HD * e:HD * e + HD] = 1
    key = np.arange(WIN)
    dist = np.abs(i[:, None] + CH - key[None, :]).astype(f)
    seen = (key[None, :] // CH == i[:, None] // CH) | (key[None, :] // CH == i[:, None] // CH + 1)
    slopes = np.exp2(-8.0 * np.arange(1, HEADS + 1, dtype=f) / HEADS).astype(f)
    alibi = np.stack([np.where(seen, -slopes[h] * dist, -HID) for h in range(HEADS)], 1).astype(f)
    first = alibi.copy()
    first[:, :, 0:CH] = -HID
    chunks = np.ones((P, 512), f)
    chunks[:, ::CH] = 0
    return eye, lower, lower.T, lower.T + eye, levels, ones8, spread, alibi, first, chunks


def kernel(**inputs):
    import concourse.bacc as bacc
    from concourse.bass_utils import run_bass_kernel_spmd

    x = {n: np.asarray(v) for n, v in inputs.items()}
    f = np.float32
    eye, lower, upper, uppeq, levels, ones8, spread, alibi, first, chunks = constants()

    def tall(v):
        return np.ascontiguousarray(v.reshape(-1, P).T)

    def wide(v):
        return np.ascontiguousarray(np.broadcast_to(v.reshape(1, -1), (P, v.size)))

    bonus = np.zeros((P, 8), f)
    rk = x["rwkv_r_k"][0]
    for h in range(HEADS):
        bonus[HD * (h % 2):HD * (h % 2) + HD, h] = rk[h]
    par = np.concatenate([tall(x["rwkv_mu"][0]), tall(x["rwkv_w0"][0]), tall(x["rwkv_a0"][0]), tall(x["rwkv_k_k"][0]),
                          tall(x["rwkv_k_a"][0])] + [tall(x["ffn_conv_w"][0, n]) for n in range(3)]
                         + [tall(x["ffn_conv_b"][0]), bonus], 1)
    cst = np.concatenate([eye, lower, upper, uppeq, *levels, ones8.reshape(P, -1),
                          wide(x["attn_sinks"])], 1)
    feed = {
        "x": x["x"][0], "w_in": x["w_in"][0], "w_out": x["w_out"][0], "ffn_w_up": x["ffn_w_up"][0],
        "ffn_w_down": x["ffn_w_down"][0], "par": par, "cst": cst, "spread": spread, "alibi": alibi, "first": first,
        "edge": np.ascontiguousarray(alibi[:, :, 0:CH]),
        "chunks": chunks, "lora": np.concatenate([x["rwkv_w_w2"][0], x["rwkv_w_a2"][0]], 0),
        "wg2": x["rwkv_w_g2"][0], "ln_w": wide(x["rwkv_ln_w"]), "ln_b": wide(x["rwkv_ln_b"]),
        "g_mix_pre": wide(x["norm_mix_pre"]), "g_mix_post": wide(x["norm_mix_post"]),
        "g_ffn_pre": wide(x["norm_ffn_pre"]), "g_ffn_post": wide(x["norm_ffn_post"]),
    }
    nc = bacc.Bacc("TRN2", target_bir_lowering=False, num_devices=1)
    arrays, aps = {}, {}
    for name, v in feed.items():
        v = np.ascontiguousarray(v)
        arrays[f"in_{name}"] = v
        aps[name] = nc.dram_tensor(f"in_{name}", v.shape, mybir.dt.from_np(v.dtype), kind="ExternalInput").ap()
    out = nc.dram_tensor("out", (SEQ, D), F32, kind="ExternalOutput").ap()
    build(nc, aps, out)
    r = run_bass_kernel_spmd(nc, [arrays], core_ids=[0])
    return r.results[0]["out"].reshape(1, SEQ, D)
```
